# Optimizing a Trainium2 kernel written in Bass

```python
import math
import jax, jax.numpy as jnp
from jax import lax
import numpy as np

D_MODEL = 1024
BATCH = 1
SEQ = 512
DEPTH = 2

HEAD_DIM = 64
FOURIER_WIDTH = D_MODEL // 4
FOURIER_CH = HEAD_DIM
N_FOURIER_GROUPS = FOURIER_WIDTH // FOURIER_CH
ATTN_WIDTH = D_MODEL // 2
N_Q_HEADS = ATTN_WIDTH // HEAD_DIM
N_KV_HEADS = 2
KV_WIDTH = N_KV_HEADS * HEAD_DIM
MEM_WIDTH = D_MODEL // 4
N_MEM_HEADS = MEM_WIDTH // HEAD_DIM
N_MEM = 256
MIX_WIDTH = FOURIER_WIDTH + ATTN_WIDTH + MEM_WIDTH
IN_WIDTH = FOURIER_WIDTH + ATTN_WIDTH + 2 * KV_WIDTH + MEM_WIDTH
WINDOW = 128
BLOCK = 128
ROPE_THETA = 10000.0
D_FF = -(-8 * D_MODEL // (3 * 256)) * 256
EPS = 1e-6
NEG_INF = -1e30


def _rmsnorm(x, g):
    xf = x.astype(jnp.float32)
    y = xf * lax.rsqrt(jnp.mean(xf * xf, axis=-1, keepdims=True) + EPS)
    return (y * g.astype(jnp.float32)).astype(x.dtype)

def _rope(t, positions):
    half = HEAD_DIM // 2
    inv_freq = jnp.exp(-math.log(ROPE_THETA) * jnp.arange(half, dtype=jnp.float32) * (2.0 / HEAD_DIM))
    ang = positions.astype(jnp.float32)[:, :, None] * inv_freq
    cos = jnp.cos(ang)[:, :, None, :]
    sin = jnp.sin(ang)[:, :, None, :]
    tf = t.astype(jnp.float32)
    t1, t2 = tf[..., :half], tf[..., half:]
    return jnp.concatenate([t1 * cos - t2 * sin, t2 * cos + t1 * sin], axis=-1).astype(t.dtype)

def _fourier_mix(u, w_f):
    b, s, _ = u.shape
    ug = u.reshape(b, s, N_FOURIER_GROUPS, FOURIER_CH).astype(jnp.float32)
    spec = jnp.fft.fftn(ug, axes=(1, 3), norm='ortho').real
    y = jnp.einsum('bsgc,gce->bsge', spec.astype(u.dtype), w_f)
    return y.reshape(b, s, FOURIER_WIDTH)

def _window_attn(q, k, v, sink):
    b, s, _, _ = q.shape
    nb = s // BLOCK
    grp = N_Q_HEADS // N_KV_HEADS

    def bands(t):
        tp = jnp.pad(t, ((0, 0), (BLOCK, BLOCK), (0, 0), (0, 0)))
        tp = tp.reshape(b, nb + 2, BLOCK, N_KV_HEADS, HEAD_DIM)
        return jnp.concatenate([tp[:, :-2], tp[:, 1:-1], tp[:, 2:]], axis=2)

    kb, vb = bands(k), bands(v)
    qb = q.reshape(b, nb, BLOCK, N_KV_HEADS, grp, HEAD_DIM)
    scores = jnp.einsum('bnqhgd,bnjhd->bnhgqj', qb, kb).astype(jnp.float32) * (HEAD_DIM ** -0.5)
    blk = jnp.arange(nb)[:, None, None] * BLOCK
    qpos = blk + jnp.arange(BLOCK)[None, :, None]
    kpos = blk - BLOCK + jnp.arange(3 * BLOCK)[None, None, :]
    valid = (kpos >= 0) & (kpos < s) & (jnp.abs(qpos - kpos) <= WINDOW)
    scores = jnp.where(valid[None, :, None, None], scores, NEG_INF)
    sink_b = jnp.broadcast_to(sink.astype(jnp.float32).reshape(1, 1, N_KV_HEADS, grp, 1, 1),
                              scores.shape[:-1] + (1,))
    probs = jax.nn.softmax(jnp.concatenate([scores, sink_b], axis=-1), axis=-1)[..., :-1]
    out = jnp.einsum('bnhgqj,bnjhd->bnqhgd', probs.astype(v.dtype), vb)
    return out.reshape(b, s, N_Q_HEADS * HEAD_DIM)

def _memory_attn(q, km, vm):
    b, s, _, _ = q.shape
    scores = jnp.einsum('bshd,bmhd->bhsm', q, km).astype(jnp.float32) * (HEAD_DIM ** -0.5)
    probs = jax.nn.softmax(scores, axis=-1)
    out = jnp.einsum('bhsm,bmhd->bshd', probs.astype(vm.dtype), vm)
    return out.reshape(b, s, MEM_WIDTH)

def first_inputs(seed: int = 0) -> dict:
    key = jax.random.key(seed)
    ks = jax.random.split(key, 20)
    f32 = jnp.float32

    def nrm(k, shape, scale):
        return jax.random.normal(k, shape, f32) * scale

    def gain(k, shape):
        return 1.0 + 0.05 * jax.random.normal(k, shape, f32)

    x = jax.random.normal(ks[0], (BATCH, SEQ, D_MODEL), f32)
    mem = jax.random.normal(ks[1], (BATCH, N_MEM, D_MODEL), f32)
    positions = jnp.broadcast_to(jnp.arange(SEQ, dtype=jnp.int32)[None, :], (BATCH, SEQ))
    return {
        'x': x,
        'mem': mem,
        'positions': positions,
        'g_pre_mix': gain(ks[2], (DEPTH, D_MODEL)),
        'w_in': nrm(ks[3], (DEPTH, D_MODEL, IN_WIDTH), D_MODEL ** -0.5),
        'w_fourier': nrm(ks[4], (DEPTH, N_FOURIER_GROUPS, FOURIER_CH, FOURIER_CH), FOURIER_CH ** -0.5),
        'sink': nrm(ks[5], (DEPTH, N_Q_HEADS), 0.5),
        'g_mem': gain(ks[6], (DEPTH, D_MODEL)),
        'w_mem_kv': nrm(ks[7], (DEPTH, D_MODEL, 2 * MEM_WIDTH), D_MODEL ** -0.5),
        'g_grp': gain(ks[8], (DEPTH, MIX_WIDTH)),
        'w_out': nrm(ks[9], (DEPTH, MIX_WIDTH, D_MODEL), MIX_WIDTH ** -0.5),
        'g_post_mix': gain(ks[10], (DEPTH, D_MODEL)),
        'g_pre_ffn': gain(ks[11], (DEPTH, D_MODEL)),
        'w_ffn_in': nrm(ks[12], (DEPTH, D_MODEL, 2 * D_FF), D_MODEL ** -0.5),
        'w_ffn_out': nrm(ks[13], (DEPTH, D_FF, D_MODEL), D_FF ** -0.5),
        'g_post_ffn': gain(ks[14], (DEPTH, D_MODEL)),
    }

def first_block(x, mem, positions, g_pre_mix, w_in, w_fourier, sink, g_mem, w_mem_kv, g_grp,
              w_out, g_post_mix, g_pre_ffn, w_ffn_in, w_ffn_out, g_post_ffn):
    b, s, _ = x.shape
    m = mem.shape[1]
    splits = [FOURIER_WIDTH,
              FOURIER_WIDTH + ATTN_WIDTH,
              FOURIER_WIDTH + ATTN_WIDTH + KV_WIDTH,
              FOURIER_WIDTH + ATTN_WIDTH + 2 * KV_WIDTH]
    for l in range(DEPTH):
        h = _rmsnorm(x, g_pre_mix[l])
        z = h @ w_in[l]
        zf, zq, zk, zv, zm = jnp.split(z, splits, axis=-1)

        y_f = _fourier_mix(zf, w_fourier[l])

        q = _rope(zq.reshape(b, s, N_Q_HEADS, HEAD_DIM), positions)
        k = _rope(zk.reshape(b, s, N_KV_HEADS, HEAD_DIM), positions)
        v = zv.reshape(b, s, N_KV_HEADS, HEAD_DIM)
        y_a = _window_attn(q, k, v, sink[l])

        mkv = _rmsnorm(mem, g_mem[l]) @ w_mem_kv[l]
        km, vm = jnp.split(mkv, 2, axis=-1)
        km = km.reshape(b, m, N_MEM_HEADS, HEAD_DIM)
        vm = vm.reshape(b, m, N_MEM_HEADS, HEAD_DIM)
        y_m = _memory_attn(zm.reshape(b, s, N_MEM_HEADS, HEAD_DIM), km, vm)

        gg = g_grp[l]
        y = jnp.concatenate([
            _rmsnorm(y_f, gg[:FOURIER_WIDTH]),
            _rmsnorm(y_a, gg[FOURIER_WIDTH:FOURIER_WIDTH + ATTN_WIDTH]),
            _rmsnorm(y_m, gg[FOURIER_WIDTH + ATTN_WIDTH:]),
        ], axis=-1) @ w_out[l]
        x = x + _rmsnorm(y, g_post_mix[l])

        h = _rmsnorm(x, g_pre_ffn[l])
        gate, up = jnp.split(h @ w_ffn_in[l], 2, axis=-1)
        f = (jax.nn.silu(gate) * up) @ w_ffn_out[l]
        x = x + _rmsnorm(f, g_post_ffn[l])
    return x


D_FF_2 = 2816
NORM_EPS = 1e-6
LRU_WIDTH = 512
LRU_HEADS = 8
LRU_HEAD_DIM = LRU_WIDTH // LRU_HEADS
LRU_CONV_WIDTH = 4
LRU_C = 8.0
MLA_HEADS = 8
QK_NOPE_DIM = 64
QK_ROPE_DIM = 32
V_HEAD_DIM = 64
Q_LORA_RANK = 384
KV_LORA_RANK = 256
Q_BLOCK = 128
CONV_CH = 512
CONV_WIDTH = 31
N_BRANCH = 3
IN_A = 2 * LRU_WIDTH
IN_B = Q_LORA_RANK + KV_LORA_RANK + QK_ROPE_DIM
IN_C = 2 * CONV_CH
IN_G = N_BRANCH * D_MODEL
D_IN = IN_A + IN_B + IN_C + IN_G
MAX_POS_OFFSET = 4096


def rms_norm(x, g):
    xf = x.astype(jnp.float32)
    y = xf * lax.rsqrt(jnp.mean(xf * xf, axis=-1, keepdims=True) + NORM_EPS)
    return (y * g.astype(jnp.float32)).astype(x.dtype)

def layer_norm(x, g, b):
    xf = x.astype(jnp.float32)
    mu = jnp.mean(xf, axis=-1, keepdims=True)
    var = jnp.mean(jnp.square(xf - mu), axis=-1, keepdims=True)
    y = (xf - mu) * lax.rsqrt(var + NORM_EPS)
    return (y * g.astype(jnp.float32) + b.astype(jnp.float32)).astype(x.dtype)

def swiglu(x, w1, w2):
    gu = x @ w1
    g, u = gu[..., :D_FF_2], gu[..., D_FF_2:]
    return (jax.nn.silu(g) * u) @ w2

def causal_depthwise_conv(x, w, b):
    k = w.shape[0]
    y = lax.conv_general_dilated(
        x, w[:, None, :].astype(x.dtype), window_strides=(1,), padding=[(k - 1, 0)],
        dimension_numbers=('NWC', 'WIO', 'NWC'), feature_group_count=x.shape[-1])
    return y + b.astype(x.dtype)

def rg_lru(x, w_gate, b_gate, lam):
    b, s, w = x.shape
    xf = x.astype(jnp.float32)
    xh = xf.reshape(b, s, LRU_HEADS, LRU_HEAD_DIM)
    gates = jnp.einsum('bshd,hde->bshe', xh, w_gate.astype(jnp.float32)) + b_gate.astype(jnp.float32)
    r = jax.nn.sigmoid(gates[..., :LRU_HEAD_DIM]).reshape(b, s, w)
    i = jax.nn.sigmoid(gates[..., LRU_HEAD_DIM:]).reshape(b, s, w)
    log_a = -LRU_C * r * jax.nn.softplus(-lam.astype(jnp.float32))
    a = jnp.exp(log_a)
    u = jnp.sqrt(-jnp.expm1(2.0 * log_a)) * (i * xf)

    def combine(left, right):
        a_l, h_l = left
        a_r, h_r = right
        return a_l * a_r, a_r * h_l + h_r

    _, h = lax.associative_scan(combine, (a, u), axis=1)
    return h.astype(x.dtype)

def rope_tables(positions):
    inv_freq = ROPE_THETA ** (-jnp.arange(0, QK_ROPE_DIM, 2, dtype=jnp.float32) / QK_ROPE_DIM)
    ang = positions.astype(jnp.float32)[..., None] * inv_freq
    return jnp.cos(ang), jnp.sin(ang)

def apply_rope(x, cos, sin):
    half = x.shape[-1] // 2
    x1, x2 = x[..., :half], x[..., half:]
    cos = cos.astype(x.dtype)
    sin = sin.astype(x.dtype)
    return jnp.concatenate([x1 * cos - x2 * sin, x2 * cos + x1 * sin], axis=-1)

def mla_branch(cq, ckv, kpe, positions, q_norm, w_uq, kv_norm, w_ukv, w_o):
    b, s, _ = cq.shape
    q = (rms_norm(cq, q_norm) @ w_uq).reshape(b, s, MLA_HEADS, QK_NOPE_DIM + QK_ROPE_DIM)
    q_nope, q_pe = q[..., :QK_NOPE_DIM], q[..., QK_NOPE_DIM:]
    kv = (rms_norm(ckv, kv_norm) @ w_ukv).reshape(b, s, MLA_HEADS, QK_NOPE_DIM + V_HEAD_DIM)
    k_nope, v = kv[..., :QK_NOPE_DIM], kv[..., QK_NOPE_DIM:]
    cos, sin = rope_tables(positions)
    q_pe = apply_rope(q_pe, cos[:, :, None, :], sin[:, :, None, :])
    k_pe = apply_rope(kpe, cos, sin)
    n_blk = s // Q_BLOCK
    qn_blocks = q_nope.reshape(b, n_blk, Q_BLOCK, MLA_HEADS, QK_NOPE_DIM).swapaxes(0, 1)
    qp_blocks = q_pe.reshape(b, n_blk, Q_BLOCK, MLA_HEADS, QK_ROPE_DIM).swapaxes(0, 1)
    scale = (QK_NOPE_DIM + QK_ROPE_DIM) ** -0.5
    key_idx = jnp.arange(s)

    def attend(args):
        qn, qp, blk = args
        sc = (jnp.einsum('bqhd,bkhd->bhqk', qn, k_nope, preferred_element_type=jnp.float32)
              + jnp.einsum('bqhr,bkr->bhqk', qp, k_pe, preferred_element_type=jnp.float32)) * scale
        q_idx = blk * Q_BLOCK + jnp.arange(Q_BLOCK)
        mask = key_idx[None, :] <= q_idx[:, None]
        sc = jnp.where(mask, sc, jnp.finfo(jnp.float32).min)
        p = jax.nn.softmax(sc, axis=-1).astype(v.dtype)
        return jnp.einsum('bhqk,bkhd->bqhd', p, v)

    o = lax.map(attend, (qn_blocks, qp_blocks, jnp.arange(n_blk)))
    o = o.swapaxes(0, 1).reshape(b, s, MLA_HEADS * V_HEAD_DIM)
    return o @ w_o

def conformer_conv_branch(pc, dw_w, dw_b, ln_g, ln_b, w_pw, b_pw):
    c = pc[..., :CONV_CH] * jax.nn.sigmoid(pc[..., CONV_CH:])
    c = causal_depthwise_conv(c, dw_w, dw_b)
    c = jax.nn.silu(layer_norm(c, ln_g, ln_b))
    return c @ w_pw + b_pw

def hybrid_mixer(h, positions, w_in, b_in, lru_conv_w, lru_conv_b, lru_w_gate, lru_b_gate,
                 lru_lambda, lru_w_out, q_norm, w_uq, kv_norm, w_ukv, mla_w_o,
                 conv_dw_w, conv_dw_b, conv_ln_g, conv_ln_b, conv_w_out, conv_b_out, w_out):
    proj = h @ w_in + b_in
    o1, o2, o3 = IN_A, IN_A + IN_B, IN_A + IN_B + IN_C
    pa, pb, pc, pg = proj[..., :o1], proj[..., o1:o2], proj[..., o2:o3], proj[..., o3:]
    xa = causal_depthwise_conv(pa[..., :LRU_WIDTH], lru_conv_w, lru_conv_b)
    y_a = (rg_lru(xa, lru_w_gate, lru_b_gate, lru_lambda) * jax.nn.gelu(pa[..., LRU_WIDTH:])) @ lru_w_out
    cq = pb[..., :Q_LORA_RANK]
    ckv = pb[..., Q_LORA_RANK:Q_LORA_RANK + KV_LORA_RANK]
    kpe = pb[..., Q_LORA_RANK + KV_LORA_RANK:]
    y_b = mla_branch(cq, ckv, kpe, positions, q_norm, w_uq, kv_norm, w_ukv, mla_w_o)
    y_c = conformer_conv_branch(pc, conv_dw_w, conv_dw_b, conv_ln_g, conv_ln_b, conv_w_out, conv_b_out)
    gates = jax.nn.sigmoid(pg.astype(jnp.float32)).astype(h.dtype)
    gates = gates.reshape(*pg.shape[:-1], N_BRANCH, D_MODEL)
    merged = gates[..., 0, :] * y_a + gates[..., 1, :] * y_b + gates[..., 2, :] * y_c
    return merged @ w_out

def second_inputs(seed: int = 0) -> dict:
    key = jax.random.key(seed)
    ks = iter(jax.random.split(key, 48))
    L = DEPTH

    def w(shape, fan_in):
        return jax.random.normal(next(ks), shape, jnp.float32) * fan_in ** -0.5

    def gain(shape):
        return 1.0 + 0.02 * jax.random.normal(next(ks), shape, jnp.float32)

    def bias(shape):
        return 0.02 * jax.random.normal(next(ks), shape, jnp.float32)

    x = jax.random.normal(next(ks), (BATCH, SEQ, D_MODEL), jnp.float32)
    offsets = jax.random.randint(next(ks), (BATCH, 1), 0, MAX_POS_OFFSET, dtype=jnp.int32)
    positions = offsets + jnp.arange(SEQ, dtype=jnp.int32)[None, :]
    u = jax.random.uniform(next(ks), (L, LRU_WIDTH), jnp.float32, 0.9, 0.999)
    a0 = u ** (1.0 / LRU_C)
    lru_lambda = jnp.log(a0) - jnp.log1p(-a0)
    return {
        'x': x,
        'positions': positions,
        'ffn1_norm': gain((L, D_MODEL)),
        'ffn1_w1': w((L, D_MODEL, 2 * D_FF_2), D_MODEL),
        'ffn1_w2': w((L, D_FF_2, D_MODEL), D_FF_2),
        'mix_norm': gain((L, D_MODEL)),
        'w_in': w((L, D_MODEL, D_IN), D_MODEL),
        'b_in': bias((L, D_IN)),
        'lru_conv_w': w((L, LRU_CONV_WIDTH, LRU_WIDTH), LRU_CONV_WIDTH),
        'lru_conv_b': bias((L, LRU_WIDTH)),
        'lru_w_gate': w((L, LRU_HEADS, LRU_HEAD_DIM, 2 * LRU_HEAD_DIM), LRU_HEAD_DIM),
        'lru_b_gate': bias((L, LRU_HEADS, 2 * LRU_HEAD_DIM)),
        'lru_lambda': lru_lambda,
        'lru_w_out': w((L, LRU_WIDTH, D_MODEL), LRU_WIDTH),
        'q_norm': gain((L, Q_LORA_RANK)),
        'w_uq': w((L, Q_LORA_RANK, MLA_HEADS * (QK_NOPE_DIM + QK_ROPE_DIM)), Q_LORA_RANK),
        'kv_norm': gain((L, KV_LORA_RANK)),
        'w_ukv': w((L, KV_LORA_RANK, MLA_HEADS * (QK_NOPE_DIM + V_HEAD_DIM)), KV_LORA_RANK),
        'mla_w_o': w((L, MLA_HEADS * V_HEAD_DIM, D_MODEL), MLA_HEADS * V_HEAD_DIM),
        'conv_dw_w': w((L, CONV_WIDTH, CONV_CH), CONV_WIDTH),
        'conv_dw_b': bias((L, CONV_CH)),
        'conv_ln_g': gain((L, CONV_CH)),
        'conv_ln_b': bias((L, CONV_CH)),
        'conv_w_out': w((L, CONV_CH, D_MODEL), CONV_CH),
        'conv_b_out': bias((L, D_MODEL)),
        'w_out': w((L, D_MODEL, D_MODEL), D_MODEL),
        'ffn2_norm': gain((L, D_MODEL)),
        'ffn2_w1': w((L, D_MODEL, 2 * D_FF_2), D_MODEL),
        'ffn2_w2': w((L, D_FF_2, D_MODEL), D_FF_2),
        'final_norm': gain((D_MODEL,)),
    }

def second_block(x, positions, ffn1_norm, ffn1_w1, ffn1_w2, mix_norm, w_in, b_in,
              lru_conv_w, lru_conv_b, lru_w_gate, lru_b_gate, lru_lambda, lru_w_out,
              q_norm, w_uq, kv_norm, w_ukv, mla_w_o,
              conv_dw_w, conv_dw_b, conv_ln_g, conv_ln_b, conv_w_out, conv_b_out,
              w_out, ffn2_norm, ffn2_w1, ffn2_w2, final_norm):
    for l in range(DEPTH):
        x = x + 0.5 * swiglu(rms_norm(x, ffn1_norm[l]), ffn1_w1[l], ffn1_w2[l])
        x = x + hybrid_mixer(
            rms_norm(x, mix_norm[l]), positions, w_in[l], b_in[l],
            lru_conv_w[l], lru_conv_b[l], lru_w_gate[l], lru_b_gate[l], lru_lambda[l], lru_w_out[l],
            q_norm[l], w_uq[l], kv_norm[l], w_ukv[l], mla_w_o[l],
            conv_dw_w[l], conv_dw_b[l], conv_ln_g[l], conv_ln_b[l], conv_w_out[l], conv_b_out[l],
            w_out[l])
        x = x + 0.5 * swiglu(rms_norm(x, ffn2_norm[l]), ffn2_w1[l], ffn2_w2[l])
    return rms_norm(x, final_norm)


def setup_inputs(seed=0):
    out = dict(first_inputs(seed))
    for name, value in second_inputs(seed + 1).items():
        if name != "x":
            out[name + "_2"] = value
    return out


def reference(
    x, mem, positions, g_pre_mix, w_in, w_fourier, sink, g_mem, w_mem_kv, g_grp, w_out,
    g_post_mix, g_pre_ffn, w_ffn_in, w_ffn_out, g_post_ffn, positions_2, ffn1_norm_2, ffn1_w1_2,
    ffn1_w2_2, mix_norm_2, w_in_2, b_in_2, lru_conv_w_2, lru_conv_b_2, lru_w_gate_2,
    lru_b_gate_2, lru_lambda_2, lru_w_out_2, q_norm_2, w_uq_2, kv_norm_2, w_ukv_2, mla_w_o_2,
    conv_dw_w_2, conv_dw_b_2, conv_ln_g_2, conv_ln_b_2, conv_w_out_2, conv_b_out_2, w_out_2,
    ffn2_norm_2, ffn2_w1_2, ffn2_w2_2, final_norm_2,
):
    x = first_block(
        x, mem, positions, g_pre_mix, w_in, w_fourier, sink, g_mem, w_mem_kv, g_grp, w_out,
        g_post_mix, g_pre_ffn, w_ffn_in, w_ffn_out, g_post_ffn,
    )
    return second_block(
        x, positions_2, ffn1_norm_2, ffn1_w1_2, ffn1_w2_2, mix_norm_2, w_in_2, b_in_2,
        lru_conv_w_2, lru_conv_b_2, lru_w_gate_2, lru_b_gate_2, lru_lambda_2, lru_w_out_2,
        q_norm_2, w_uq_2, kv_norm_2, w_ukv_2, mla_w_o_2, conv_dw_w_2, conv_dw_b_2, conv_ln_g_2,
        conv_ln_b_2, conv_w_out_2, conv_b_out_2, w_out_2, ffn2_norm_2, ffn2_w1_2, ffn2_w2_2,
        final_norm_2,
    )


_drawn_inputs = setup_inputs


def setup_inputs(seed=0):
    import zlib

    import numpy as np

    out = dict(_drawn_inputs(seed))
    spreads = {}
    factors = {'sink': 8.0,
     'ffn1_norm_2': 8.0,
     'mix_norm_2': 4.463,
     'lru_conv_b_2': 2.886,
     'lru_b_gate_2': 25.369,
     'q_norm_2': 8.0,
     'kv_norm_2': 8.0,
     'conv_dw_b_2': 20.977,
     'conv_ln_g_2': 64.0,
     'conv_ln_b_2': 64.0,
     'conv_b_out_2': 47.665,
     'ffn2_norm_2': 8.0,
     'final_norm_2': 21.48,
     'b_in_2': 2.826}
    for name, (base, spread) in spreads.items():
        noise = np.random.default_rng([zlib.crc32(name.encode()), seed]).standard_normal(out[name].shape)
        drawn = base * np.exp(spread * noise) if base else spread * noise
        out[name] = __import__('jax').numpy.asarray(drawn.astype(out[name].dtype))
    for name, factor in factors.items():
        out[name] = (out[name] * factor).astype(out[name].dtype)
    return out
```

```python
from contextlib import ExitStack

import numpy as np

import concourse.bass as bass
from concourse import mybir

F32 = mybir.dt.float32
F32R = mybir.dt.float32r
I32 = mybir.dt.int32
ALU = mybir.AluOpType
ACT = mybir.ActivationFunctionType

P = 128
DEPTH = 2
SEQ = 512
D = 1024
DC = D // P
TC = SEQ // P
MEM = 256
FF = 2816
FC = FF // P
HEAD = 64
WINDOW_HEADS = 8
MEM_HEADS = 4
IN_1 = 1280
LRU = 512
LC = LRU // P
Q_RANK = 384
KV_RANK = 256
MLA_HEADS = 8
QK = 96
PE_DIM = 32
CONV_TAPS = 31
LRU_TAPS = 4
IN_B = 1024
IN_C = IN_B + Q_RANK + KV_RANK + PE_DIM
IN_G = IN_C + 1024
D_IN = IN_G + 3 * D
EPS = 1e-6
MASKED = -1e30
UNIT = 16 * P

PARAM_ROWS = [
    ("g_pre_mix", 8), ("g_mem", 8), ("g_grp", 8), ("g_post_mix", 8), ("g_pre_ffn", 8),
    ("g_post_ffn", 8), ("ffn1_norm", 8), ("mix_norm", 8), ("b_a", 8), ("b_b", 5), ("b_kpe", 1),
    ("b_c", 8), ("b_g", 24), ("conv4_w", 16), ("conv4_b", 4), ("b_r", 4), ("b_i", 4),
    ("lambda", 4), ("q_norm", 3), ("kv_norm", 2), ("dw_b", 4), ("ln_g", 4),
    ("ln_b", 4), ("conv_b_out", 8), ("ffn2_norm", 8),
    ("final_norm", DC // DEPTH),
]


def param_columns():
    at, columns = 0, {}
    for name, rows in PARAM_ROWS:
        if at // P != (at + DEPTH * rows - 1) // P:
            at = -(-at // P) * P
        columns[name] = (at, rows)
        at += DEPTH * rows
    at = -(-at // P) * P
    columns["dw_w"] = (at, P)
    return columns, at // P + DEPTH


def rope_frequencies():
    half1 = HEAD // 2
    f1 = np.exp(np.float32(-np.log(10000.0)) * np.arange(half1, dtype=np.float32) * np.float32(2.0 / HEAD))
    f2 = np.float32(10000.0) ** (-np.arange(0, PE_DIM, 2, dtype=np.float32) / np.float32(PE_DIM))
    out = np.zeros((P, 2), np.float32)
    out[:, 0] = np.tile(f1.astype(np.float32), P // half1)
    out[HEAD:HEAD + PE_DIM, 1] = np.tile(f2.astype(np.float32), 2)
    return out


def rotate_half(n, half):
    m = np.zeros((n, n), np.float32)
    for r in range(n):
        base, j = r - r % (2 * half), r % (2 * half)
        if j < half:
            m[base + j + half, r] = -1.0
        else:
            m[base + j - half, r] = 1.0
    return m


CONSTS = {}


def constants():
    parts = []

    def add(name, a):
        wide = np.zeros((P, a.shape[1]), np.float32)
        wide[:a.shape[0]] = a
        CONSTS[name] = (sum(p.shape[1] for p in parts), a.shape[1])
        parts.append(wide)

    i = np.arange(P)
    add("ident", np.eye(P, dtype=np.float32))
    causal = np.where(i[None, :] <= i[:, None], 0.0, MASKED)
    add("causal", np.concatenate([np.zeros((P, 3 * P)), causal], axis=1))
    r96 = np.zeros((P, QK), np.float32)
    r96[HEAD:QK, HEAD:QK] = rotate_half(PE_DIM, PE_DIM // 2)
    add("rot96", r96)
    add("freq", rope_frequencies())
    before = np.where(i[None, :] >= i[:, None], 0.0, MASKED)
    add("window", np.concatenate([before, np.zeros((P, P)), causal], axis=1))
    rot = rotate_half(P, HEAD // 2)
    add("rot_q", rot)
    for j in range(2):
        dup = np.zeros((P, P), np.float32)
        dup[HEAD * j + i % HEAD, i] = 1.0
        add(f"dup{j}", dup)
        add(f"rot_k{j}", dup @ rot)
    n = np.arange(HEAD)
    ang = 2 * np.pi * ((n[:, None] * n[None, :]) % HEAD) / HEAD
    for name, m in (("dft_cos", np.cos(ang) / 8.0), ("dft_sin", -np.sin(ang) / 8.0)):
        add(name, np.kron(np.eye(2), m).astype(np.float32))
    return np.ascontiguousarray(np.concatenate(parts, axis=1).astype(np.float32))


def sequence_dft():
    n = np.arange(SEQ)
    ang = 2 * np.pi * ((n[:, None] * n[None, :]) % SEQ) / SEQ
    return np.ascontiguousarray(
        (np.stack([np.cos(ang), np.sin(ang)], axis=1) / np.sqrt(SEQ)).astype(np.float32))


class Tally:

    wrong = []
    carrier = None

    def __init__(self, eng_name):
        self.eng_name = eng_name
        self.before, self.n = {}, {}
        self.layer = self.turn = None
        self.per_layer, self.per_turn = {}, {}
        self.unit = self.split = self.group = 0

    def apart(self, eng):
        eng.sem_inc(self.carrier, 1)

    def one(self, name, by=1):
        self.n[name] = self.n.get(name, 0) + by
        return by

    def now(self, name):
        value = self.before.get(name, 0) + self.n.get(name, 0)
        if self.layer is not None and self.per_layer.get(name, 0):
            value = self.layer * self.per_layer[name] + value
        if self.turn is not None and self.per_turn.get(name, 0):
            value = self.turn * self.per_turn[name] + value
        return value

    def next(self, name, by=1):
        self.one(name, by)
        return self.now(name)

    def layers(self, eng, per_layer, label):
        self.apart(eng)
        with eng.Fori(0, DEPTH) as layer:
            for name, n in self.n.items():
                self.before[name] = self.before.get(name, 0) + n
            self.layer, self.n, self.per_layer = layer, {}, per_layer
            yield layer
            for name, n in self.n.items():
                if n and n != per_layer.get(name, 0):
                    self.wrong.append((label, name, n, self.eng_name))
            for name, n in per_layer.items():
                self.before[name] = self.before.get(name, 0) + DEPTH * n
            self.layer, self.n = None, {}

    def turns(self, eng, first, end, per_turn, label):
        start = dict(self.n)
        self.apart(eng)
        with eng.Fori(first, end) as turn:
            self.per_turn = per_turn
            self.turn = turn
            for name, n in per_turn.items():
                self.n[name] = self.n.get(name, 0) - first * n
            shifted = dict(self.n)
            yield turn
            for name in set(self.n):
                made = self.n[name] - shifted.get(name, 0)
                if name in per_turn and made == 0:
                    self.n[name] = start.get(name, 0)
                    continue
                if made != per_turn.get(name, 0):
                    self.wrong.append((label, name, made, self.eng_name))
                self.n[name] = start.get(name, 0) + (end - first) * made
            self.turn = None


GROUPS = ((0, 1), (2, 3, 4, 5), (6, 7))

PER_LAYER = {
    "one": {"ah_ready": 32, "al_ready": 32, "c1_loaded": 128, "dft_loaded": 16, "diag_ready": 8,
        "dve_step": 202, "e_ready": 48, "four_copied": 7, "four_ready": 7, "h_ready": 11, "hh_ready": 11,
        "hi_ready": 46, "hl_ready": 11, "lo_ready": 46, "m_ready": 48, "mem_loaded": 16, "o_ready": 6,
        "o_used": 6, "p_ready": 48, "piece_done": 46, "pow_asked": 8, "pow_done": 8, "pt_ready": 48,
        "raw_loaded0": 736, "raw_loaded1": 736, "read_out0": 19, "read_out1": 19, "rope_ready": 6,
        "rot_ready": 8, "rot_used": 8, "s_ready": 48, "silu_ready": 11, "sq_ready": 48, "sq_used": 48,
        "src_ready": 8, "sum_ready": 16, "swap_copied": 6, "swap_ready": 6, "t_ready": 48, "wf_loaded": 32,
        "wf_zeroed": 1, "x_ready": 2},
    "two": {"act_step": 4, "ah_ready": 57, "al_ready": 37, "bias_done": 18, "branch_ready": 8,
        "centred": 1, "conv_done": 1, "diag_ready": 6, "dve_step": 256, "e2_ready": 4, "e_ready": 32,
        "gate_loaded": 64, "gate_ready": 16, "gate_zeroed": 1, "gates_ready": 8, "h_ready": 22,
        "hh_ready": 22, "hi_ready": 110, "hl_ready": 30, "ln_ready": 1, "lo_ready": 110, "m_ready": 32,
        "mean_ready": 1, "merged_ready": 8, "o_ready": 4, "o_used": 4, "p_ready": 32, "piece_done": 116,
        "pow_asked": 6, "pow_done": 6, "pt_ready": 32, "raw_loaded0": 1760, "raw_loaded1": 1760,
        "read_out0": 50, "read_out1": 50, "region_free": 1, "root_asked": 4, "root_done": 4,
        "rope_ready": 16, "rot_ready": 9, "rot_used": 9, "s_ready": 32, "sig_ready": 8, "silu_ready": 22,
        "sq_ready": 33, "sq_used": 33, "src_ready": 13, "sum_ready": 12, "swap_copied": 8, "swap_ready": 8,
        "t_ready": 32, "v_ready": 4, "x_ready": 3, "xa_ready": 4},
}
PER_TURN = {
    "ffn_in": {"h_ready": 1, "hh_ready": 1, "hi_ready": 2, "hl_ready": 1, "lo_ready": 2, "piece_done": 2,
        "raw_loaded0": 32, "raw_loaded1": 32, "read_out0": 1, "read_out1": 1, "silu_ready": 1},
    "ffn_out": {"hi_ready": 6, "lo_ready": 6, "piece_done": 6, "raw_loaded0": 96, "raw_loaded1": 96,
        "read_out0": 1, "read_out1": 1, "sq_ready": 4, "sq_used": 4},
    "w_out": {"hi_ready": 2, "lo_ready": 2, "piece_done": 2, "raw_loaded0": 32, "raw_loaded1": 32,
        "read_out0": 1, "read_out1": 1},
    "merge": {"ah_ready": 2, "dve_step": 4, "gate_ready": 4, "hi_ready": 6, "hl_ready": 2, "lo_ready": 6,
        "merged_ready": 2, "piece_done": 6, "raw_loaded0": 96, "raw_loaded1": 96, "read_out0": 3,
        "read_out1": 3, "src_ready": 2},
}


def two_blocks(nc, t, out):
    columns, n_param_tiles = param_columns()

    base = -(-nc.sbuf_base // 64) * 64
    top = [base]

    def place(name, shape, dt=F32, at=None):
        size = 4 * int(np.prod(shape[1:]))
        offset = top[0] if at is None else at
        if at is None:
            top[0] += -(-size // 32) * 32
        return nc.alloc_sbuf_tensor_at(name, shape, dt, offset=offset)

    KB = 1024
    xT = place("xT", [P, DC, SEQ])
    raw = place("raw", [P, 2, UNIT])
    w_hi = place("w_hi", [P, 2, UNIT], F32R)
    w_lo = place("w_lo", [P, 2, UNIT], F32R)
    ident = place("ident", [P, P])
    ones = place("ones", [P, P])
    rot96 = place("rot96", [P, QK])
    causal = place("causal", [P, SEQ])
    freq = place("freq", [P, 2])
    params = place("params", [P, n_param_tiles * P])
    stats = place("stats", [P, 4, 32])
    sinks = place("sinks", [P, DEPTH * WINDOW_HEADS])
    decay = place("decay", [P, 2, DEPTH * LC])
    tiny = place("tiny", [P, 6, DEPTH * LC])
    mean_sq = place("mean_sq", [P, TC])
    minus_half = place("minus_half", [P, TC])
    rs = place("rs", [P, SEQ])
    rs_b = place("rs_b", [P, SEQ])
    cosT = place("cosT", [P, SEQ])
    sinT = place("sinT", [P, SEQ])
    X = place("X", [P, 4, SEQ])
    REGION_A = top[0]
    a_hi = place("a_hi", [P, DC, SEQ], F32R)
    a_lo = place("a_lo", [P, DC, SEQ], F32R)
    y_ffn = place("y_ffn", [P, DC, SEQ], at=REGION_A)
    dft = place("dft", [P, TC, 2, SEQ], at=REGION_A)
    ab = place("ab", [P, TC, SEQ], at=REGION_A + 16 * KB)
    rows = place("rows", [P, n_param_tiles, P], at=REGION_A)
    out_tok = place("out_tok", [P, TC, D], at=REGION_A)
    REGION_B = top[0]
    h_hi = place("h_hi", [P, FC, SEQ], F32R)
    h_lo = place("h_lo", [P, FC, SEQ], F32R)
    x_tok = place("x_tok", [P, TC, D], at=REGION_B)
    b1 = [REGION_B]

    def in_b(name, shape, dt=F32):
        at = b1[0]
        b1[0] += 4 * int(np.prod(shape[1:]))
        assert b1[0] <= top[0]
        return place(name, shape, dt, at=at)

    mem_tok = place("mem_tok", [P, MEM // P, D], at=REGION_B)
    memT = place("memT", [P, DC, MEM], at=REGION_B + 8 * KB)
    y_mix = in_b("y_mix", [P, DC, SEQ])
    zfT = in_b("zfT", [P, 2, SEQ])
    qT = in_b("qT", [P, 4, SEQ])
    zkT = in_b("zkT", [P, SEQ])
    kT = in_b("kT", [P, 2, SEQ])
    vT = in_b("vT", [P, SEQ])
    v_tok = in_b("v_tok", [P, TC, P])
    zmT = in_b("zmT", [P, 2, SEQ])
    kmT = in_b("kmT", [P, 2, MEM])
    vmT = in_b("vmT", [P, 2, MEM])
    vm_tok = in_b("vm_tok", [P, 2, 2 * P])
    wf = in_b("wf", [P, 2, P])
    mf = in_b("mf", [P, 2, 2, P])
    c1 = {name: in_b("c_" + name, [P, CONSTS[name][1]])
          for name in ("window", "rot_q", "dup0", "rot_k0", "dup1", "rot_k1", "dft_cos", "dft_sin")}
    m_hi = in_b("m_hi", [P, DC, MEM], F32R)
    m_lo = in_b("m_lo", [P, DC, MEM], F32R)
    b1[0] = REGION_B
    yc_hi = in_b("yc_hi", [P, LC, SEQ], F32R)
    yc_lo = in_b("yc_lo", [P, LC, SEQ], F32R)
    ya_hi = in_b("ya_hi", [P, LC, SEQ], F32R)
    ya_lo = in_b("ya_lo", [P, LC, SEQ], F32R)
    yb_hi = in_b("yb_hi", [P, LC, SEQ], F32R)
    yb_lo = in_b("yb_lo", [P, LC, SEQ], F32R)
    REGION_T = b1[0]
    conv = in_b("conv", [P, LC, SEQ])
    gelu = in_b("gelu", [P, LC, SEQ])
    xa = in_b("xa", [P, LC, SEQ])
    glu = in_b("glu", [P, LC, SEQ + CONV_TAPS - 1])
    xpad = place("xpad", [P, LC, SEQ + LRU_TAPS - 1], at=REGION_B)
    sig = place("sig", [P, LC, 2, SEQ], at=REGION_B)
    craw = place("craw", [P, 6, SEQ], at=REGION_B + 32 * KB)
    gate_w = place("gate_w", [P, LC, 2, P], at=REGION_B + 44 * KB)
    q_head = place("q_head", [P, MLA_HEADS, SEQ], at=REGION_T)
    kv_head = place("kv_head", [P, MLA_HEADS, SEQ], at=REGION_T + 16 * KB)
    v_head = place("v_head", [P, TC, MLA_HEADS * HEAD], at=REGION_T + 32 * KB)
    mg_hi = place("mg_hi", [P, DC, SEQ], F32R, at=REGION_T)
    mg_lo = place("mg_lo", [P, DC, SEQ], F32R, at=REGION_T + 16 * KB)

    def step(q, k, v, n, out, mask, opens, closes, scale, sink=None):
        return dict(q=q, k=k, v=v, n=n, out=out, mask=mask, opens=opens, closes=closes, scale=scale, sink=sink)

    def window_steps(q, k, v):
        steps = []
        for h in range(WINDOW_HEADS):
            half, kv = (h % 2) * HEAD, h // (WINDOW_HEADS // 2)
            for b in range(TC):
                first, end = max(b - 1, 0), min(b + 2, TC)
                steps.append(step(
                    q[half:half + HEAD, h // 2, b * P:(b + 1) * P], k[half:half + HEAD, kv, first * P:end * P],
                    [v[:, j, kv * HEAD:(kv + 1) * HEAD] for j in range(first, end)], (end - first) * P,
                    (half, b * P), c1["window"][:, (first - b + 1) * P:(end - b + 1) * P],
                    h % 2 == 0 and b == 0, h % 2 == 1 and b == TC - 1, HEAD ** -0.5, h))
        return steps

    def memory_steps(q, k, v):
        steps = []
        for h in range(MEM_HEADS):
            half = (h % 2) * HEAD
            for b in range(TC):
                steps.append(step(
                    q[half:half + HEAD, h // 2, b * P:(b + 1) * P], k[half:half + HEAD, h // 2, :],
                    [v[:, j, h * HEAD:(h + 1) * HEAD] for j in range(MEM // P)], MEM,
                    (half, b * P), causal[:, 0:MEM], h % 2 == 0 and b == 0, h % 2 == 1 and b == TC - 1, HEAD ** -0.5))
        return steps

    def mla_steps(q, k, v):
        steps = []
        for h in range(MLA_HEADS):
            for b in range(TC):
                n = (b + 1) * P
                steps.append(step(
                    q[0:QK, h, b * P:n], k[0:QK, h, 0:n], [v[:, j, h * HEAD:(h + 1) * HEAD] for j in range(b + 1)], n,
                    ((h % 2) * HEAD, b * P), causal[:, SEQ - n:SEQ], h % 2 == 0 and b == 0, h % 2 == 1 and b == TC - 1,
                    QK ** -0.5))
        return steps

    stack = ExitStack()
    with stack:
        G = [stack.enter_context(nc.psum_tensor(f"products{i}", [P, 2, SEQ], F32)) for i in range(2)]
        B4, B5, B6, B7 = (stack.enter_context(nc.psum_tensor(f"small{i}", [P, SEQ], F32)) for i in range(4))
        sems = {}

        def sem(name):
            sems[name] = stack.enter_context(nc.semaphore(name))
            return sems[name]

        raw_loaded = [sem("raw_loaded0"), sem("raw_loaded1")]
        hi_ready = sem("hi_ready")
        lo_ready = sem("lo_ready")
        piece_done = sem("piece_done")
        read_out = [sem("read_out0"), sem("read_out1")]
        consts_loaded, x_loaded, rows_zeroed = sem("consts_loaded"), sem("x_loaded"), sem("rows_zeroed")
        rows_loaded, pos_loaded, turned = sem("rows_loaded"), sem("pos_loaded"), sem("turned")
        turn_copied, angle, table = sem("turn_copied"), sem("angle"), sem("table")
        soft_in, soft_exp, setup_done = sem("soft_in"), sem("soft_exp"), sem("setup_done")
        sin_done = sem("sin_done")
        x_ready = sem("x_ready")
        src_ready = sem("src_ready")
        ah_ready, al_ready = sem("ah_ready"), sem("al_ready")
        sq_ready, sq_used = sem("sq_ready"), sem("sq_used")
        sum_ready = sem("sum_ready")
        pow_asked, pow_done = sem("pow_asked"), sem("pow_done")
        diag_ready = sem("diag_ready")
        root_asked, root_done = sem("root_asked"), sem("root_done")
        dve_step, act_step, pool_step = sem("dve_step"), sem("act_step"), sem("pool_step")
        silu_ready, h_ready, hh_ready, hl_ready = (sem(n) for n in ("silu_ready", "h_ready", "hh_ready", "hl_ready"))
        y_copied = sem("y_copied")
        mem_loaded, c1_loaded, wf_zeroed, wf_loaded, dft_loaded = (
            sem(n) for n in ("mem_loaded", "c1_loaded", "wf_zeroed", "wf_loaded", "dft_loaded"))
        rot_ready, rot_used, rope_ready = sem("rot_ready"), sem("rot_used"), sem("rope_ready")
        swap_ready, swap_copied = sem("swap_ready"), sem("swap_copied")
        four_ready, four_copied = sem("four_ready"), sem("four_copied")
        s_ready, m_ready, e_ready, p_ready = (sem(n) for n in ("s_ready", "m_ready", "e_ready", "p_ready"))
        t_ready, pt_ready, o_ready, o_used = (sem(n) for n in ("t_ready", "pt_ready", "o_ready", "o_used"))
        region_free, gate_zeroed, gate_loaded = sem("region_free"), sem("gate_zeroed"), sem("gate_loaded")
        branch_ready = sem("branch_ready")
        bias_done, xa_ready = sem("bias_done"), sem("xa_ready")
        gates_ready, sig_ready, e2_ready, v_ready = (sem(n) for n in ("gates_ready", "sig_ready", "e2_ready", "v_ready"))
        conv_done, mean_ready, centred, ln_ready = (sem(n) for n in ("conv_done", "mean_ready", "centred", "ln_ready"))
        gate_ready, merged_ready = sem("gate_ready"), sem("merged_ready")
        final_ready, tok_copied, stored = sem("final_ready"), sem("tok_copied"), sem("stored")

        Tally.carrier = sem("wait_carrier")
        row_loads = row_copies(t, rows, columns)
        n_setup_loads = 5

        block = stack.enter_context(nc.Block())

        def col(name, l, c, last=P):
            first, step = columns[name]
            return params[0:last, bass.ds(l * step + (first + c), 1)]

        def wide(ap, n):
            return ap.unsqueeze(1).broadcast_to([ap.shape[0], n, ap.shape[-1]])

        @block.sync
        def _(sp):
            c = Tally("sync")
            sp.dma_start(x_tok[:], t["x"].rearrange("o (t p) d -> p (o t) d", p=P)).then_inc(x_loaded, 16)

            def unit(*parts):
                s = c.unit % 2
                c.unit += 1
                assert len(parts) == 2
                sp.wait_ge(lo_ready, c.next("lo_ready"))
                c.apart(sp)
                for w, l, row, nk, first, n, at in parts:
                    sp.dma_start(
                        raw[:, s, at:at + nk * n].rearrange("p (k n) -> p k n", n=n),
                        t[w][bass.ds(l, 1), row:row + nk * P, bass.ds(first, n)].rearrange("o (k p) n -> p (o k) n", p=P),
                    ).then_inc(raw_loaded[s], 16)

            def tall(w, l, first, n=2 * P, row=0, nk=DC):
                half = nk // 2
                unit((w, l, row, half, first, n, 0), (w, l, row + half * P, nk - half, first, n, half * n))

            def ffn(w1, w2, l, label):
                tall(w1, l, 0)
                tall(w1, l, FF)
                for i in c.turns(sp, 1, FF // (2 * P), PER_TURN["ffn_in"], "ffn_in"):
                    tall(w1, l, i * (2 * P))
                    tall(w1, l, i * (2 * P) + FF)
                for i in c.turns(sp, 0, 2, PER_TURN["ffn_out"], "ffn_out"):
                    for j in range(2):
                        for row, nk in ((0, 8), (8, 8), (16, 6)):
                            tall(w2, l, i * (4 * P) + 2 * P * j, row=row * P, nk=nk)

            for l in c.layers(sp, PER_LAYER["one"], "one"):
                tall("w_in", l, 0)
                tall("w_in", l, 2 * P)
                tall("w_in", l, 4 * P)
                tall("w_in", l, 6 * P, P)
                tall("w_in", l, 7 * P, P)
                tall("w_in", l, 8 * P)
                for j in range(2):
                    tall("w_mem_kv", l, 2 * P * j)
                for i in c.turns(sp, 0, 2, PER_TURN["w_out"], "w_out"):
                    for j in range(2):
                        tall("w_out", l, i * (4 * P) + 2 * P * j)
                ffn("w_ffn_in", "w_ffn_out", l, "one")
            for l in c.layers(sp, PER_LAYER["two"], "two"):
                ffn("ffn1_w1_2", "ffn1_w2_2", l, "two")
                for j in range(LC):
                    unit(("w_in_2", l, 0, DC, IN_C + P * j, P, 0), ("w_in_2", l, 0, DC, IN_C + LRU + P * j, P, UNIT // 2))
                for j in range(4):
                    tall("w_in_2", l, 2 * P * j)
                tall("w_in_2", l, IN_B)
                tall("w_in_2", l, IN_B + 2 * P)
                tall("w_in_2", l, IN_B + 4 * P, n=P + PE_DIM)
                for j in range(2):
                    unit(("w_uq_2", l, 0, 2, 4 * QK * j, 4 * QK, 0), ("w_uq_2", l, 2 * P, 1, 4 * QK * j, 4 * QK, 8 * QK))
                unit(("w_ukv_2", l, 0, 1, 0, 2 * LRU, 0), ("w_ukv_2", l, P, 1, 0, 2 * LRU, 2 * LRU))
                for i in c.turns(sp, 0, DC // 2, PER_TURN["merge"], "merge"):
                    for j in range(2):
                        at = i * (2 * P) + P * j
                        unit(("w_in_2", l, 0, DC, at + IN_G, P, 0), ("w_in_2", l, 0, DC, at + (IN_G + D), P, UNIT // 2))
                        unit(("w_in_2", l, 0, DC, at + (IN_G + 2 * D), P, 0), ("lru_w_out_2", l, 0, LC, at, P, UNIT // 2))
                        unit(("mla_w_o_2", l, 0, LC, at, P, 0), ("conv_w_out_2", l, 0, LC, at, P, LC * P))
                for i in c.turns(sp, 0, 2, PER_TURN["w_out"], "w_out"):
                    for j in range(2):
                        tall("w_out_2", l, i * (4 * P) + 2 * P * j)
                ffn("ffn2_w1_2", "ffn2_w2_2", l, "two")
            for s in range(2):
                sp.wait_ge(lo_ready, c.next("lo_ready"))
                sp.sem_inc(raw_loaded[s], 32)
            for tc in range(TC):
                sp.wait_ge(tok_copied, c.next("tok_copied"))
                sp.dma_start(out[0, tc * P:(tc + 1) * P, :], out_tok[:, tc, :]).then_inc(stored, 16)
            sp.wait_ge(stored, 16 * TC)

        @block.tensor
        def _(pe):
            c = Tally("tensor")
            c.n["lo_ready"] = 2
            c.n["sq_used"] = 1

            def take_unit():
                pe.wait_ge(lo_ready, c.next("lo_ready"))
                c.unit += 1

            def piece(blocks, first=True, last=True, n=SEQ, fresh=None):
                s = (c.unit - 1) % 2
                pair = c.group % 2
                if first:
                    pe.wait_ge(read_out[pair], c.next(f"read_out{pair}"))
                for b, (m, terms) in enumerate(blocks):
                    for k, (at, hi, lo) in enumerate(terms):
                        if fresh and b == 0:
                            pe.wait_ge(sems[fresh], c.next(fresh))
                        for q, (w, x) in enumerate(((w_hi, hi), (w_hi, lo), (w_lo, hi))):
                            mm = pe.matmul(G[pair][0:m, b, 0:n], w[:, s, at:at + m], x,
                                           start=first and k == 0 and q == 0,
                                           stop=last and k == len(terms) - 1 and q == 2)
                mm.then_inc(piece_done, 1)
                if last:
                    c.group += 1

            def tall(nk, width, hi, lo, k0=0, blocks=2, **how):
                piece([(P, [(k * width + b * P, hi[:, k0 + k, :], lo[:, k0 + k, :]) for k in range(nk)])
                       for b in range(blocks)], **how)

            def full(fresh=None, blocks=2, hi=a_hi, lo=a_lo, n=SEQ):
                take_unit()
                tall(DC, blocks * P, hi, lo, blocks=blocks, fresh=fresh, n=n)

            def sum_channels(n=SEQ):
                pe.wait_ge(sq_used, c.now("sq_used"))
                for i in range(n // P):
                    mm = pe.matmul(B7[:, i:i + 1], X[:, 1, i * P:(i + 1) * P], ones[:, 0:1], start=True, stop=True)
                mm.then_inc(sum_ready, 1)
                pe.wait_ge(diag_ready, c.next("diag_ready"))
                pe.matmul(B7[:, 0:n], ones[:], X[:, 1, 0:n], start=True, stop=True).then_inc(sum_ready, 1)

            def ffn(post_norm):
                full(fresh="al_ready")
                c.one("sq_used", DC)
                sum_channels()
                full()
                for _ in c.turns(pe, 1, FF // (2 * P), PER_TURN["ffn_in"], "ffn_in"):
                    full()
                    full()
                pe.wait_ge(hl_ready, c.next("hl_ready", FF // (2 * P)))
                for _ in c.turns(pe, 0, 2, PER_TURN["ffn_out"], "ffn_out"):
                    for j in range(2):
                        for k0, nk in ((0, 8), (8, 8), (16, 6)):
                            take_unit()
                            tall(nk, 2 * P, h_hi, h_lo, k0=k0, first=k0 == 0, last=k0 == 16)
                if post_norm:
                    c.one("sq_used", DC)
                    sum_channels()

            def attention(steps):
                n = len(steps)
                for s in range(n + 2):
                    if s < n:
                        st = steps[s]
                        bank = (B4, B5)[s % 2]
                        pe.matmul(bank[:, 0:st["n"]], st["q"], st["k"], start=True, stop=True).then_inc(s_ready, 1)
                    if 1 <= s <= n:
                        st = steps[s - 1]
                        pe.wait_ge(p_ready, c.next("p_ready"))
                        if s >= 2:
                            pe.wait_ge(pt_ready, c.now("pt_ready") + 1)
                        for j in range(st["n"] // P):
                            mm = pe.transpose(B6[:, j * P:(j + 1) * P], X[:, (s - 1) % 2, j * P:(j + 1) * P], ident[:])
                        mm.then_inc(t_ready, 1)
                    if s >= 2:
                        st = steps[s - 2]
                        pe.wait_ge(pt_ready, c.next("pt_ready"))
                        if st["opens"] and s > 2:
                            pe.wait_ge(o_used, c.next("o_used"))
                        vs = st["v"]
                        r0, c0 = st["out"]
                        for j, v in enumerate(vs):
                            mm = pe.matmul(B7[r0:r0 + HEAD, c0:c0 + P], v, X[:, 2 + s % 2, j * P:(j + 1) * P],
                                           start=j == 0, stop=j == len(vs) - 1)
                        if st["closes"]:
                            mm.then_inc(o_ready, 1)
                c.one("o_used")

            def all_read_out():
                for p in range(2):
                    pe.wait_ge(read_out[p], c.now(f"read_out{p}") + 1)

            pe.wait_ge(consts_loaded, c.next("consts_loaded", 16 * n_setup_loads))
            pe.wait_ge(rows_loaded, c.next("rows_loaded", 16 * len(row_loads)))
            for i in range(n_param_tiles):
                if i >= 2:
                    pe.wait_ge(turn_copied, i - 1)
                pe.transpose((B4, B5)[i % 2][:, 0:P], rows[:, i, :], ident[:]).then_inc(turned, 1)
            pe.wait_ge(x_loaded, 16)
            for i in range(DC):
                pe.wait_ge(turn_copied, n_param_tiles + i - 1)
                for tc in range(TC):
                    mm = pe.transpose((B4, B5)[(n_param_tiles + i) % 2][:, tc * P:(tc + 1) * P], x_tok[:, tc, i * P:(i + 1) * P], ident[:])
                mm.then_inc(turned, 1)

            for l in c.layers(pe, PER_LAYER["one"], "one"):
                full(fresh="al_ready")
                c.one("sq_used", DC)
                sum_channels()
                pe.wait_ge(mem_loaded, c.next("mem_loaded", 16))
                for i in range(DC // 2):
                    if i:
                        pe.wait_ge(swap_copied, c.next("swap_copied"))
                    for j in range(4):
                        mm = pe.transpose(B6[:, j * P:(j + 1) * P],
                                          mem_tok[:, j % 2, (2 * i + j // 2) * P:(2 * i + j // 2 + 1) * P], ident[:])
                    mm.then_inc(swap_ready, 1)
                c.one("swap_copied")
                full()
                full()
                full(blocks=1)
                full(blocks=1)
                full()
                take_unit()
                tall(DC, 2 * P, m_hi, m_lo, fresh="al_ready", n=MEM)
                c.one("sq_used", DC)
                sum_channels(MEM)
                full(hi=m_hi, lo=m_lo, n=MEM)
                pe.wait_ge(c1_loaded, c.next("c1_loaded", 16 * len(c1)))
                all_read_out()
                for i in range(4):
                    if i >= 2:
                        pe.wait_ge(rot_used, c.next("rot_used"))
                    pe.matmul((B4, B5)[i % 2][:], c1["rot_q"][:], qT[:, i, :], start=True, stop=True).then_inc(rot_ready, 1)
                for j in range(2):
                    for bank, name in ((B4, f"dup{j}"), (B5, f"rot_k{j}")):
                        pe.wait_ge(rot_used, c.next("rot_used"))
                        pe.matmul(bank[:], c1[name][:], zkT[:], start=True, stop=True).then_inc(rot_ready, 1)
                c.one("rot_used", 2)
                pe.wait_ge(swap_copied, c.now("swap_copied"))
                for j in range(TC):
                    mm = pe.transpose(B6[:, j * P:(j + 1) * P], vT[:, j * P:(j + 1) * P], ident[:])
                mm.then_inc(swap_ready, 1)
                for j in range(4):
                    mm = pe.transpose(B7[:, j * P:(j + 1) * P], vmT[:, j % 2, (j // 2) * P:(j // 2 + 1) * P], ident[:])
                mm.then_inc(swap_ready, 1)
                pe.wait_ge(wf_loaded, c.next("wf_loaded", 32))
                pe.wait_ge(rot_used, c.now("rot_used"))
                for j in range(2):
                    for i, name in enumerate(("dft_cos", "dft_sin")):
                        at = (2 * j + i) * P
                        mm = pe.matmul(B4[:, at:at + P], c1[name][:], wf[:, j, :], start=True, stop=True)
                mm.then_inc(four_ready, 1)
                for tc in range(TC):
                    pe.wait_ge(four_copied, c.next("four_copied"))
                    for j in range(2):
                        mm = pe.matmul((B5, B4)[tc % 2][:, j * 2 * P:(j + 1) * 2 * P], zfT[:, j, tc * P:(tc + 1) * P],
                                       mf[:, j, :, :], start=True, stop=True)
                    mm.then_inc(four_ready, 1)
                pe.wait_ge(four_copied, c.next("four_copied"))
                pe.wait_ge(dft_loaded, c.next("dft_loaded", 16))
                for j in range(2):
                    for tc in range(TC):
                        for i in range(2):
                            mm = pe.matmul((B4, B5)[j][:], ab[:, tc, (2 * j + i) * P:(2 * j + i + 1) * P], dft[:, tc, i, :],
                                           start=tc == 0 and i == 0, stop=tc == TC - 1 and i == 1)
                    mm.then_inc(four_ready, 1)
                c.one("four_copied", 2)
                pe.wait_ge(four_copied, c.now("four_copied"))
                c.one("swap_copied", 2)
                pe.wait_ge(swap_copied, c.now("swap_copied"))
                pe.wait_ge(rope_ready, c.next("rope_ready", 6))
                attention(window_steps(qT, kT, v_tok))
                attention(memory_steps(zmT, kmT, vm_tok))
                for chunks in GROUPS:
                    c.one("sq_used", len(chunks))
                    sum_channels()
                take_unit()
                tall(DC, 2 * P, a_hi, a_lo, fresh="al_ready")
                full()
                full()
                full()
                c.one("sq_used", DC)
                sum_channels()
                ffn(True)
            for l in c.layers(pe, PER_LAYER["two"], "two"):
                ffn(False)
                full_two_parts = [(P, [(b * UNIT // 2 + k * P, a_hi[:, k, :], a_lo[:, k, :]) for k in range(DC)]) for b in range(2)]
                take_unit()
                piece(full_two_parts, fresh="al_ready")
                c.one("sq_used", DC)
                sum_channels()
                for _ in range(LC - 1):
                    take_unit()
                    piece(full_two_parts)
                for _ in range(4):
                    full()
                full()
                full()
                take_unit()
                wide_n = P + PE_DIM
                piece([(P, [(k * wide_n, a_hi[:, k, :], a_lo[:, k, :]) for k in range(DC)])])
                piece([(QK, [(k * wide_n + HEAD, a_hi[:, k, :], a_lo[:, k, :]) for k in range(DC)])])
                pe.wait_ge(gate_loaded, c.next("gate_loaded", 64))
                for i in range(LC):
                    pe.wait_ge(xa_ready, c.next("xa_ready"))
                    if i:
                        pe.wait_ge(sig_ready, c.next("sig_ready", 2))
                    for j in range(2):
                        pe.matmul((B4, B5)[j][:], gate_w[:, i, j, :], xa[:, i, :], start=True, stop=True).then_inc(gates_ready, 1)
                c.one("sig_ready", 2)
                pe.wait_ge(conv_done, c.next("conv_done"))
                for i in range(LC):
                    mm = pe.matmul(B7[:], ones[:], conv[:, i, :], start=i == 0, stop=i == LC - 1)
                mm.then_inc(mean_ready, 1)
                c.one("sq_used", LC)
                sum_channels()
                c.one("sq_used", 3)
                sum_channels()
                c.one("sq_used", 2)
                sum_channels()
                for u in range(2):
                    take_unit()
                    for g in range(2):
                        piece([(QK, [(k * 4 * QK + (2 * g + b) * QK, a_hi[:, k, :], a_lo[:, k, :]) for k in range(3)])
                               for b in range(2)], fresh="al_ready" if u == g == 0 else None)
                take_unit()
                for g in range(4):
                    piece([(P, [(k * 2 * LRU + (2 * g + b) * P, a_hi[:, 3 + k, :], a_lo[:, 3 + k, :]) for k in range(2)])
                           for b in range(2)], fresh="al_ready" if g == 0 else None)
                pe.wait_ge(sig_ready, c.now("sig_ready"))
                all_read_out()
                pe.matmul(B4[0:QK, :], rot96[0:QK, :], craw[0:QK, 5, :], start=True, stop=True).then_inc(rot_ready, 1)
                for h in range(MLA_HEADS):
                    if h >= 1:
                        pe.wait_ge(rot_used, c.next("rot_used"))
                    pe.matmul((B5, B4)[h % 2][0:QK, :], rot96[0:QK, :], q_head[0:QK, h, :], start=True, stop=True).then_inc(rot_ready, 1)
                c.one("rot_used", 2)
                for h in range(MLA_HEADS):
                    if h:
                        pe.wait_ge(swap_copied, c.next("swap_copied"))
                    for j in range(TC):
                        mm = pe.transpose(B6[:, j * P:(j + 1) * P], kv_head[:, h, j * P:(j + 1) * P], ident[:])
                    mm.then_inc(swap_ready, 1)
                c.one("swap_copied")
                pe.wait_ge(swap_copied, c.now("swap_copied"))
                pe.wait_ge(rope_ready, c.next("rope_ready", 2 * MLA_HEADS))
                pe.wait_ge(rot_used, c.now("rot_used"))
                attention(mla_steps(q_head, kv_head, v_head))
                pe.wait_ge(o_used, c.now("o_used"))
                pe.wait_ge(branch_ready, c.next("branch_ready", 2 * LC))
                pe.wait_ge(al_ready, c.next("al_ready", DC))

                def eight(at):
                    return (P, [(at + k * P, a_hi[:, k, :], a_lo[:, k, :]) for k in range(DC)])

                def four(at, hi, lo):
                    return (P, [(at + k * P, hi[:, k, :], lo[:, k, :]) for k in range(LC)])

                for _ in c.turns(pe, 0, DC // 2, PER_TURN["merge"], "merge"):
                    for j in range(2):
                        take_unit()
                        piece([eight(0), eight(UNIT // 2)])
                        take_unit()
                        piece([eight(0), four(UNIT // 2, ya_hi, ya_lo)])
                        take_unit()
                        piece([four(0, yb_hi, yb_lo), four(LC * P, yc_hi, yc_lo)])
                pe.wait_ge(hl_ready, c.next("hl_ready", DC))
                for _ in c.turns(pe, 0, 2, PER_TURN["w_out"], "w_out"):
                    for j in range(2):
                        take_unit()
                        tall(DC, 2 * P, mg_hi, mg_lo)
                ffn(False)
            c.one("sq_used", DC)
            sum_channels()
            pe.wait_ge(final_ready, 1)
            for tc in range(TC):
                if tc:
                    pe.wait_ge(tok_copied, tc)
                for i in range(DC):
                    mm = pe.transpose((B4, B5)[i // 4][:, (i % 4) * P:(i % 4 + 1) * P], xT[:, i, tc * P:(tc + 1) * P], ident[:])
                mm.then_inc(turned, 1)

        @block.scalar
        def _(act):
            c = Tally("scalar")
            c.n.update(read_out0=1, read_out1=1, sq_used=1)

            def split_hi():
                s = c.split % 2
                c.split += 1
                act.wait_ge(raw_loaded[s], c.next(f"raw_loaded{s}", 32))
                act.activation(w_hi[:, s, :], raw[:, s, :], ACT.Copy).then_inc(hi_ready, 1)

            def unit_done(pieces=1):
                act.wait_ge(piece_done, c.next("piece_done", pieces))
                split_hi()

            def out_name():
                name = c.group % 2
                c.group += 1
                return name

            def group_read():
                p = out_name()
                act.wait_ge(read_out[p], c.next(f"read_out{p}"))

            def group_skipped():
                c.one(f"read_out{out_name()}")

            def square(src, n=SEQ, at_register=False):
                act.wait_ge(sq_used, c.now("sq_used"))
                if at_register:
                    c.apart(act)
                act.activation(X[:, 0, 0:n], src, ACT.Square).then_inc(sq_ready, 1)
                c.one("sq_used")

            def operand(gain, l, squares=True):
                c.apart(act)
                for i in range(DC):
                    act.activation(a_hi[:, i, :], xT[:, i, :], ACT.Copy, scale=col(gain, l, i)).then_inc(ah_ready, 1)
                    if squares:
                        square(xT[:, i, :])

            def ffn(gain, l, post_norm):
                act.wait_ge(x_ready, c.next("x_ready"))
                operand(gain, l)

                def gate_and_up(i):
                    unit_done()
                    group_read()
                    act.activation(X[:, 0:2, :], X[:, 0:2, :], ACT.Silu).then_inc(silu_ready, 1)
                    unit_done()
                    group_skipped()
                    act.wait_ge(h_ready, c.next("h_ready"))
                    c.apart(act)
                    act.activation(h_hi[:, bass.ds(i * 2, 2), :], X[:, 2:4, :], ACT.Copy).then_inc(hh_ready, 1)

                gate_and_up(0)
                for i in c.turns(act, 1, FF // (2 * P), PER_TURN["ffn_in"], "ffn_in"):
                    gate_and_up(i)
                for i in c.turns(act, 0, 2, PER_TURN["ffn_out"], "ffn_out"):
                    for j in range(2):
                        for _ in range(3):
                            unit_done()
                        if post_norm:
                            copy_and_square(y_ffn, i * 4 + 2 * j)
                        else:
                            group_skipped()

            def copy_and_square(y, chunk):
                p = out_name()
                c.apart(act)
                act.activation(y[:, bass.ds(chunk, 2), :], G[p][:], ACT.Copy).then_inc(read_out[p], c.one(f"read_out{p}"))
                act.wait_ge(read_out[p], c.now(f"read_out{p}"))
                for b in range(2):
                    square(y[:, bass.ds(chunk + b, 1), :].rearrange("p o n -> p (o n)"), at_register=True)

            def attention(steps, l, leave):
                n = len(steps)
                for s in range(n + 2):
                    if s < n:
                        st = steps[s]
                        tile = X[:, s % 2, 0:st["n"]]
                        act.wait_ge(m_ready, c.next("m_ready"))
                        e = act.activation(tile, tile, ACT.Exp, bias=stats[:, 3, s:s + 1], scale=st["scale"],
                                           accum_out=stats[:, 1, s:s + 1])
                        if st["sink"] is not None:
                            e = act.activation(stats[:, 2, s:s + 1], sinks[:, bass.ds(l * WINDOW_HEADS + st["sink"], 1)],
                                               ACT.Exp, bias=stats[:, 3, s:s + 1])
                        e.then_inc(e_ready, 1)
                    if 1 <= s <= n:
                        st = steps[s - 1]
                        act.wait_ge(t_ready, c.next("t_ready"))
                        act.activation(X[:, 2 + (s - 1) % 2, 0:st["n"]], B6[:, 0:st["n"]], ACT.Copy).then_inc(pt_ready, 1)
                    if s >= 2 and steps[s - 2]["closes"]:
                        act.wait_ge(o_ready, c.next("o_ready"))
                        leave()

            act.dma_start(ident[:], t["consts"][:, CONSTS["ident"][0]:CONSTS["ident"][0] + P]).then_inc(consts_loaded, 16)
            for name, tile in (("rot96", rot96), ("causal", causal), ("freq", freq)):
                at, n = CONSTS[name]
                act.dma_start(tile[:], t["consts"][:, at:at + n]).then_inc(consts_loaded, 16)
            act.dma_start(sinks[:], t["sink"].rearrange("l h -> (l h)").partition_broadcast(P)).then_inc(consts_loaded, 16)
            act.dma_start(X[:, 0, :].bitcast(I32), t["positions"][0].partition_broadcast(P)).then_inc(pos_loaded, 16)
            act.wait_ge(rows_zeroed, 1)
            for dst, src in row_loads:
                act.dma_start(dst, src).then_inc(rows_loaded, 16)
            split_hi()
            split_hi()

            def sines(rope_block):
                act.wait_ge(angle, c.next("angle"))
                act.activation(sinT[:], X[:, 3, :], ACT.Sin).then_inc(sin_done, 1)
                act.wait_ge(angle, c.next("angle"))
                act.activation(cosT[:], X[:, 3, :], ACT.Sin).then_inc(sin_done, 1)

            sines(0)
            act.wait_ge(soft_in, 1)
            act.activation(tiny[:, 2, :], tiny[:, 1, :], ACT.Exp).then_inc(soft_exp, 1)

            for l in c.layers(act, PER_LAYER["one"], "one"):
                act.wait_ge(x_ready, c.next("x_ready"))
                operand("g_pre_mix", l)
                unit_done()
                group_skipped()
                for i in range(DC // 2):
                    act.wait_ge(swap_ready, c.next("swap_ready"))
                    act.activation(memT[:, 2 * i:2 * i + 2, :], B6[:], ACT.Copy).then_inc(swap_copied, 1)
                act.wait_ge(swap_copied, c.next("swap_copied", DC // 2))
                c.apart(act)
                for i in range(DC):
                    act.activation(m_hi[:, i, :], memT[:, i, :], ACT.Copy, scale=col("g_mem", l, i)).then_inc(ah_ready, 1)
                    square(memT[:, i, :], MEM)
                for _ in range(7):
                    unit_done()
                    group_skipped()
                act.wait_ge(swap_ready, c.next("swap_ready"))
                act.activation(v_tok[:], B6[:], ACT.Copy).then_inc(swap_copied, 1)
                act.wait_ge(swap_ready, c.next("swap_ready"))
                act.activation(vm_tok[:], B7[:], ACT.Copy).then_inc(swap_copied, 1)
                c.one("swap_copied", 2)
                act.wait_ge(four_ready, c.next("four_ready"))
                act.activation(mf[:], B4[:], ACT.Copy).then_inc(four_copied, 1)
                for tc in range(TC):
                    act.wait_ge(four_ready, c.next("four_ready"))
                    act.activation(ab[:, tc, :], (B5, B4)[tc % 2][:], ACT.Copy).then_inc(four_copied, 1)
                for j in range(2):
                    act.wait_ge(four_ready, c.next("four_ready"))
                    act.activation(y_mix[:, j, :], (B4, B5)[j][:], ACT.Copy).then_inc(four_copied, 1)
                c.one("four_copied", 3 + TC)
                chunk = iter(range(2, DC))

                def leave():
                    act.activation(y_mix[:, next(chunk), :], B7[:], ACT.Copy).then_inc(o_used, c.one("o_used"))

                attention(window_steps(qT, kT, v_tok), l, leave)
                attention(memory_steps(zmT, kmT, vm_tok), l, leave)
                act.wait_ge(o_used, c.now("o_used"))
                act.wait_ge(four_copied, c.now("four_copied"))
                for chunks in GROUPS:
                    for i in chunks:
                        square(y_mix[:, i, :])
                    for i in chunks:
                        act.wait_ge(src_ready, c.next("src_ready"))
                        act.activation(a_hi[:, i, :], X[:, 2 + i % 2, :], ACT.Copy).then_inc(ah_ready, 1)
                for j in range(4):
                    unit_done()
                    copy_and_square(y_mix, 2 * j)
                ffn("g_pre_ffn", l, True)

            act.wait_ge(x_ready, c.next("x_ready"))
            act.dma_start(X[:, 0, :].bitcast(I32), t["positions_2"][0].partition_broadcast(P)).then_inc(pos_loaded, 16)
            sines(1)
            for l in c.layers(act, PER_LAYER["two"], "two"):
                ffn("ffn1_norm", l, False)
                act.wait_ge(x_ready, c.next("x_ready"))
                operand("mix_norm", l)
                for j in range(LC):
                    unit_done()
                    group_read()
                    c.apart(act)
                    act.activation(X[:, 3, :], X[:, 3, :], ACT.Sigmoid, bias=col("b_c", l, LC + j)).then_inc(bias_done, 1)
                for j in range(4):
                    unit_done()
                    group_read()
                    c.apart(act)
                    for b in range(2):
                        i = 2 * j + b
                        dst = xpad[:, i, LRU_TAPS - 1:] if j < 2 else gelu[:, i - LC, :]
                        act.activation(dst, X[:, 2 + b, :], ACT.Identity if j < 2 else ACT.Gelu_apprx_tanh,
                                       bias=col("b_a", l, i)).then_inc(bias_done, 1)
                for j in range(4):
                    if j != 2:
                        unit_done()
                    else:
                        act.wait_ge(piece_done, c.next("piece_done"))
                    group_read()
                    c.apart(act)
                    if j < 2:
                        for b in range(2):
                            act.activation(craw[:, 2 * j + b, :], X[:, 2 + b, :], ACT.Identity,
                                           bias=col("b_b", l, 2 * j + b)).then_inc(bias_done, 1)
                    elif j == 2:
                        act.activation(craw[:, 4, :], X[:, 2, :], ACT.Identity, bias=col("b_b", l, 4)).then_inc(bias_done, 1)
                    else:
                        act.activation(craw[0:QK, 5, :], X[0:QK, 2, :], ACT.Identity,
                                       bias=col("b_kpe", l, 0, QK)).then_inc(bias_done, 1)
                c.one("bias_done", LC + 8 + 6)
                act.wait_ge(bias_done, c.now("bias_done"))
                act.wait_ge(xa_ready, c.next("xa_ready", LC))
                for i in range(LC):
                    for j, name in enumerate(("b_r", "b_i")):
                        act.wait_ge(gates_ready, c.next("gates_ready"))
                        c.apart(act)
                        act.activation(sig[:, i, j, :], (B4, B5)[j][:], ACT.Sigmoid, bias=col(name, l, i)).then_inc(sig_ready, 1)
                c.one("sig_ready", 2 * LC)
                act.wait_ge(sig_ready, c.now("sig_ready"))
                for i in range(LC):
                    if i:
                        act.wait_ge(root_asked, c.next("root_asked"))
                    c.apart(act)
                    once, twice = (decay[:, j, bass.ds(l * LC + i, 1)] for j in range(2))
                    act.activation(X[:, 1, :], sig[:, i, 0, :], ACT.Tanh, scale=once)
                    act.activation(X[:, 2, :], sig[:, i, 0, :], ACT.Exp, scale=twice)
                    act.activation(sig[:, i, 0, :], sig[:, i, 0, :], ACT.Exp, scale=once).then_inc(e2_ready, 1)
                act.wait_ge(root_asked, c.next("root_asked"))
                for i in range(LC):
                    act.activation(sig[:, i, 1, :], sig[:, i, 1, :], ACT.Sqrt, scale=-1.0).then_inc(root_done, 1)
                act.wait_ge(v_ready, c.next("v_ready", LC))
                for i in range(LC):
                    act.activation(ya_hi[:, i, :], gelu[:, i, :], ACT.Copy).then_inc(ah_ready, 1)
                act.wait_ge(centred, c.next("centred"))
                for i in range(LC):
                    square(conv[:, i, :])
                act.wait_ge(ln_ready, c.next("ln_ready"))
                c.apart(act)
                for i in range(LC):
                    act.activation(conv[:, i, :], conv[:, i, :], ACT.Silu, bias=col("ln_b", l, i),
                                   scale=col("ln_g", l, i)).then_inc(act_step, c.one("act_step"))
                    act.wait_ge(act_step, c.now("act_step"))
                    act.activation(yc_hi[:, i, :], conv[:, i, :], ACT.Copy).then_inc(ah_ready, 1)
                for first, end in ((0, 3), (3, 5)):
                    for i in range(first, end):
                        square(craw[:, i, :])
                    for i in range(first, end):
                        act.wait_ge(src_ready, c.next("src_ready"))
                        act.activation(a_hi[:, i, :], X[:, 2 + i % 2, :], ACT.Copy).then_inc(ah_ready, 1)
                for m, tile, first, end in ((QK, q_head, 0, 4), (QK, q_head, 4, 8), (P, kv_head, 0, 8)):
                    for h in range(first, end, 2):
                        act.wait_ge(piece_done, c.next("piece_done"))
                        p = out_name()
                        act.activation(tile[0:m, h:h + 2, :], G[p][0:m], ACT.Copy).then_inc(read_out[p], c.one(f"read_out{p}"))
                    split_hi()
                operand("mix_norm", l, squares=False)
                for h in range(MLA_HEADS):
                    act.wait_ge(swap_ready, c.next("swap_ready"))
                    act.activation(v_head[:, :, h * HEAD:(h + 1) * HEAD],
                                   B6[:].rearrange("p (t e) -> p t e", t=TC)[:, :, HEAD:P], ACT.Copy).then_inc(swap_copied, 1)
                pair = iter(range(LC))

                def leave():
                    act.activation(yb_hi[:, next(pair), :], B7[:], ACT.Copy).then_inc(ah_ready, 1)

                attention(mla_steps(q_head, kv_head, v_head), l, leave)
                for i in c.turns(act, 0, DC // 2, PER_TURN["merge"], "merge"):
                    for j in range(2):
                        chunk = i * 2 + j
                        unit_done()
                        group_read()
                        c.apart(act)
                        for b in range(2):
                            g = act.activation(X[:, b, :], X[:, b, :], ACT.Sigmoid, bias=col("b_g", l, chunk + DC * b))
                        g.then_inc(gate_ready, c.one("gate_ready"))
                        unit_done()
                        group_skipped()
                        act.wait_ge(src_ready, c.next("src_ready"))
                        c.apart(act)
                        act.activation(X[:, 2, :], X[:, 2, :], ACT.Sigmoid,
                                       bias=col("b_g", l, chunk + DC * 2)).then_inc(gate_ready, c.one("gate_ready"))
                        unit_done()
                        group_skipped()
                        act.wait_ge(merged_ready, c.next("merged_ready"))
                        c.apart(act)
                        act.activation(mg_hi[:, bass.ds(chunk, 1), :].rearrange("p o n -> p (o n)"), X[:, 0, :],
                                       ACT.Copy).then_inc(ah_ready, 1)
                for _ in c.turns(act, 0, 2, PER_TURN["w_out"], "w_out"):
                    for j in range(2):
                        unit_done()
                        group_skipped()
                ffn("ffn2_norm", l, False)
            act.wait_ge(x_ready, c.next("x_ready"))
            for i in range(DC):
                square(xT[:, i, :])
            for tc in range(TC):
                act.wait_ge(turned, n_param_tiles + DC + 1 + tc)
                act.activation(out_tok[:, tc, 0:SEQ], B4[:], ACT.Copy)
                act.activation(out_tok[:, tc, SEQ:D], B5[:], ACT.Copy).then_inc(tok_copied, 1)

        @block.vector
        def _(dve):
            c = Tally("vector")

            def settled():
                dve.wait_ge(dve_step, c.now("dve_step"))

            def stepped(ins):
                ins.then_inc(dve_step, c.one("dve_step"))

            def split_lo():
                s = c.split % 2
                c.split += 1
                dve.wait_ge(hi_ready, c.next("hi_ready"))
                dve.tensor_tensor(w_lo[:, s, :], raw[:, s, :], w_hi[:, s, :].bitcast(F32), ALU.subtract).then_inc(lo_ready, 1)

            def piece():
                dve.wait_ge(piece_done, c.next("piece_done"))

            def group():
                p = c.group % 2
                c.group += 1
                return p

            def taken(ins, p):
                ins.then_inc(read_out[p], c.one(f"read_out{p}"))

            def scaled(dst, p, r, n=SEQ, blocks=2):
                taken(dve.tensor_tensor(dst, G[p][:, 0:blocks, 0:n], wide(r[:, 0:n], blocks), ALU.mult), p)

            def begin_sum(signal=None):
                zero = dve.memset(X[:, 1, :], 0.0)
                if signal is None:
                    stepped(zero)
                    settled()
                else:
                    zero.then_inc(signal, 1)

            def add_square(n=SEQ):
                dve.wait_ge(sq_ready, c.next("sq_ready"))
                dve.tensor_tensor(X[:, 1, 0:n], X[:, 1, 0:n], X[:, 0, 0:n], ALU.add).then_inc(sq_used, c.one("sq_used"))

            def inverse_rms(dst, d, n=SEQ):
                dve.wait_ge(sum_ready, c.next("sum_ready"))
                tiles = n // P
                dve.tensor_scalar(mean_sq[:, 0:tiles], B7[:, 0:tiles], 1.0 / d, EPS, ALU.mult, ALU.add).then_inc(pow_asked, 1)
                dve.wait_ge(pow_done, c.next("pow_done"))
                for i in range(tiles):
                    last = dve.tensor_scalar(X[:, 1, i * P:(i + 1) * P], ident[:], mean_sq[:, i:i + 1], None, ALU.mult)
                last.then_inc(diag_ready, 1)
                dve.wait_ge(sum_ready, c.next("sum_ready"))
                stepped(dve.tensor_copy(dst[:, 0:n], B7[:, 0:n]))
                settled()

            def operand(src, gain, l, squares=True):
                for i in range(DC):
                    dve.wait_ge(ah_ready, c.next("ah_ready"))
                    dve.scalar_tensor_tensor(a_lo[:, i, :], src[:, i, :], col(gain, l, i), a_hi[:, i, :].bitcast(F32),
                                             ALU.mult, ALU.subtract).then_inc(al_ready, c.one("al_ready"))
                    if squares:
                        add_square()

            def low_of(dst, full, hi, signal):
                dve.wait_ge(ah_ready, c.next("ah_ready"))
                dve.tensor_tensor(dst, full, hi.bitcast(F32), ALU.subtract).then_inc(sems[signal], 1)

            def normalised(src, chunks, gain, first, l):
                def low(i):
                    low_of(a_lo[:, i, :], X[:, 2 + i % 2, :], a_hi[:, i, :], "al_ready")
                    c.one("al_ready")
                for i in chunks:
                    dve.wait_ge(al_ready, c.now("al_ready"))
                    dve.scalar_tensor_tensor(X[:, 2 + i % 2, :], src[:, i, :], col(gain, l, i - first), rs_b[:],
                                             ALU.mult, ALU.mult).then_inc(src_ready, c.one("src_ready"))
                    if i != chunks[0]:
                        low(i - 1)
                low(chunks[-1])

            def post_norm(y, gain, l):
                inverse_rms(rs_b, D)
                for i in range(0, DC, 2):
                    if i:
                        settled()
                    for b in range(2):
                        stepped(dve.scalar_tensor_tensor(X[:, 2 + b, :], y[:, i + b, :], col(gain, l, i + b), rs_b[:],
                                                         ALU.mult, ALU.mult))
                    settled()
                    stepped(dve.tensor_tensor(xT[:, i:i + 2, :], xT[:, i:i + 2, :], X[:, 2:4, :], ALU.add))
                settled()

            def ffn(gain, l, post, scale):
                begin_sum(x_ready)
                operand(xT, gain, l)
                inverse_rms(rs, D)

                def gate_and_up(i, peeled=False):
                    piece()
                    scaled(X[:, 0:2, :], group(), rs)
                    split_lo()
                    piece()
                    p = group()
                    if not peeled:
                        dve.wait_ge(hl_ready, c.now("hl_ready"))
                    scaled(X[:, 2:4, :], p, rs)
                    dve.wait_ge(silu_ready, c.next("silu_ready"))
                    dve.wait_ge(read_out[p], c.now(f"read_out{p}"))
                    dve.tensor_tensor(X[:, 2:4, :], X[:, 2:4, :], X[:, 0:2, :], ALU.mult).then_inc(h_ready, 1)
                    split_lo()
                    dve.wait_ge(hh_ready, c.next("hh_ready"))
                    dve.tensor_tensor(h_lo[:, bass.ds(i * 2, 2), :], X[:, 2:4, :],
                                      h_hi[:, bass.ds(i * 2, 2), :].bitcast(F32), ALU.subtract).then_inc(hl_ready, c.one("hl_ready"))

                gate_and_up(0, peeled=True)
                for i in c.turns(dve, 1, FF // (2 * P), PER_TURN["ffn_in"], "ffn_in"):
                    gate_and_up(i)
                if post:
                    begin_sum()
                for i in c.turns(dve, 0, 2, PER_TURN["ffn_out"], "ffn_out"):
                    for j in range(2):
                        for _ in range(3):
                            piece()
                            split_lo()
                        p = group()
                        if post:
                            c.one(f"read_out{p}")
                            for _ in range(2):
                                add_square()
                        else:
                            x2 = xT[:, bass.ds(i * 4 + 2 * j, 2), :]
                            taken(dve.scalar_tensor_tensor(x2, G[p][:], scale, x2, ALU.mult, ALU.add), p)
                if post:
                    post_norm(y_ffn, post, l)
                else:
                    for p in range(2):
                        dve.wait_ge(read_out[p], c.now(f"read_out{p}"))

            def attention(steps, l, leave=None):
                n = len(steps)
                for s in range(n + 2):
                    if s < n:
                        st = steps[s]
                        tile, m = X[:, s % 2, 0:st["n"]], stats[:, 0, s:s + 1]
                        if s >= 2:
                            dve.wait_ge(t_ready, c.next("t_ready"))
                        dve.wait_ge(s_ready, c.next("s_ready"))
                        c.apart(dve)
                        stepped(dve.tensor_tensor_reduce(tile, (B4, B5)[s % 2][:, 0:st["n"]], st["mask"], 1.0, -3.0e38,
                                                         ALU.add, ALU.max, m))
                        settled()
                        if st["sink"] is None:
                            dve.tensor_scalar(stats[:, 3, s:s + 1], m, -st["scale"], None, ALU.mult).then_inc(m_ready, 1)
                        else:
                            stepped(dve.tensor_scalar(m, m, st["scale"], sinks[:, bass.ds(l * WINDOW_HEADS + st["sink"], 1)],
                                                      ALU.mult, ALU.max))
                            settled()
                            dve.tensor_scalar(stats[:, 3, s:s + 1], m, -1.0, None, ALU.mult).then_inc(m_ready, 1)
                    if 1 <= s <= n:
                        st = steps[s - 1]
                        total = stats[:, 1, s - 1:s]
                        dve.wait_ge(e_ready, c.next("e_ready"))
                        if st["sink"] is not None:
                            stepped(dve.tensor_tensor(total, total, stats[:, 2, s - 1:s], ALU.add))
                            settled()
                        stepped(dve.reciprocal(stats[:, 0, s - 1:s], total))
                        settled()
                        tile = X[:, (s - 1) % 2, 0:st["n"]]
                        dve.tensor_scalar(tile, tile, stats[:, 0, s - 1:s], None, ALU.mult).then_inc(p_ready, 1)
                    if s >= 2 and steps[s - 2]["closes"] and leave:
                        leave()
                c.one("t_ready", 2)
                dve.wait_ge(t_ready, c.now("t_ready"))
                dve.wait_ge(p_ready, c.next("p_ready", n))

            def rope_tables(column):
                two_pi = 2 * np.pi
                c1_, rest = 6.28125, two_pi - 6.28125
                c2_ = float(np.round(rest * 2 ** 19) / 2 ** 19)
                c3_ = float(np.round((rest - c2_) * 2 ** 30) / 2 ** 30)
                c4_ = float(rest - c2_ - c3_)
                dve.wait_ge(pos_loaded, c.next("pos_loaded", 16))
                stepped(dve.tensor_copy(X[:, 1, :], X[:, 0, :].bitcast(I32)))
                settled()
                stepped(dve.tensor_scalar(X[:, 1, :], X[:, 1, :], freq[:, column:column + 1], None, ALU.mult))
                settled()
                for quarter in (0.0, 0.25):
                    stepped(dve.tensor_scalar(X[:, 2, :], X[:, 1, :], 1.0 / two_pi, quarter, ALU.mult, ALU.add))
                    settled()
                    stepped(dve.tensor_scalar(X[:, 2, :], X[:, 2, :], 1.5 * 2.0 ** 23, None, ALU.add))
                    settled()
                    stepped(dve.tensor_scalar(X[:, 2, :], X[:, 2, :], -1.5 * 2.0 ** 23, None, ALU.add))
                    settled()
                    src = X[:, 1, :]
                    for part in (c1_, c2_, c3_, c4_):
                        stepped(dve.scalar_tensor_tensor(X[:, 3, :], X[:, 2, :], -part, src, ALU.mult, ALU.add))
                        settled()
                        src = X[:, 3, :]
                    if quarter:
                        stepped(dve.tensor_scalar(X[:, 3, :], X[:, 3, :], float(np.pi / 2), None, ALU.add))
                        settled()
                    dve.tensor_scalar(X[:, 3, :], X[:, 3, :], 3.1415925, -3.1415925, ALU.min, ALU.max).then_inc(angle, 1)
                    dve.wait_ge(sin_done, c.next("sin_done"))

            dve.wait_ge(pool_step, 2)
            dve.memset(rows[:], 0.0).then_inc(rows_zeroed, 1)
            dve.memset(ones[:], 1.0).then_inc(sq_used, c.one("sq_used"))
            dve.memset(tiny[:, 0, :], 0.0).then_inc(read_out[0], c.one("read_out0"))
            dve.memset(tiny[:, 4, :], 0.0).then_inc(read_out[1], c.one("read_out1"))
            for s in range(2):
                dve.memset(raw[:, s, :], 0.0).then_inc(lo_ready, 1)
            for i in range(n_param_tiles):
                dve.wait_ge(turned, i + 1)
                dve.tensor_copy(params[:, i * P:(i + 1) * P], (B4, B5)[i % 2][:, 0:P]).then_inc(turn_copied, 1)
            for i in range(DC):
                dve.wait_ge(turned, n_param_tiles + i + 1)
                dve.tensor_copy(xT[:, i, :], (B4, B5)[(n_param_tiles + i) % 2][:]).then_inc(turn_copied, 1)
            dve.wait_ge(turn_copied, n_param_tiles + DC)
            dve.wait_ge(consts_loaded, c.next("consts_loaded", 16 * n_setup_loads))
            split_lo()
            split_lo()
            rope_tables(0)
            lam_at = columns["lambda"][0]
            lam = params[:, lam_at:lam_at + DEPTH * LC]
            v = [tiny[:, i, :] for i in range(6)]
            stepped(dve.tensor_scalar(v[0], lam, -1.0, None, ALU.mult))
            settled()
            dve.tensor_tensor(v[1], v[0], lam, ALU.min).then_inc(soft_in, 1)
            dve.wait_ge(soft_exp, 1)
            stepped(dve.tensor_scalar(v[3], v[2], 2.0, None, ALU.add))
            settled()
            stepped(dve.reciprocal(v[4], v[3]))
            settled()
            stepped(dve.tensor_tensor(v[2], v[2], v[4], ALU.mult))
            settled()
            stepped(dve.tensor_tensor(v[3], v[2], v[2], ALU.mult))
            settled()
            stepped(dve.tensor_scalar(v[4], v[3], 1.0 / 15, 1.0 / 13, ALU.mult, ALU.add))
            settled()
            for odd in (11, 9, 7, 5, 3, 1):
                stepped(dve.tensor_tensor(v[4], v[4], v[3], ALU.mult))
                settled()
                stepped(dve.tensor_scalar(v[4], v[4], 1.0 / odd, None, ALU.add))
                settled()
            stepped(dve.tensor_tensor(v[4], v[4], v[2], ALU.mult))
            stepped(dve.tensor_scalar(v[5], v[0], 0.0, None, ALU.max))
            settled()
            stepped(dve.scalar_tensor_tensor(v[3], v[4], 2.0, v[5], ALU.mult, ALU.add))
            settled()
            stepped(dve.tensor_scalar(decay[:, 0, :], v[3], -8.0, None, ALU.mult))
            stepped(dve.tensor_scalar(decay[:, 1, :], v[3], -16.0, None, ALU.mult))
            settled()

            for l in c.layers(dve, PER_LAYER["one"], "one"):
                begin_sum(x_ready)
                operand(xT, "g_pre_mix", l)
                inverse_rms(rs, D)
                piece()
                scaled(zfT[:], group(), rs)
                split_lo()
                begin_sum()
                for i in range(DC):
                    dve.wait_ge(ah_ready, c.next("ah_ready"))
                    dve.scalar_tensor_tensor(m_lo[:, i, :], memT[:, i, :], col("g_mem", l, i), m_hi[:, i, :].bitcast(F32),
                                             ALU.mult, ALU.subtract).then_inc(al_ready, c.one("al_ready"))
                    add_square(MEM)
                for dst, blocks in ((qT[:, 0:2, :], 2), (qT[:, 2:4, :], 2), (zkT[:].unsqueeze(1), 1),
                                    (vT[:].unsqueeze(1), 1), (zmT[:], 2)):
                    piece()
                    scaled(dst, group(), rs, blocks=blocks)
                    split_lo()
                inverse_rms(rs_b, D, MEM)
                for dst in (kmT, vmT):
                    piece()
                    scaled(dst[:], group(), rs_b, n=MEM)
                    split_lo()
                for p in range(2):
                    dve.wait_ge(read_out[p], c.now(f"read_out{p}"))
                for i in range(4):
                    if i:
                        dve.wait_ge(rope_ready, c.now("rope_ready"))
                    dve.wait_ge(rot_ready, c.next("rot_ready"))
                    dve.tensor_tensor(X[:, 2, :], (B4, B5)[i % 2][:], sinT[:], ALU.mult).then_inc(rot_used, c.one("rot_used"))
                    stepped(dve.tensor_tensor(qT[:, i, :], qT[:, i, :], cosT[:], ALU.mult))
                    dve.wait_ge(rot_used, c.now("rot_used"))
                    settled()
                    dve.tensor_tensor(qT[:, i, :], qT[:, i, :], X[:, 2, :], ALU.add).then_inc(rope_ready, c.one("rope_ready"))
                for j in range(2):
                    dve.wait_ge(rope_ready, c.now("rope_ready"))
                    dve.wait_ge(rot_ready, c.next("rot_ready", 2))
                    dve.tensor_tensor(kT[:, j, :], B4[:], cosT[:], ALU.mult).then_inc(rot_used, c.one("rot_used"))
                    dve.tensor_tensor(X[:, 2, :], B5[:], sinT[:], ALU.mult).then_inc(rot_used, c.one("rot_used"))
                    dve.wait_ge(rot_used, c.now("rot_used"))
                    dve.tensor_tensor(kT[:, j, :], kT[:, j, :], X[:, 2, :], ALU.add).then_inc(rope_ready, c.one("rope_ready"))
                attention(window_steps(qT, kT, v_tok), l)
                attention(memory_steps(zmT, kmT, vm_tok), l)
                for chunks in GROUPS:
                    begin_sum()
                    for _ in chunks:
                        add_square()
                    inverse_rms(rs_b, P * len(chunks))
                    normalised(y_mix, chunks, "g_grp", 0, l)
                begin_sum()
                for j in range(4):
                    piece()
                    p = group()
                    c.one(f"read_out{p}")
                    split_lo()
                    for _ in range(2):
                        add_square()
                post_norm(y_mix, "g_post_mix", l)
                ffn("g_pre_ffn", l, "g_post_ffn", None)

            begin_sum(x_ready)
            rope_tables(1)
            for l in c.layers(dve, PER_LAYER["two"], "two"):
                ffn("ffn1_norm", l, None, 0.5)
                stepped(dve.memset(glu[:, :, 0:CONV_TAPS - 1], 0.0))
                dve.memset(xpad[:, :, 0:LRU_TAPS - 1], 0.0).then_inc(region_free, 1)
                begin_sum(x_ready)
                operand(xT, "mix_norm", l)
                inverse_rms(rs, D)
                settled()

                def conv_taps(first, end):
                    at, per = columns["dw_w"]
                    for n in range(first, end):
                        i, k = n // CONV_TAPS, n % CONV_TAPS
                        w = params[:, bass.ds(l * per + (at + k * LC + i), 1)]
                        src = glu[:, i, k:k + SEQ]
                        if k == 0:
                            stepped(dve.tensor_scalar(conv[:, i, :], src, w, col("dw_b", l, i), ALU.mult, ALU.add))
                        else:
                            settled()
                            tap = dve.scalar_tensor_tensor(conv[:, i, :], src, w, conv[:, i, :], ALU.mult, ALU.add)
                            if n < LC * CONV_TAPS - 1:
                                stepped(tap)
                            else:
                                tap.then_inc(conv_done, 1)

                def short_conv(i):
                    at, per = columns["conv4_w"]
                    for k in range(LRU_TAPS):
                        w = params[:, bass.ds(l * per + (at + k * LC + i), 1)]
                        src = xpad[:, i, k:k + SEQ]
                        if k == 0:
                            stepped(dve.tensor_scalar(xa[:, i, :], src, w, col("conv4_b", l, i), ALU.mult, ALU.add))
                        else:
                            settled()
                            tap = dve.scalar_tensor_tensor(xa[:, i, :], src, w, xa[:, i, :], ALU.mult, ALU.add)
                            if k < LRU_TAPS - 1:
                                stepped(tap)
                            else:
                                tap.then_inc(xa_ready, c.one("xa_ready"))

                taps = 0
                for j in range(LC):
                    piece()
                    scaled(X[:, 2:4, :], group(), rs)
                    split_lo()
                    if j:
                        conv_taps(taps, taps + 11)
                        taps += 11
                    dve.wait_ge(bias_done, c.next("bias_done"))
                    stepped(dve.scalar_tensor_tensor(glu[:, j, CONV_TAPS - 1:], X[:, 2, :], col("b_c", l, j), X[:, 3, :],
                                                     ALU.add, ALU.mult))
                    settled()
                for j in range(4):
                    piece()
                    scaled(X[:, 2:4, :], group(), rs)
                    split_lo()
                    conv_taps(taps, taps + 12)
                    taps += 12
                    dve.wait_ge(bias_done, c.next("bias_done", 2))
                    if j < 2:
                        short_conv(2 * j)
                        short_conv(2 * j + 1)
                for j in range(4):
                    piece()
                    p = group()
                    if j < 2:
                        scaled(X[:, 2:4, :], p, rs)
                    elif j == 2:
                        scaled(X[:, 2:3, :], p, rs, blocks=1)
                    else:
                        taken(dve.tensor_tensor(X[0:QK, 2, :], G[p][0:QK, 0, :], rs[0:QK, :], ALU.mult), p)
                    if j != 2:
                        split_lo()
                    conv_taps(taps, taps + 8)
                    taps += 8
                    dve.wait_ge(bias_done, c.next("bias_done", 2 if j < 2 else 1))
                conv_taps(taps, LC * CONV_TAPS)
                settled()
                for i in range(LC):
                    dve.wait_ge(e2_ready, c.next("e2_ready"))
                    stepped(dve.scalar_tensor_tensor(X[:, 2, :], X[:, 2, :], 1.0, X[:, 1, :], ALU.add, ALU.mult))
                    stepped(dve.tensor_tensor(xa[:, i, :], sig[:, i, 1, :], xa[:, i, :], ALU.mult))
                    settled()
                    dve.tensor_copy(sig[:, i, 1, :], X[:, 2, :]).then_inc(root_asked, 1)
                for i in range(LC):
                    dve.wait_ge(root_done, c.next("root_done"))
                    stepped(dve.tensor_tensor(xa[:, i, :], xa[:, i, :], sig[:, i, 1, :], ALU.mult))
                    settled()
                    stepped(dve.tensor_tensor_scan(X[:, 3, :], sig[:, i, 0, :], xa[:, i, :], 0.0, ALU.mult, ALU.add))
                    settled()
                    dve.tensor_tensor(gelu[:, i, :], gelu[:, i, :], X[:, 3, :], ALU.mult).then_inc(v_ready, c.one("v_ready"))
                dve.wait_ge(v_ready, c.now("v_ready"))
                for i in range(LC):
                    low_of(ya_lo[:, i, :], gelu[:, i, :], ya_hi[:, i, :], "branch_ready")
                dve.wait_ge(mean_ready, c.next("mean_ready"))
                stepped(dve.tensor_scalar(X[:, 3, :], B7[:], 1.0 / LRU, None, ALU.mult))
                begin_sum()
                dve.tensor_tensor(conv[:], conv[:], wide(X[:, 3, :], LC), ALU.subtract).then_inc(centred, c.one("centred"))
                dve.wait_ge(centred, c.now("centred"))
                for _ in range(LC):
                    add_square()
                inverse_rms(rs_b, LRU)
                dve.tensor_tensor(conv[:], conv[:], wide(rs_b[:], LC), ALU.mult).then_inc(ln_ready, c.one("ln_ready"))
                for i in range(LC):
                    low_of(yc_lo[:, i, :], conv[:, i, :], yc_hi[:, i, :], "branch_ready")
                for first, end, gain in ((0, 3, "q_norm"), (3, 5, "kv_norm")):
                    begin_sum()
                    for _ in range(first, end):
                        add_square()
                    inverse_rms(rs_b, P * (end - first))
                    normalised(craw, tuple(range(first, end)), gain, first, l)
                for pieces in (2, 2, 4):
                    for _ in range(pieces):
                        piece()
                        c.one(f"read_out{group()}")
                    split_lo()
                operand(xT, "mix_norm", l, squares=False)
                turn = slice(HEAD, QK)
                dve.wait_ge(rot_ready, c.next("rot_ready"))
                stepped(dve.tensor_tensor(X[turn, 2, :], B4[turn, :], sinT[turn, :], ALU.mult))
                stepped(dve.tensor_tensor(craw[turn, 5, :], craw[turn, 5, :], cosT[turn, :], ALU.mult))
                settled()
                dve.tensor_tensor(craw[turn, 5, :], craw[turn, 5, :], X[turn, 2, :], ALU.add).then_inc(rot_used, c.one("rot_used"))
                dve.wait_ge(rot_used, c.now("rot_used"))
                for h in range(MLA_HEADS):
                    if h:
                        dve.wait_ge(rope_ready, c.now("rope_ready"))
                    dve.wait_ge(rot_ready, c.next("rot_ready"))
                    dve.tensor_tensor(X[turn, 2, :], (B5, B4)[h % 2][turn, :], sinT[turn, :], ALU.mult).then_inc(rot_used, c.one("rot_used"))
                    stepped(dve.tensor_tensor(q_head[turn, h, :], q_head[turn, h, :], cosT[turn, :], ALU.mult))
                    dve.wait_ge(rot_used, c.now("rot_used"))
                    settled()
                    dve.tensor_tensor(q_head[turn, h, :], q_head[turn, h, :], X[turn, 2, :], ALU.add).then_inc(rope_ready, c.one("rope_ready"))
                dve.wait_ge(swap_copied, c.next("swap_copied", MLA_HEADS))
                for h in range(MLA_HEADS):
                    dve.tensor_copy(kv_head[turn, h, :], craw[turn, 5, :]).then_inc(rope_ready, c.one("rope_ready"))
                dve.wait_ge(rope_ready, c.now("rope_ready"))
                pair = iter(range(LC))

                def leave():
                    i = next(pair)
                    low_of(yb_lo[:, i, :], B7[:], yb_hi[:, i, :], "o_used")

                attention(mla_steps(q_head, kv_head, v_head), l, leave)
                for i in c.turns(dve, 0, DC // 2, PER_TURN["merge"], "merge"):
                    for j in range(2):
                        chunk = i * 2 + j
                        piece()
                        dve.wait_ge(hl_ready, c.now("hl_ready"))
                        scaled(X[:, 0:2, :], group(), rs)
                        split_lo()
                        piece()
                        p = group()
                        dve.tensor_tensor(X[:, 2, :], G[p][:, 0, :], rs[:], ALU.mult).then_inc(src_ready, c.one("src_ready"))
                        dve.wait_ge(gate_ready, c.next("gate_ready"))
                        taken(dve.tensor_tensor(X[:, 0, :], X[:, 0, :], G[p][:, 1, :], ALU.mult), p)
                        split_lo()
                        piece()
                        q = group()
                        stepped(dve.tensor_tensor(X[:, 1, :], X[:, 1, :], G[q][:, 0, :], ALU.mult))
                        dve.wait_ge(gate_ready, c.next("gate_ready"))
                        taken(dve.scalar_tensor_tensor(X[:, 2, :], G[q][:, 1, :], col("conv_b_out", l, chunk), X[:, 2, :],
                                                       ALU.add, ALU.mult), q)
                        settled()
                        stepped(dve.tensor_tensor(X[:, 0, :], X[:, 0, :], X[:, 1, :], ALU.add))
                        settled()
                        dve.wait_ge(read_out[q], c.now(f"read_out{q}"))
                        dve.tensor_tensor(X[:, 0, :], X[:, 0, :], X[:, 2, :], ALU.add).then_inc(merged_ready, c.one("merged_ready"))
                        split_lo()
                        low_of(mg_lo[:, bass.ds(chunk, 1), :].rearrange("p o n -> p (o n)"), X[:, 0, :],
                               mg_hi[:, bass.ds(chunk, 1), :].rearrange("p o n -> p (o n)"), "hl_ready")
                        c.one("hl_ready")
                for i in c.turns(dve, 0, 2, PER_TURN["w_out"], "w_out"):
                    for j in range(2):
                        piece()
                        p = group()
                        x2 = xT[:, bass.ds(i * 4 + 2 * j, 2), :]
                        taken(dve.tensor_tensor(x2, x2, G[p][:], ALU.add), p)
                        split_lo()
                for p in range(2):
                    dve.wait_ge(read_out[p], c.now(f"read_out{p}"))
                ffn("ffn2_norm", l, None, 0.5)
            begin_sum(x_ready)
            for _ in range(DC):
                add_square()
            inverse_rms(rs, D)
            first = columns["final_norm"][0]
            for i in range(DC):
                last = dve.scalar_tensor_tensor(xT[:, i, :], xT[:, i, :], params[:, first + i:first + i + 1], rs[:],
                                                ALU.mult, ALU.mult)
            last.then_inc(final_ready, 1)

        @block.gpsimd
        def _(pool):
            c = Tally("gpsimd")

            def inverse_roots(n):
                for _ in range(n):
                    pool.wait_ge(pow_asked, c.next("pow_asked"))
                    pool.tensor_tensor(mean_sq[:], mean_sq[:], minus_half[:], ALU.pow).then_inc(pow_done, 1)

            pool.memset(minus_half[:], -0.5).then_inc(pool_step, 1)
            pool.memset(mean_sq[:], 1.0).then_inc(pool_step, 1)
            pool.wait_ge(pool_step, 2)
            pool.wait_ge(x_loaded, 16)
            for l in c.layers(pool, PER_LAYER["one"], "one"):
                pool.wait_ge(x_ready, c.next("x_ready"))
                c.apart(pool)
                pool.dma_start(mem_tok[:], t["mem"].rearrange("o (t p) d -> p (o t) d", p=P)).then_inc(mem_loaded, 16)
                inverse_roots(1)
                for name, tile in c1.items():
                    at, n = CONSTS[name]
                    pool.dma_start(tile[:], t["consts"][:, at:at + n]).then_inc(c1_loaded, 16)
                pool.memset(wf[:], 0.0).then_inc(wf_zeroed, 1)
                pool.wait_ge(wf_zeroed, c.next("wf_zeroed"))
                c.apart(pool)
                for half in range(2):
                    pool.dma_start(wf[half * HEAD:(half + 1) * HEAD, :, half * HEAD:(half + 1) * HEAD],
                                   t["w_fourier"][bass.ds(l, 1), half::2].rearrange("o j c e -> c (o j) e")).then_inc(wf_loaded, 16)
                inverse_roots(1)
                pool.wait_ge(piece_done, c.next("piece_done", 6))
                c.apart(pool)
                pool.dma_start(dft[:], t["dft"].rearrange("(t p) i n -> p t i n", p=P)).then_inc(dft_loaded, 16)
                c.one("x_ready")
                c.one("piece_done", PER_LAYER["one"].get("piece_done", 6) - 6)
                inverse_roots(6)
            for l in c.layers(pool, PER_LAYER["two"], "two"):
                inverse_roots(1)
                pool.wait_ge(region_free, c.next("region_free"))
                c.apart(pool)
                pool.memset(gate_w[:], 0.0).then_inc(gate_zeroed, 1)
                pool.wait_ge(gate_zeroed, c.next("gate_zeroed"))
                c.apart(pool)
                for half in range(2):
                    for i in range(2):
                        pool.dma_start(
                            gate_w[half * HEAD:(half + 1) * HEAD, :, i, half * HEAD:(half + 1) * HEAD],
                            t["lru_w_gate_2"][bass.ds(l, 1), half::2, :, i * HEAD:(i + 1) * HEAD].rearrange("o j c e -> c (o j) e"),
                        ).then_inc(gate_loaded, 16)
                inverse_roots(5)
            inverse_roots(1)

    if Tally.wrong:
        raise ValueError(sorted({w[:3] for w in Tally.wrong}))


def row_copies(t, rows, columns):
    whole = {"g_pre_mix": "g_pre_mix", "g_mem": "g_mem", "g_grp": "g_grp", "g_post_mix": "g_post_mix",
             "g_pre_ffn": "g_pre_ffn", "g_post_ffn": "g_post_ffn", "ffn1_norm": "ffn1_norm_2",
             "mix_norm": "mix_norm_2", "conv4_b": "lru_conv_b_2", "lambda": "lru_lambda_2", "q_norm": "q_norm_2",
             "kv_norm": "kv_norm_2", "dw_b": "conv_dw_b_2", "ln_g": "conv_ln_g_2", "ln_b": "conv_ln_b_2",
             "conv_b_out": "conv_b_out_2", "ffn2_norm": "ffn2_norm_2"}
    biases = {"b_a": 0, "b_b": IN_B, "b_c": IN_C, "b_g": IN_G}
    counts = dict(PARAM_ROWS, dw_w=CONV_TAPS * LC)
    out = []
    for name, n in counts.items():
        first, step = columns[name]
        for l in range(DEPTH):
            at = first + l * step
            dst = rows[at % P:at % P + n, at // P, :]
            if name in whole:
                src = t[whole[name]][l].rearrange("(c p) -> c p", p=P)
            elif name in biases:
                src = t["b_in_2"][l, biases[name]:biases[name] + n * P].rearrange("(c p) -> c p", p=P)
            elif name == "b_kpe":
                dst = dst[:, 0:QK]
                src = t["b_in_2"][l:l + 1, IN_C - QK:IN_C]
            elif name in ("b_r", "b_i"):
                half = HEAD * (name == "b_i")
                dst = dst.rearrange("c (t e) -> c t e", t=2)
                src = t["lru_b_gate_2"][l, :, half:half + HEAD].rearrange("(c t) e -> c t e", t=2)
            elif name == "conv4_w":
                src = t["lru_conv_w_2"][l].rearrange("k (c p) -> (k c) p", p=P)
            elif name == "dw_w":
                src = t["conv_dw_w_2"][l].rearrange("k (c p) -> (k c) p", p=P)
            else:
                assert name == "final_norm"
                src = t["final_norm_2"].rearrange("(c p) -> c p", p=P)[l * n:(l + 1) * n, :]
            out.append((dst, src))
    return out


_INS = ["x", "mem", "positions", "w_in", "w_fourier", "w_mem_kv", "w_out", "w_ffn_in", "w_ffn_out", "sink",
        "g_pre_mix", "g_mem", "g_grp", "g_post_mix", "g_pre_ffn", "g_post_ffn",
        "positions_2", "ffn1_norm_2", "ffn1_w1_2", "ffn1_w2_2", "mix_norm_2", "w_in_2", "b_in_2", "lru_conv_w_2",
        "lru_conv_b_2", "lru_w_gate_2", "lru_b_gate_2", "lru_lambda_2", "lru_w_out_2", "q_norm_2", "w_uq_2",
        "kv_norm_2", "w_ukv_2", "mla_w_o_2", "conv_dw_w_2", "conv_dw_b_2", "conv_ln_g_2", "conv_ln_b_2",
        "conv_w_out_2", "conv_b_out_2", "w_out_2", "ffn2_norm_2", "ffn2_w1_2", "ffn2_w2_2", "final_norm_2"]


def kernel(**inputs):
    import concourse.bacc as _bacc
    from concourse.bass_utils import run_bass_kernel_spmd as _run

    nc = _bacc.Bacc("TRN2", target_bir_lowering=False, num_devices=1)
    arrays, t = {}, {}
    for name in _INS:
        arrays[f"in_{name}"] = np.ascontiguousarray(inputs[name])
    arrays["in_consts"] = constants()
    arrays["in_dft"] = sequence_dft()
    for name, a in arrays.items():
        t[name[3:]] = nc.dram_tensor(name, a.shape, mybir.dt.from_np(a.dtype), kind="ExternalInput").ap()
    out = nc.dram_tensor("out_x", (1, SEQ, D), F32, kind="ExternalOutput").ap()
    two_blocks(nc, t, out)
    r = _run(nc, [arrays], core_ids=[0])
    return r.results[0]["out_x"]
```

```python
from contextlib import ExitStack

import numpy as np

import concourse.bass as bass
from concourse import mybir

F32 = mybir.dt.float32
F32R = mybir.dt.float32r
I32 = mybir.dt.int32
ALU = mybir.AluOpType
ACT = mybir.ActivationFunctionType

P = 128
DEPTH = 2
SEQ = 512
D = 1024
DC = D // P
TC = SEQ // P
MEM = 256
FF = 2816
FC = FF // P
HEAD = 64
WINDOW_HEADS = 8
MEM_HEADS = 4
IN_1 = 1280
LRU = 512
LC = LRU // P
Q_RANK = 384
KV_RANK = 256
MLA_HEADS = 8
QK = 96
PE_DIM = 32
CONV_TAPS = 31
LRU_TAPS = 4
IN_B = 1024
IN_C = IN_B + Q_RANK + KV_RANK + PE_DIM
IN_G = IN_C + 1024
D_IN = IN_G + 3 * D
EPS = 1e-6
MASKED = -1e30
UNIT = 16 * P

PARAM_ROWS = [
    ("g_pre_mix", 8), ("g_mem", 8), ("g_grp", 8), ("g_post_mix", 8), ("g_pre_ffn", 8),
    ("g_post_ffn", 8), ("ffn1_norm", 8), ("mix_norm", 8), ("b_a", 8), ("b_b", 5), ("b_kpe", 1),
    ("b_c", 8), ("b_g", 24), ("conv4_w", 16), ("conv4_b", 4), ("b_r", 4), ("b_i", 4),
    ("lambda", 4), ("q_norm", 3), ("kv_norm", 2), ("dw_b", 4), ("ln_g", 4),
    ("ln_b", 4), ("conv_b_out", 8), ("ffn2_norm", 8),
    ("final_norm", DC // DEPTH),
]


def param_columns():
    at, columns = 0, {}
    for name, rows in PARAM_ROWS:
        if at // P != (at + DEPTH * rows - 1) // P:
            at = -(-at // P) * P
        columns[name] = (at, rows)
        at += DEPTH * rows
    at = -(-at // P) * P
    columns["dw_w"] = (at, P)
    return columns, at // P + DEPTH


def rope_frequencies():
    half1 = HEAD // 2
    f1 = np.exp(np.float32(-np.log(10000.0)) * np.arange(half1, dtype=np.float32) * np.float32(2.0 / HEAD))
    f2 = np.float32(10000.0) ** (-np.arange(0, PE_DIM, 2, dtype=np.float32) / np.float32(PE_DIM))
    out = np.zeros((P, 2), np.float32)
    out[:, 0] = np.tile(f1.astype(np.float32), P // half1)
    out[HEAD:HEAD + PE_DIM, 1] = np.tile(f2.astype(np.float32), 2)
    return out


def rotate_half(n, half):
    m = np.zeros((n, n), np.float32)
    for r in range(n):
        base, j = r - r % (2 * half), r % (2 * half)
        if j < half:
            m[base + j + half, r] = -1.0
        else:
            m[base + j - half, r] = 1.0
    return m


CONSTS = {}


def constants():
    parts = []

    def add(name, a):
        wide = np.zeros((P, a.shape[1]), np.float32)
        wide[:a.shape[0]] = a
        CONSTS[name] = (sum(p.shape[1] for p in parts), a.shape[1])
        parts.append(wide)

    i = np.arange(P)
    add("ident", np.eye(P, dtype=np.float32))
    causal = np.where(i[None, :] <= i[:, None], 0.0, MASKED)
    add("causal", np.concatenate([np.zeros((P, 3 * P)), causal], axis=1))
    r96 = np.zeros((P, QK), np.float32)
    r96[HEAD:QK, HEAD:QK] = rotate_half(PE_DIM, PE_DIM // 2)
    add("rot96", r96)
    add("freq", rope_frequencies())
    before = np.where(i[None, :] >= i[:, None], 0.0, MASKED)
    add("window", np.concatenate([before, np.zeros((P, P)), causal], axis=1))
    rot = rotate_half(P, HEAD // 2)
    add("rot_q", rot)
    for j in range(2):
        dup = np.zeros((P, P), np.float32)
        dup[HEAD * j + i % HEAD, i] = 1.0
        add(f"dup{j}", dup)
        add(f"rot_k{j}", dup @ rot)
    n = np.arange(HEAD)
    ang = 2 * np.pi * ((n[:, None] * n[None, :]) % HEAD) / HEAD
    for name, m in (("dft_cos", np.cos(ang) / 8.0), ("dft_sin", -np.sin(ang) / 8.0)):
        add(name, np.kron(np.eye(2), m).astype(np.float32))
    return np.ascontiguousarray(np.concatenate(parts, axis=1).astype(np.float32))


def sequence_dft():
    n = np.arange(SEQ)
    ang = 2 * np.pi * ((n[:, None] * n[None, :]) % SEQ) / SEQ
    return np.ascontiguousarray(
        (np.stack([np.cos(ang), np.sin(ang)], axis=1) / np.sqrt(SEQ)).astype(np.float32))


class Tally:

    wrong = []
    carrier = None

    def __init__(self, eng_name):
        self.eng_name = eng_name
        self.before, self.n = {}, {}
        self.layer = self.turn = None
        self.per_layer, self.per_turn = {}, {}
        self.unit = self.split = self.group = 0

    def apart(self, eng):
        eng.sem_inc(self.carrier, 1)

    def one(self, name, by=1):
        self.n[name] = self.n.get(name, 0) + by
        return by

    def now(self, name):
        value = self.before.get(name, 0) + self.n.get(name, 0)
        if self.layer is not None and self.per_layer.get(name, 0):
            value = self.layer * self.per_layer[name] + value
        if self.turn is not None and self.per_turn.get(name, 0):
            value = self.turn * self.per_turn[name] + value
        return value

    def next(self, name, by=1):
        self.one(name, by)
        return self.now(name)

    def layers(self, eng, per_layer, label):
        self.apart(eng)
        with eng.Fori(0, DEPTH) as layer:
            for name, n in self.n.items():
                self.before[name] = self.before.get(name, 0) + n
            self.layer, self.n, self.per_layer = layer, {}, per_layer
            yield layer
            for name, n in self.n.items():
                if n and n != per_layer.get(name, 0):
                    self.wrong.append((label, name, n, self.eng_name))
            for name, n in per_layer.items():
                self.before[name] = self.before.get(name, 0) + DEPTH * n
            self.layer, self.n = None, {}

    def turns(self, eng, first, end, per_turn, label):
        start = dict(self.n)
        self.apart(eng)
        with eng.Fori(first, end) as turn:
            self.per_turn = per_turn
            self.turn = turn
            for name, n in per_turn.items():
                self.n[name] = self.n.get(name, 0) - first * n
            shifted = dict(self.n)
            yield turn
            for name in set(self.n):
                made = self.n[name] - shifted.get(name, 0)
                if name in per_turn and made == 0:
                    self.n[name] = start.get(name, 0)
                    continue
                if made != per_turn.get(name, 0):
                    self.wrong.append((label, name, made, self.eng_name))
                self.n[name] = start.get(name, 0) + (end - first) * made
            self.turn = None


GROUPS = ((0, 1), (2, 3, 4, 5), (6, 7))
RANKS = ((0, 1, 2), (3, 4))

PER_LAYER = {
    "one": {"ah_ready": 32, "al_ready": 32, "c1_loaded": 128, "dft_loaded": 16, "diag_ready": 8,
        "dve_step": 162, "e_ready": 48, "four_copied": 7, "four_ready": 7, "h_ready": 11, "hh_ready": 11,
        "hi_ready": 46, "hl_ready": 11, "lo_ready": 46, "m_ready": 48, "mem_loaded": 16, "o_ready": 6,
        "o_used": 6, "p_ready": 48, "piece_done": 46, "pow_asked": 6, "pow_done": 6, "pt_ready": 48,
        "raw_loaded0": 736, "raw_loaded1": 736, "read_out0": 19, "read_out1": 19, "rope_ready": 6,
        "rot_ready": 8, "rot_used": 8, "s_ready": 48, "silu_ready": 11, "sq_ready": 48, "sq_used": 40,
        "src_ready": 8, "sum_ready": 14, "swap_copied": 6, "swap_ready": 6, "t_ready": 48,
        "totals_ready": 1, "wf_loaded": 32, "wf_zeroed": 1, "x_ready": 16},
    "two": {"act_step": 4, "ah_ready": 57, "al_ready": 37, "angle": 2, "bias_done": 18, "branch_ready": 8,
        "centred": 1, "conv_done": 1, "diag_ready": 6, "dve_step": 294, "e2_ready": 4, "e_ready": 32,
        "gate_loaded": 64, "gate_ready": 16, "gate_zeroed": 1, "gates_ready": 8, "h_ready": 22,
        "hh_ready": 22, "hi_ready": 110, "hl_ready": 30, "ln_ready": 4, "lo_ready": 110, "m_ready": 32,
        "mean_ready": 1, "merged_ready": 8, "o_ready": 4, "o_used": 4, "p_ready": 32, "piece_done": 116,
        "pos_loaded": 16, "pow_asked": 5, "pow_done": 5, "pt_ready": 32, "raw_loaded0": 1760,
        "raw_loaded1": 1760, "read_out0": 50, "read_out1": 50, "region_free": 1, "root_asked": 4,
        "root_done": 4, "rope_ready": 16, "rot_ready": 9, "rot_used": 9, "s_ready": 32, "sig_ready": 8,
        "silu_ready": 22, "sin_done": 2, "soft_exp": 1, "soft_in": 1, "sq_ready": 33, "sq_used": 24,
        "src_ready": 13, "sum_ready": 11, "swap_copied": 8, "swap_ready": 8, "t_ready": 32,
        "totals_ready": 2, "v_ready": 4, "x_ready": 24, "xa_ready": 4},
}
PER_TURN = {
    "ffn_in": {"h_ready": 1, "hh_ready": 1, "hi_ready": 2, "hl_ready": 1, "lo_ready": 2, "piece_done": 2,
        "raw_loaded0": 32, "raw_loaded1": 32, "read_out0": 1, "read_out1": 1, "silu_ready": 1},
    "ffn_out": {"hi_ready": 6, "lo_ready": 6, "piece_done": 6, "raw_loaded0": 96, "raw_loaded1": 96,
        "read_out0": 1, "read_out1": 1, "sq_ready": 4, "sq_used": 4},
    "w_out": {"hi_ready": 2, "lo_ready": 2, "piece_done": 2, "raw_loaded0": 32, "raw_loaded1": 32,
        "read_out0": 1, "read_out1": 1},
    "merge": {"ah_ready": 2, "dve_step": 4, "gate_ready": 4, "hi_ready": 6, "hl_ready": 2, "lo_ready": 6,
        "merged_ready": 2, "piece_done": 6, "raw_loaded0": 96, "raw_loaded1": 96, "read_out0": 3,
        "read_out1": 3, "src_ready": 2},
}


def two_blocks(nc, t, out):
    columns, n_param_tiles = param_columns()

    base = -(-nc.sbuf_base // 64) * 64
    top = [base]

    def place(name, shape, dt=F32, at=None):
        size = 4 * int(np.prod(shape[1:]))
        offset = top[0] if at is None else at
        if at is None:
            top[0] += -(-size // 32) * 32
        return nc.alloc_sbuf_tensor_at(name, shape, dt, offset=offset)

    KB = 1024
    xT = place("xT", [P, DC, SEQ])
    raw = place("raw", [P, 2, UNIT])
    w_hi = place("w_hi", [P, 2, UNIT], F32R)
    w_lo = place("w_lo", [P, 2, UNIT], F32R)
    ident = place("ident", [P, P])
    ones = place("ones", [P, P])
    rot96 = place("rot96", [P, QK])
    causal = place("causal", [P, SEQ])
    freq = place("freq", [P, 2])
    params = place("params", [P, n_param_tiles * P])
    stats = place("stats", [P, 4, 32])
    sinks = place("sinks", [P, DEPTH * WINDOW_HEADS])
    minus_sinks = place("minus_sinks", [P, DEPTH * WINDOW_HEADS])
    decay = place("decay", [P, 2, DEPTH * LC])
    tiny = place("tiny", [P, 6, DEPTH * LC])
    mean_sq = place("mean_sq", [P, len(GROUPS) * TC])
    minus_half = place("minus_half", [P, len(GROUPS) * TC])
    rs = place("rs", [P, SEQ])
    rs_b = place("rs_b", [P, SEQ])
    cosT = place("cosT", [P, SEQ])
    sinT = place("sinT", [P, SEQ])
    X = place("X", [P, 4, SEQ])
    REGION_A = top[0]
    a_hi = place("a_hi", [P, DC, SEQ], F32R)
    a_lo = place("a_lo", [P, DC, SEQ], F32R)
    y_ffn = place("y_ffn", [P, DC, SEQ], at=REGION_A)
    dft = place("dft", [P, TC, 2, SEQ], at=REGION_A)
    ab = place("ab", [P, TC, SEQ], at=REGION_A + 16 * KB)
    rows = place("rows", [P, n_param_tiles, P], at=REGION_A)
    out_tok = place("out_tok", [P, TC, D], at=REGION_A)
    REGION_B = top[0]
    h_hi = place("h_hi", [P, FC, SEQ], F32R)
    h_lo = place("h_lo", [P, FC, SEQ], F32R)
    x_tok = place("x_tok", [P, TC, D], at=REGION_B)
    b1 = [REGION_B]

    def in_b(name, shape, dt=F32):
        at = b1[0]
        b1[0] += 4 * int(np.prod(shape[1:]))
        assert b1[0] <= top[0]
        return place(name, shape, dt, at=at)

    mem_tok = place("mem_tok", [P, MEM // P, D], at=REGION_B)
    memT = place("memT", [P, DC, MEM], at=REGION_B + 8 * KB)
    y_mix = in_b("y_mix", [P, DC, SEQ])
    zfT = in_b("zfT", [P, 2, SEQ])
    qT = in_b("qT", [P, 4, SEQ])
    zkT = in_b("zkT", [P, SEQ])
    kT = in_b("kT", [P, 2, SEQ])
    vT = in_b("vT", [P, SEQ])
    v_tok = in_b("v_tok", [P, TC, P])
    zmT = in_b("zmT", [P, 2, SEQ])
    kmT = in_b("kmT", [P, 2, MEM])
    vmT = in_b("vmT", [P, 2, MEM])
    vm_tok = in_b("vm_tok", [P, 2, 2 * P])
    wf = in_b("wf", [P, 2, P])
    mf = in_b("mf", [P, 2, 2, P])
    c1 = {name: in_b("c_" + name, [P, CONSTS[name][1]])
          for name in ("window", "rot_q", "dup0", "rot_k0", "dup1", "rot_k1", "dft_cos", "dft_sin")}
    m_hi = in_b("m_hi", [P, DC, MEM], F32R)
    m_lo = in_b("m_lo", [P, DC, MEM], F32R)
    b1[0] = REGION_B
    yc_hi = in_b("yc_hi", [P, LC, SEQ], F32R)
    yc_lo = in_b("yc_lo", [P, LC, SEQ], F32R)
    ya_hi = in_b("ya_hi", [P, LC, SEQ], F32R)
    ya_lo = in_b("ya_lo", [P, LC, SEQ], F32R)
    yb_hi = in_b("yb_hi", [P, LC, SEQ], F32R)
    yb_lo = in_b("yb_lo", [P, LC, SEQ], F32R)
    REGION_T = b1[0]
    conv = in_b("conv", [P, LC, SEQ])
    gelu = in_b("gelu", [P, LC, SEQ])
    xa = in_b("xa", [P, LC, SEQ])
    glu = in_b("glu", [P, LC, SEQ + CONV_TAPS - 1])
    xpad = place("xpad", [P, LC, SEQ + LRU_TAPS - 1], at=REGION_B)
    sig = place("sig", [P, LC, 2, SEQ], at=REGION_B)
    craw_sq = place("craw_sq", [P, 5, SEQ], at=REGION_B + 16 * KB)
    lru_tmp = place("lru_tmp", [P, 3, SEQ], at=REGION_B + 26 * KB)
    craw = place("craw", [P, 6, SEQ], at=REGION_B + 32 * KB)
    gate_w = place("gate_w", [P, LC, 2, P], at=REGION_B + 44 * KB)
    q_head = place("q_head", [P, MLA_HEADS, SEQ], at=REGION_T)
    kv_head = place("kv_head", [P, MLA_HEADS, SEQ], at=REGION_T + 16 * KB)
    v_head = place("v_head", [P, TC, MLA_HEADS * HEAD], at=REGION_T + 32 * KB)
    mg_hi = place("mg_hi", [P, DC, SEQ], F32R, at=REGION_T)
    mg_lo = place("mg_lo", [P, DC, SEQ], F32R, at=REGION_T + 16 * KB)

    def step(q, k, v, n, out, mask, opens, closes, scale, sink=None):
        return dict(q=q, k=k, v=v, n=n, out=out, mask=mask, opens=opens, closes=closes, scale=scale, sink=sink)

    def window_steps(q, k, v):
        steps = []
        for h in range(WINDOW_HEADS):
            half, kv = (h % 2) * HEAD, h // (WINDOW_HEADS // 2)
            for b in range(TC):
                first, end = max(b - 1, 0), min(b + 2, TC)
                steps.append(step(
                    q[half:half + HEAD, h // 2, b * P:(b + 1) * P], k[half:half + HEAD, kv, first * P:end * P],
                    [v[:, j, kv * HEAD:(kv + 1) * HEAD] for j in range(first, end)], (end - first) * P,
                    (half, b * P), c1["window"][:, (first - b + 1) * P:(end - b + 1) * P],
                    h % 2 == 0 and b == 0, h % 2 == 1 and b == TC - 1, HEAD ** -0.5, h))
        return steps

    def memory_steps(q, k, v):
        steps = []
        for h in range(MEM_HEADS):
            half = (h % 2) * HEAD
            for b in range(TC):
                steps.append(step(
                    q[half:half + HEAD, h // 2, b * P:(b + 1) * P], k[half:half + HEAD, h // 2, :],
                    [v[:, j, h * HEAD:(h + 1) * HEAD] for j in range(MEM // P)], MEM,
                    (half, b * P), causal[:, 0:MEM], h % 2 == 0 and b == 0, h % 2 == 1 and b == TC - 1, HEAD ** -0.5))
        return steps

    def mla_steps(q, k, v):
        steps = []
        for h in range(MLA_HEADS):
            for b in range(TC):
                n = (b + 1) * P
                steps.append(step(
                    q[0:QK, h, b * P:n], k[0:QK, h, 0:n], [v[:, j, h * HEAD:(h + 1) * HEAD] for j in range(b + 1)], n,
                    ((h % 2) * HEAD, b * P), causal[:, SEQ - n:SEQ], h % 2 == 0 and b == 0, h % 2 == 1 and b == TC - 1,
                    QK ** -0.5))
        return steps

    stack = ExitStack()
    with stack:
        G = [stack.enter_context(nc.psum_tensor(f"products{i}", [P, 2, SEQ], F32)) for i in range(2)]
        B4, B5, B6, B7 = (stack.enter_context(nc.psum_tensor(f"small{i}", [P, SEQ], F32)) for i in range(4))
        sems = {}

        def sem(name):
            sems[name] = stack.enter_context(nc.semaphore(name))
            return sems[name]

        raw_loaded = [sem("raw_loaded0"), sem("raw_loaded1")]
        hi_ready = sem("hi_ready")
        lo_ready = sem("lo_ready")
        piece_done = sem("piece_done")
        read_out = [sem("read_out0"), sem("read_out1")]
        consts_loaded, x_loaded, rows_zeroed = sem("consts_loaded"), sem("x_loaded"), sem("rows_zeroed")
        rows_loaded, pos_loaded, turned = sem("rows_loaded"), sem("pos_loaded"), sem("turned")
        turn_copied, angle, table = sem("turn_copied"), sem("angle"), sem("table")
        soft_in, soft_exp, setup_done = sem("soft_in"), sem("soft_exp"), sem("setup_done")
        sin_done = sem("sin_done")
        x_ready = sem("x_ready")
        src_ready = sem("src_ready")
        ah_ready, al_ready = sem("ah_ready"), sem("al_ready")
        sq_ready, sq_used = sem("sq_ready"), sem("sq_used")
        totals_ready = sem("totals_ready")
        sum_ready = sem("sum_ready")
        pow_asked, pow_done = sem("pow_asked"), sem("pow_done")
        diag_ready = sem("diag_ready")
        root_asked, root_done = sem("root_asked"), sem("root_done")
        dve_step, act_step, pool_step = sem("dve_step"), sem("act_step"), sem("pool_step")
        silu_ready, h_ready, hh_ready, hl_ready = (sem(n) for n in ("silu_ready", "h_ready", "hh_ready", "hl_ready"))
        y_copied = sem("y_copied")
        mem_loaded, c1_loaded, wf_zeroed, wf_loaded, dft_loaded = (
            sem(n) for n in ("mem_loaded", "c1_loaded", "wf_zeroed", "wf_loaded", "dft_loaded"))
        rot_ready, rot_used, rope_ready = sem("rot_ready"), sem("rot_used"), sem("rope_ready")
        swap_ready, swap_copied = sem("swap_ready"), sem("swap_copied")
        four_ready, four_copied = sem("four_ready"), sem("four_copied")
        s_ready, m_ready, e_ready, p_ready = (sem(n) for n in ("s_ready", "m_ready", "e_ready", "p_ready"))
        t_ready, pt_ready, o_ready, o_used = (sem(n) for n in ("t_ready", "pt_ready", "o_ready", "o_used"))
        region_free, gate_zeroed, gate_loaded = sem("region_free"), sem("gate_zeroed"), sem("gate_loaded")
        branch_ready = sem("branch_ready")
        bias_done, xa_ready = sem("bias_done"), sem("xa_ready")
        gates_ready, sig_ready, e2_ready, v_ready = (sem(n) for n in ("gates_ready", "sig_ready", "e2_ready", "v_ready"))
        conv_done, mean_ready, centred, ln_ready = (sem(n) for n in ("conv_done", "mean_ready", "centred", "ln_ready"))
        gate_ready, merged_ready = sem("gate_ready"), sem("merged_ready")
        final_ready, tok_copied, stored = sem("final_ready"), sem("tok_copied"), sem("stored")

        Tally.carrier = sem("wait_carrier")
        row_loads = row_copies(t, rows, columns)
        n_setup_loads = 5

        block = stack.enter_context(nc.Block())

        def col(name, l, c, last=P):
            first, step = columns[name]
            return params[0:last, bass.ds(l * step + (first + c), 1)]

        prob_tiles = [X[:, i, :] for i in range(3)]
        turned_tiles = [X[:, 3, :], rs_b]

        mix_squares = [qT[:, i, :] for i in range(4)] + [tile[:, i, :] for tile in (zmT, kT) for i in range(2)]
        conv_squares = [craw[:, i, :] for i in range(LC)]
        lru_tanh, lru_square = (lru_tmp[:, 0, :], lru_tmp[:, 1, :]), (lru_tmp[:, 2, :], rs_b[:])
        rank_squares = [craw_sq[:, i, :] for i in range(5)]

        def wide(ap, n):
            return ap.unsqueeze(1).broadcast_to([ap.shape[0], n, ap.shape[-1]])

        @block.sync
        def _(sp):
            c = Tally("sync")
            sp.dma_start(x_tok[:], t["x"].rearrange("o (t p) d -> p (o t) d", p=P)).then_inc(x_loaded, 16)
            sp.wait_ge(rows_zeroed, 1)
            for dst, src in row_loads[1::2]:
                sp.dma_start(dst, src).then_inc(rows_loaded, 16)

            def unit(*parts):
                s = c.unit % 2
                c.unit += 1
                assert len(parts) == 2
                sp.wait_ge(lo_ready, c.next("lo_ready"))
                c.apart(sp)
                for w, l, row, nk, first, n, at in parts:
                    sp.dma_start(
                        raw[:, s, at:at + nk * n].rearrange("p (k n) -> p k n", n=n),
                        t[w][bass.ds(l, 1), row:row + nk * P, bass.ds(first, n)].rearrange("o (k p) n -> p (o k) n", p=P),
                    ).then_inc(raw_loaded[s], 16)

            def tall(w, l, first, n=2 * P, row=0, nk=DC):
                half = nk // 2
                unit((w, l, row, half, first, n, 0), (w, l, row + half * P, nk - half, first, n, half * n))

            def ffn(w1, w2, l, label):
                tall(w1, l, 0)
                tall(w1, l, FF)
                for i in c.turns(sp, 1, FF // (2 * P), PER_TURN["ffn_in"], "ffn_in"):
                    tall(w1, l, i * (2 * P))
                    tall(w1, l, i * (2 * P) + FF)
                for i in c.turns(sp, 0, 2, PER_TURN["ffn_out"], "ffn_out"):
                    for j in range(2):
                        for row, nk in ((0, 8), (8, 8), (16, 6)):
                            tall(w2, l, i * (4 * P) + 2 * P * j, row=row * P, nk=nk)

            for l in c.layers(sp, PER_LAYER["one"], "one"):
                tall("w_in", l, 0)
                tall("w_in", l, 2 * P)
                tall("w_in", l, 4 * P)
                tall("w_in", l, 6 * P, P)
                tall("w_in", l, 7 * P, P)
                tall("w_in", l, 8 * P)
                for j in range(2):
                    tall("w_mem_kv", l, 2 * P * j)
                for i in c.turns(sp, 0, 2, PER_TURN["w_out"], "w_out"):
                    for j in range(2):
                        tall("w_out", l, i * (4 * P) + 2 * P * j)
                ffn("w_ffn_in", "w_ffn_out", l, "one")
            for l in c.layers(sp, PER_LAYER["two"], "two"):
                ffn("ffn1_w1_2", "ffn1_w2_2", l, "two")
                for j in range(LC):
                    unit(("w_in_2", l, 0, DC, IN_C + P * j, P, 0), ("w_in_2", l, 0, DC, IN_C + LRU + P * j, P, UNIT // 2))
                for j in range(4):
                    tall("w_in_2", l, 2 * P * j)
                tall("w_in_2", l, IN_B)
                tall("w_in_2", l, IN_B + 2 * P)
                tall("w_in_2", l, IN_B + 4 * P, n=P + PE_DIM)
                unit(("w_ukv_2", l, 0, 1, 0, 2 * LRU, 0), ("w_ukv_2", l, P, 1, 0, 2 * LRU, 2 * LRU))
                for j in range(2):
                    unit(("w_uq_2", l, 0, 2, 4 * QK * j, 4 * QK, 0), ("w_uq_2", l, 2 * P, 1, 4 * QK * j, 4 * QK, 8 * QK))
                for i in c.turns(sp, 0, DC // 2, PER_TURN["merge"], "merge"):
                    for j in range(2):
                        at = i * (2 * P) + P * j
                        unit(("w_in_2", l, 0, DC, at + IN_G, P, 0), ("w_in_2", l, 0, DC, at + (IN_G + D), P, UNIT // 2))
                        unit(("w_in_2", l, 0, DC, at + (IN_G + 2 * D), P, 0), ("lru_w_out_2", l, 0, LC, at, P, UNIT // 2))
                        unit(("mla_w_o_2", l, 0, LC, at, P, 0), ("conv_w_out_2", l, 0, LC, at, P, LC * P))
                for i in c.turns(sp, 0, 2, PER_TURN["w_out"], "w_out"):
                    for j in range(2):
                        tall("w_out_2", l, i * (4 * P) + 2 * P * j)
                ffn("ffn2_w1_2", "ffn2_w2_2", l, "two")
            for s in range(2):
                sp.wait_ge(lo_ready, c.next("lo_ready"))
                sp.sem_inc(raw_loaded[s], 32)
            for tc in range(TC):
                sp.wait_ge(tok_copied, c.next("tok_copied"))
                sp.dma_start(out[0, tc * P:(tc + 1) * P, :], out_tok[:, tc, :]).then_inc(stored, 16)
            sp.wait_ge(stored, 16 * TC)

        @block.tensor
        def _(pe):
            c = Tally("tensor")
            c.n["lo_ready"] = 2
            c.n["sq_used"] = 1

            def take_unit():
                pe.wait_ge(lo_ready, c.next("lo_ready"))
                c.unit += 1

            def piece(blocks, first=True, last=True, n=SEQ, fresh=None, between=None):
                s = (c.unit - 1) % 2
                pair = c.group % 2
                if first:
                    pe.wait_ge(read_out[pair], c.next(f"read_out{pair}"))
                for b, (m, terms) in enumerate(blocks):
                    if b == 1 and between:
                        between()
                    for k, (at, hi, lo) in enumerate(terms):
                        if fresh and b == 0:
                            pe.wait_ge(sems[fresh], c.next(fresh))
                        for q, (w, x) in enumerate(((w_hi, hi), (w_hi, lo), (w_lo, hi))):
                            mm = pe.matmul(G[pair][0:m, b, 0:n], w[:, s, at:at + m], x,
                                           start=first and k == 0 and q == 0,
                                           stop=last and k == len(terms) - 1 and q == 2)
                mm.then_inc(piece_done, 1)
                if last:
                    c.group += 1

            def tall(nk, width, hi, lo, k0=0, blocks=2, **how):
                piece([(P, [(k * width + b * P, hi[:, k0 + k, :], lo[:, k0 + k, :]) for k in range(nk)])
                       for b in range(blocks)], **how)

            def full(fresh=None, blocks=2, hi=a_hi, lo=a_lo, n=SEQ, between=None):
                take_unit()
                tall(DC, blocks * P, hi, lo, blocks=blocks, fresh=fresh, n=n, between=between)

            def sum_channels(n=SEQ):
                pe.wait_ge(sq_used, c.now("sq_used"))
                for i in range(n // P):
                    mm = pe.matmul(B7[:, i:i + 1], X[:, 1, i * P:(i + 1) * P], ones[:, 0:1], start=True, stop=True)
                mm.then_inc(sum_ready, 1)

            def sum_groups(totals, between=None):
                pe.wait_ge(totals_ready, c.next("totals_ready"))
                for g, total in enumerate(totals):
                    for i in range(TC):
                        at = g * TC + i
                        mm = pe.matmul(B7[:, at:at + 1], total[:, i * P:(i + 1) * P], ones[:, 0:1], start=True, stop=True)
                mm.then_inc(sum_ready, 1)
                if between:
                    between()
                for bank, total in zip((B4, B5, B6), totals):
                    pe.wait_ge(diag_ready, c.next("diag_ready"))
                    pe.matmul(bank[:], ones[:], total, start=True, stop=True).then_inc(sum_ready, 1)

            def spread(n=SEQ):
                pe.wait_ge(diag_ready, c.next("diag_ready"))
                pe.matmul(B7[:, 0:n], ones[:], X[:, 1, 0:n], start=True, stop=True).then_inc(sum_ready, 1)

            def ffn(post_norm):
                full(fresh="al_ready")
                c.one("sq_used", DC)
                sum_channels()
                full(between=spread)
                for _ in c.turns(pe, 1, FF // (2 * P), PER_TURN["ffn_in"], "ffn_in"):
                    full()
                    full()
                pe.wait_ge(hl_ready, c.next("hl_ready", FF // (2 * P)))
                for _ in c.turns(pe, 0, 2, PER_TURN["ffn_out"], "ffn_out"):
                    for j in range(2):
                        for k0, nk in ((0, 8), (8, 8), (16, 6)):
                            take_unit()
                            tall(nk, 2 * P, h_hi, h_lo, k0=k0, first=k0 == 0, last=k0 == 16)
                if post_norm:
                    c.one("sq_used", DC)
                    sum_channels()
                    spread()

            def attention(steps):
                n = len(steps)
                for s in range(n + 3):
                    if s < n:
                        st = steps[s]
                        if s >= 2:
                            pe.wait_ge(m_ready, c.next("m_ready"))
                        pe.matmul((B4, B5)[s % 2][:, 0:st["n"]], st["q"], st["k"], start=True, stop=True).then_inc(s_ready, 1)
                    if 2 <= s < n + 2:
                        st, tile = steps[s - 2], prob_tiles[(s - 2) % 3]
                        pe.wait_ge(p_ready, c.next("p_ready"))
                        if s >= 3:
                            pe.wait_ge(pt_ready, c.now("pt_ready") + 1)
                        for j in range(st["n"] // P):
                            mm = pe.transpose(B6[:, j * P:(j + 1) * P], tile[:, j * P:(j + 1) * P], ident[:])
                        mm.then_inc(t_ready, 1)
                    if s >= 3:
                        st, tile = steps[s - 3], turned_tiles[(s - 3) % 2]
                        pe.wait_ge(pt_ready, c.next("pt_ready"))
                        if st["opens"] and s > 3:
                            pe.wait_ge(o_used, c.next("o_used"))
                        vs = st["v"]
                        r0, c0 = st["out"]
                        for j, v in enumerate(vs):
                            mm = pe.matmul(B7[r0:r0 + HEAD, c0:c0 + P], v, tile[:, j * P:(j + 1) * P],
                                           start=j == 0, stop=j == len(vs) - 1)
                        if st["closes"]:
                            mm.then_inc(o_ready, 1)
                c.one("m_ready", 2)
                c.one("o_used")

            def all_read_out():
                for p in range(2):
                    pe.wait_ge(read_out[p], c.now(f"read_out{p}") + 1)

            pe.wait_ge(consts_loaded, c.next("consts_loaded", 16 * n_setup_loads))
            pe.wait_ge(x_loaded, 16)
            for i in range(DC):
                if i >= 2:
                    pe.wait_ge(turn_copied, i - 1)
                for tc in range(TC):
                    mm = pe.transpose((B4, B5)[i % 2][:, tc * P:(tc + 1) * P], x_tok[:, tc, i * P:(i + 1) * P], ident[:])
                mm.then_inc(turned, 1)
            pe.wait_ge(rows_loaded, c.next("rows_loaded", 16 * len(row_loads)))
            for i in range(DC, DC + n_param_tiles):
                pe.wait_ge(turn_copied, i - 1)
                pe.transpose((B4, B5)[i % 2][:, 0:P], rows[:, i - DC, :], ident[:]).then_inc(turned, 1)

            for l in c.layers(pe, PER_LAYER["one"], "one"):
                full(fresh="al_ready")
                c.one("sq_used", DC)
                sum_channels()
                pe.wait_ge(mem_loaded, c.next("mem_loaded", 16))
                for i in range(DC // 2):
                    if i:
                        pe.wait_ge(swap_copied, c.next("swap_copied"))
                    for j in range(4):
                        mm = pe.transpose(B6[:, j * P:(j + 1) * P],
                                          mem_tok[:, j % 2, (2 * i + j // 2) * P:(2 * i + j // 2 + 1) * P], ident[:])
                    mm.then_inc(swap_ready, 1)
                c.one("swap_copied")
                full(between=spread)
                full()
                full(blocks=1)
                full(blocks=1)
                full()
                take_unit()
                tall(DC, 2 * P, m_hi, m_lo, fresh="al_ready", n=MEM)
                c.one("sq_used", DC)
                sum_channels(MEM)
                spread(MEM)
                full(hi=m_hi, lo=m_lo, n=MEM)
                pe.wait_ge(c1_loaded, c.next("c1_loaded", 16 * len(c1)))
                all_read_out()
                for i in range(4):
                    if i >= 2:
                        pe.wait_ge(rot_used, c.next("rot_used"))
                    pe.matmul((B4, B5)[i % 2][:], c1["rot_q"][:], qT[:, i, :], start=True, stop=True).then_inc(rot_ready, 1)
                for j in range(2):
                    for bank, name in ((B4, f"dup{j}"), (B5, f"rot_k{j}")):
                        pe.wait_ge(rot_used, c.next("rot_used"))
                        pe.matmul(bank[:], c1[name][:], zkT[:], start=True, stop=True).then_inc(rot_ready, 1)
                c.one("rot_used", 2)
                pe.wait_ge(swap_copied, c.now("swap_copied"))
                for j in range(TC):
                    mm = pe.transpose(B6[:, j * P:(j + 1) * P], vT[:, j * P:(j + 1) * P], ident[:])
                mm.then_inc(swap_ready, 1)
                for j in range(4):
                    mm = pe.transpose(B7[:, j * P:(j + 1) * P], vmT[:, j % 2, (j // 2) * P:(j // 2 + 1) * P], ident[:])
                mm.then_inc(swap_ready, 1)
                pe.wait_ge(wf_loaded, c.next("wf_loaded", 32))
                pe.wait_ge(rot_used, c.now("rot_used"))
                for j in range(2):
                    for i, name in enumerate(("dft_cos", "dft_sin")):
                        at = (2 * j + i) * P
                        mm = pe.matmul(B4[:, at:at + P], c1[name][:], wf[:, j, :], start=True, stop=True)
                mm.then_inc(four_ready, 1)
                for tc in range(TC):
                    pe.wait_ge(four_copied, c.next("four_copied"))
                    for j in range(2):
                        mm = pe.matmul((B5, B4)[tc % 2][:, j * 2 * P:(j + 1) * 2 * P], zfT[:, j, tc * P:(tc + 1) * P],
                                       mf[:, j, :, :], start=True, stop=True)
                    mm.then_inc(four_ready, 1)
                pe.wait_ge(four_copied, c.next("four_copied"))
                pe.wait_ge(dft_loaded, c.next("dft_loaded", 16))
                for j in range(2):
                    for tc in range(TC):
                        for i in range(2):
                            mm = pe.matmul((B4, B5)[j][:], ab[:, tc, (2 * j + i) * P:(2 * j + i + 1) * P], dft[:, tc, i, :],
                                           start=tc == 0 and i == 0, stop=tc == TC - 1 and i == 1)
                    mm.then_inc(four_ready, 1)
                c.one("four_copied", 2)
                pe.wait_ge(four_copied, c.now("four_copied"))
                c.one("swap_copied", 2)
                pe.wait_ge(swap_copied, c.now("swap_copied"))
                pe.wait_ge(rope_ready, c.next("rope_ready", 6))
                attention(window_steps(qT, kT, v_tok))
                attention(memory_steps(zmT, kmT, vm_tok))
                sum_groups([mix_squares[chunks[0]] for chunks in GROUPS])
                take_unit()
                tall(DC, 2 * P, a_hi, a_lo, fresh="al_ready")
                full()
                full()
                full()
                c.one("sq_used", DC)
                sum_channels()
                spread()
                ffn(True)
            for l in c.layers(pe, PER_LAYER["two"], "two"):
                ffn(False)
                full_two_parts = [(P, [(b * UNIT // 2 + k * P, a_hi[:, k, :], a_lo[:, k, :]) for k in range(DC)]) for b in range(2)]
                take_unit()
                piece(full_two_parts, fresh="al_ready")
                c.one("sq_used", DC)
                sum_channels()
                take_unit()
                piece(full_two_parts, between=spread)
                for _ in range(LC - 2):
                    take_unit()
                    piece(full_two_parts)
                for _ in range(4):
                    full()
                pe.wait_ge(gate_loaded, c.next("gate_loaded", 64))
                for i in range(LC):
                    pe.wait_ge(xa_ready, c.next("xa_ready"))
                    if i >= 2:
                        pe.wait_ge(sig_ready, c.next("sig_ready", 2))
                    for j in range(2):
                        pe.matmul((B4, B5, B6, B7)[i % 2 * 2 + j][:], gate_w[:, i, j, :], xa[:, i, :],
                                  start=True, stop=True).then_inc(gates_ready, 1)
                c.one("sig_ready", 4)
                full()
                full()
                take_unit()
                wide_n = P + PE_DIM
                piece([(P, [(k * wide_n, a_hi[:, k, :], a_lo[:, k, :]) for k in range(DC)])])
                piece([(QK, [(k * wide_n + HEAD, a_hi[:, k, :], a_lo[:, k, :]) for k in range(DC)])])

                def conv_mean():
                    pe.wait_ge(conv_done, c.next("conv_done"))
                    for i in range(LC):
                        mm = pe.matmul(B6[:], ones[:], conv[:, i, :], start=i == 0, stop=i == LC - 1)
                    mm.then_inc(mean_ready, 1)

                pe.wait_ge(sig_ready, c.now("sig_ready"))
                sum_groups([rank_squares[chunks[0]] for chunks in RANKS], between=conv_mean)
                pe.wait_ge(al_ready, c.next("al_ready", 5))
                take_unit()
                for g in range(4):
                    piece([(P, [(k * 2 * LRU + (2 * g + b) * P, a_hi[:, 3 + k, :], a_lo[:, 3 + k, :]) for k in range(2)])
                           for b in range(2)])
                sum_groups([conv_squares[0]])
                pe.matmul(B5[0:QK, :], rot96[0:QK, :], craw[0:QK, 5, :], start=True, stop=True).then_inc(rot_ready, 1)
                all_read_out()
                for h in range(MLA_HEADS):
                    if h:
                        pe.wait_ge(swap_copied, c.next("swap_copied"))
                    for j in range(TC):
                        mm = pe.transpose(B6[:, j * P:(j + 1) * P], kv_head[:, h, j * P:(j + 1) * P], ident[:])
                    mm.then_inc(swap_ready, 1)
                c.one("swap_copied")
                for u in range(2):
                    take_unit()
                    for g in range(2):
                        piece([(QK, [(k * 4 * QK + (2 * g + b) * QK, a_hi[:, k, :], a_lo[:, k, :]) for k in range(3)])
                               for b in range(2)])
                all_read_out()
                for h in range(MLA_HEADS):
                    if h >= 1:
                        pe.wait_ge(rot_used, c.next("rot_used"))
                    pe.matmul((B4, B5)[h % 2][0:QK, :], rot96[0:QK, :], q_head[0:QK, h, :], start=True, stop=True).then_inc(rot_ready, 1)
                c.one("rot_used", 2)
                pe.wait_ge(swap_copied, c.now("swap_copied"))
                pe.wait_ge(rope_ready, c.next("rope_ready", 2 * MLA_HEADS))
                pe.wait_ge(rot_used, c.now("rot_used"))
                attention(mla_steps(q_head, kv_head, v_head))
                pe.wait_ge(o_used, c.now("o_used"))
                pe.wait_ge(branch_ready, c.next("branch_ready", 2 * LC))
                pe.wait_ge(al_ready, c.next("al_ready", DC))

                def eight(at):
                    return (P, [(at + k * P, a_hi[:, k, :], a_lo[:, k, :]) for k in range(DC)])

                def four(at, hi, lo):
                    return (P, [(at + k * P, hi[:, k, :], lo[:, k, :]) for k in range(LC)])

                for _ in c.turns(pe, 0, DC // 2, PER_TURN["merge"], "merge"):
                    for j in range(2):
                        take_unit()
                        piece([eight(0), eight(UNIT // 2)])
                        take_unit()
                        piece([eight(0), four(UNIT // 2, ya_hi, ya_lo)])
                        take_unit()
                        piece([four(0, yb_hi, yb_lo), four(LC * P, yc_hi, yc_lo)])
                pe.wait_ge(hl_ready, c.next("hl_ready", DC))
                for _ in c.turns(pe, 0, 2, PER_TURN["w_out"], "w_out"):
                    for j in range(2):
                        take_unit()
                        tall(DC, 2 * P, mg_hi, mg_lo)
                ffn(False)
            c.one("sq_used", DC)
            sum_channels()
            spread()
            pe.wait_ge(final_ready, 1)
            for tc in range(TC):
                if tc:
                    pe.wait_ge(tok_copied, tc)
                for i in range(DC):
                    mm = pe.transpose((B4, B5)[i // 4][:, (i % 4) * P:(i % 4 + 1) * P], xT[:, i, tc * P:(tc + 1) * P], ident[:])
                mm.then_inc(turned, 1)

        @block.scalar
        def _(act):
            c = Tally("scalar")
            c.n.update(read_out0=1, read_out1=1, sq_used=1)

            def split_hi():
                s = c.split % 2
                c.split += 1
                act.wait_ge(raw_loaded[s], c.next(f"raw_loaded{s}", 32))
                act.activation(w_hi[:, s, :], raw[:, s, :], ACT.Copy).then_inc(hi_ready, 1)

            def unit_done(pieces=1):
                act.wait_ge(piece_done, c.next("piece_done", pieces))
                split_hi()

            def out_name():
                name = c.group % 2
                c.group += 1
                return name

            def group_read():
                p = out_name()
                act.wait_ge(read_out[p], c.next(f"read_out{p}"))

            def group_skipped():
                c.one(f"read_out{out_name()}")

            def square(src, n=SEQ, at_register=False):
                act.wait_ge(sq_used, c.now("sq_used"))
                if at_register:
                    c.apart(act)
                act.activation(X[:, 0, 0:n], src, ACT.Square).then_inc(sq_ready, 1)
                c.one("sq_used")

            def operand(gain, l):
                for i in range(DC):
                    act.wait_ge(x_ready, c.next("x_ready"))
                    c.apart(act)
                    act.activation(a_hi[:, i, :], xT[:, i, :], ACT.Copy, scale=col(gain, l, i)).then_inc(ah_ready, 1)
                for i in range(DC):
                    if i >= 3:
                        act.wait_ge(sq_used, c.now("sq_used") - 2)
                    act.activation(X[:, (0, 2, 3)[i % 3], :], xT[:, i, :], ACT.Square).then_inc(sq_ready, 1)
                    c.one("sq_used")

            def ffn(gain, l, post_norm, between=None):
                operand(gain, l)

                def gate_and_up(i):
                    unit_done()
                    group_read()
                    act.activation(X[:, 0:2, :], X[:, 0:2, :], ACT.Silu).then_inc(silu_ready, 1)
                    unit_done()
                    group_skipped()
                    act.wait_ge(h_ready, c.next("h_ready"))
                    c.apart(act)
                    act.activation(h_hi[:, bass.ds(i * 2, 2), :], X[:, 2:4, :], ACT.Copy).then_inc(hh_ready, 1)

                gate_and_up(0)
                for i in c.turns(act, 1, FF // (2 * P), PER_TURN["ffn_in"], "ffn_in"):
                    gate_and_up(i)
                if between:
                    between()
                for i in c.turns(act, 0, 2, PER_TURN["ffn_out"], "ffn_out"):
                    for j in range(2):
                        for _ in range(3):
                            unit_done()
                        if post_norm:
                            copy_and_square(y_ffn, i * 4 + 2 * j)
                        else:
                            group_skipped()

            def copy_and_square(y, chunk):
                p = out_name()
                c.apart(act)
                act.activation(y[:, bass.ds(chunk, 2), :], G[p][:], ACT.Copy).then_inc(read_out[p], c.one(f"read_out{p}"))
                act.wait_ge(read_out[p], c.now(f"read_out{p}"))
                for b in range(2):
                    square(y[:, bass.ds(chunk + b, 1), :].rearrange("p o n -> p (o n)"), at_register=True)

            def attention(steps, l, leave):
                n = len(steps)
                for s in range(n + 3):
                    if s < n:
                        st = steps[s]
                        tile = prob_tiles[s % 3][:, 0:st["n"]]
                        act.wait_ge(m_ready, c.next("m_ready"))
                        e = act.activation(tile, tile, ACT.Exp, bias=stats[:, 3, s:s + 1], scale=st["scale"],
                                           accum_out=stats[:, 1, s:s + 1])
                        if st["sink"] is not None:
                            e = act.activation(stats[:, 2, s:s + 1], sinks[:, bass.ds(l * WINDOW_HEADS + st["sink"], 1)],
                                               ACT.Exp, bias=stats[:, 3, s:s + 1])
                        e.then_inc(e_ready, 1)
                    if 2 <= s < n + 2:
                        st = steps[s - 2]
                        act.wait_ge(t_ready, c.next("t_ready"))
                        act.activation(turned_tiles[(s - 2) % 2][:, 0:st["n"]], B6[:, 0:st["n"]], ACT.Copy).then_inc(pt_ready, 1)
                    if s >= 3 and steps[s - 3]["closes"]:
                        act.wait_ge(o_ready, c.next("o_ready"))
                        leave()

            act.dma_start(ident[:], t["consts"][:, CONSTS["ident"][0]:CONSTS["ident"][0] + P]).then_inc(consts_loaded, 16)
            for name, tile in (("rot96", rot96), ("causal", causal), ("freq", freq)):
                at, n = CONSTS[name]
                act.dma_start(tile[:], t["consts"][:, at:at + n]).then_inc(consts_loaded, 16)
            act.dma_start(sinks[:], t["sink"].rearrange("l h -> (l h)").partition_broadcast(P)).then_inc(consts_loaded, 16)
            act.dma_start(X[:, 0, :].bitcast(I32), t["positions"][0].partition_broadcast(P)).then_inc(pos_loaded, c.one("pos_loaded", 16))
            act.wait_ge(rows_zeroed, 1)
            for dst, src in row_loads[0::2]:
                act.dma_start(dst, src).then_inc(rows_loaded, 16)

            def sines():
                act.wait_ge(angle, c.next("angle"))
                act.activation(sinT[:], X[:, 3, :], ACT.Sin).then_inc(sin_done, c.one("sin_done"))
                act.wait_ge(angle, c.next("angle"))
                act.activation(cosT[:], X[:, 3, :], ACT.Sin).then_inc(sin_done, c.one("sin_done"))

            sines()
            split_hi()
            split_hi()

            for l in c.layers(act, PER_LAYER["one"], "one"):
                operand("g_pre_mix", l)
                unit_done()
                group_skipped()
                for i in range(DC // 2):
                    act.wait_ge(swap_ready, c.next("swap_ready"))
                    act.activation(memT[:, 2 * i:2 * i + 2, :], B6[:], ACT.Copy).then_inc(swap_copied, 1)
                act.wait_ge(swap_copied, c.next("swap_copied", DC // 2))
                c.apart(act)
                for i in range(DC):
                    act.activation(m_hi[:, i, :], memT[:, i, :], ACT.Copy, scale=col("g_mem", l, i)).then_inc(ah_ready, 1)
                    square(memT[:, i, :], MEM)
                for _ in range(7):
                    unit_done()
                    group_skipped()
                act.wait_ge(swap_ready, c.next("swap_ready"))
                act.activation(v_tok[:], B6[:], ACT.Copy).then_inc(swap_copied, 1)
                act.wait_ge(swap_ready, c.next("swap_ready"))
                act.activation(vm_tok[:], B7[:], ACT.Copy).then_inc(swap_copied, 1)
                c.one("swap_copied", 2)
                act.wait_ge(four_ready, c.next("four_ready"))
                act.activation(mf[:], B4[:], ACT.Copy).then_inc(four_copied, 1)
                for tc in range(TC):
                    act.wait_ge(four_ready, c.next("four_ready"))
                    act.activation(ab[:, tc, :], (B5, B4)[tc % 2][:], ACT.Copy).then_inc(four_copied, 1)
                for j in range(2):
                    act.wait_ge(four_ready, c.next("four_ready"))
                    act.activation(y_mix[:, j, :], (B4, B5)[j][:], ACT.Copy).then_inc(four_copied, 1)
                c.one("four_copied", 3 + TC)
                chunk = iter(range(2, DC))

                def leave():
                    act.activation(y_mix[:, next(chunk), :], B7[:], ACT.Copy).then_inc(o_used, c.one("o_used"))

                attention(window_steps(qT, kT, v_tok), l, leave)
                attention(memory_steps(zmT, kmT, vm_tok), l, leave)
                act.wait_ge(o_used, c.now("o_used"))
                act.wait_ge(four_copied, c.now("four_copied"))
                for i in range(DC):
                    act.activation(mix_squares[i], y_mix[:, i, :], ACT.Square).then_inc(sq_ready, 1)
                for i in range(DC):
                    act.wait_ge(src_ready, c.next("src_ready"))
                    act.activation(a_hi[:, i, :], X[:, 2 + i % 2, :], ACT.Copy).then_inc(ah_ready, 1)
                for j in range(4):
                    unit_done()
                    copy_and_square(y_mix, 2 * j)
                ffn("g_pre_ffn", l, True)

            c.one("x_ready", DC)

            def tables():
                act.wait_ge(hl_ready, c.next("hl_ready", FF // (2 * P)))
                c.apart(act)
                act.dma_start(X[:, 0, :].bitcast(I32), t["positions_2"][0].partition_broadcast(P)).then_inc(
                    pos_loaded, c.one("pos_loaded", 16))
                sines()
                act.wait_ge(soft_in, c.next("soft_in"))
                act.activation(tiny[:, 2, :], tiny[:, 1, :], ACT.Exp).then_inc(soft_exp, c.one("soft_exp"))
                c.one("hl_ready", DC + FF // (2 * P))

            for l in c.layers(act, PER_LAYER["two"], "two"):
                ffn("ffn1_norm", l, False, between=tables)
                operand("mix_norm", l)
                for j in range(LC):
                    unit_done()
                    group_read()
                    c.apart(act)
                    act.activation(X[:, 3, :], X[:, 3, :], ACT.Sigmoid, bias=col("b_c", l, LC + j)).then_inc(bias_done, 1)
                for j in range(4):
                    unit_done()
                    group_read()
                    c.apart(act)
                    for b in range(2):
                        i = 2 * j + b
                        dst = xpad[:, i, LRU_TAPS - 1:] if j < 2 else gelu[:, i - LC, :]
                        act.activation(dst, X[:, 2 + b, :], ACT.Identity if j < 2 else ACT.Gelu_apprx_tanh,
                                       bias=col("b_a", l, i)).then_inc(bias_done, 1)
                act.wait_ge(xa_ready, c.next("xa_ready", LC))
                for i in range(LC):
                    for j, name in enumerate(("b_r", "b_i")):
                        act.wait_ge(gates_ready, c.next("gates_ready"))
                        c.apart(act)
                        act.activation(sig[:, i, j, :], (B4, B5, B6, B7)[i % 2 * 2 + j][:], ACT.Sigmoid,
                                       bias=col(name, l, i)).then_inc(sig_ready, 1)
                c.one("sig_ready", 2 * LC)

                def lru_powers(i):
                    if i >= 2:
                        act.wait_ge(root_asked, c.next("root_asked"))
                    c.apart(act)
                    once, twice = (decay[:, j, bass.ds(l * LC + i, 1)] for j in range(2))
                    act.activation(lru_tanh[i % 2], sig[:, i, 0, :], ACT.Tanh, scale=once)
                    act.activation(lru_square[i % 2], sig[:, i, 0, :], ACT.Exp, scale=twice)
                    act.activation(sig[:, i, 0, :], sig[:, i, 0, :], ACT.Exp, scale=once).then_inc(e2_ready, 1)

                act.wait_ge(sig_ready, c.now("sig_ready"))
                for j in range(4):
                    if j != 2:
                        unit_done()
                    else:
                        act.wait_ge(piece_done, c.next("piece_done"))
                    group_read()
                    c.apart(act)
                    if j < 2:
                        for b in range(2):
                            act.activation(craw[:, 2 * j + b, :], X[:, 2 + b, :], ACT.Identity,
                                           bias=col("b_b", l, 2 * j + b)).then_inc(bias_done, 1)
                    elif j == 2:
                        act.activation(craw[:, 4, :], X[:, 2, :], ACT.Identity, bias=col("b_b", l, 4)).then_inc(bias_done, 1)
                    else:
                        act.activation(craw[0:QK, 5, :], X[0:QK, 2, :], ACT.Identity,
                                       bias=col("b_kpe", l, 0, QK)).then_inc(bias_done, 1)
                    if j < 3:
                        lru_powers(j)
                c.one("bias_done", LC + 8 + 6)
                act.wait_ge(bias_done, c.now("bias_done"))
                c.apart(act)
                for i in range(5):
                    act.activation(rank_squares[i], craw[:, i, :], ACT.Square).then_inc(sq_ready, 1)
                lru_powers(3)
                act.wait_ge(root_asked, c.next("root_asked", 2))
                c.apart(act)
                for i in range(LC):
                    act.activation(sig[:, i, 1, :], sig[:, i, 1, :], ACT.Sqrt, scale=-1.0).then_inc(root_done, 1)
                for i in range(5):
                    act.wait_ge(src_ready, c.next("src_ready"))
                    act.activation(a_hi[:, i, :], X[:, 1 + i % 2, :], ACT.Copy).then_inc(ah_ready, 1)
                act.wait_ge(centred, c.next("centred"))
                for i in range(LC):
                    act.activation(conv_squares[i], conv[:, i, :], ACT.Square).then_inc(sq_ready, 1)
                for i in range(LC):
                    act.wait_ge(v_ready, c.next("v_ready"))
                    act.activation(ya_hi[:, i, :], gelu[:, i, :], ACT.Copy).then_inc(ah_ready, 1)

                def take_heads(m, tile, first, end):
                    for h in range(first, end, 2):
                        act.wait_ge(piece_done, c.next("piece_done"))
                        p = out_name()
                        act.activation(tile[0:m, h:h + 2, :], G[p][0:m], ACT.Copy).then_inc(read_out[p], c.one(f"read_out{p}"))
                    split_hi()

                take_heads(P, kv_head, 0, MLA_HEADS)
                for i in range(LC):
                    act.wait_ge(ln_ready, c.next("ln_ready"))
                    c.apart(act)
                    act.activation(conv[:, i, :], conv[:, i, :], ACT.Silu, bias=col("ln_b", l, i),
                                   scale=col("ln_g", l, i)).then_inc(act_step, c.one("act_step"))
                    act.wait_ge(act_step, c.now("act_step"))
                    act.activation(yc_hi[:, i, :], conv[:, i, :], ACT.Copy).then_inc(ah_ready, 1)
                for h in range(MLA_HEADS):
                    act.wait_ge(swap_ready, c.next("swap_ready"))
                    act.activation(v_head[:, :, h * HEAD:(h + 1) * HEAD],
                                   B6[:].rearrange("p (t e) -> p t e", t=TC)[:, :, HEAD:P], ACT.Copy).then_inc(swap_copied, 1)
                act.wait_ge(branch_ready, c.next("branch_ready", 2 * LC))
                take_heads(QK, q_head, 0, MLA_HEADS // 2)
                take_heads(QK, q_head, MLA_HEADS // 2, MLA_HEADS)
                pair = iter(range(LC))

                def leave():
                    i = next(pair)
                    act.activation(yb_hi[:, i, :], B7[:], ACT.Copy).then_inc(ah_ready, 1)
                    for chunk in (2 * i, 2 * i + 1):
                        act.activation(a_hi[:, chunk, :], xT[:, chunk, :], ACT.Copy,
                                       scale=col("mix_norm", l, chunk)).then_inc(ah_ready, 1)

                attention(mla_steps(q_head, kv_head, v_head), l, leave)
                for i in c.turns(act, 0, DC // 2, PER_TURN["merge"], "merge"):
                    for j in range(2):
                        chunk = i * 2 + j
                        unit_done()
                        group_read()
                        c.apart(act)
                        for b in range(2):
                            g = act.activation(X[:, b, :], X[:, b, :], ACT.Sigmoid, bias=col("b_g", l, chunk + DC * b))
                        g.then_inc(gate_ready, c.one("gate_ready"))
                        unit_done()
                        group_skipped()
                        act.wait_ge(src_ready, c.next("src_ready"))
                        c.apart(act)
                        act.activation(X[:, 2, :], X[:, 2, :], ACT.Sigmoid,
                                       bias=col("b_g", l, chunk + DC * 2)).then_inc(gate_ready, c.one("gate_ready"))
                        unit_done()
                        group_skipped()
                        act.wait_ge(merged_ready, c.next("merged_ready"))
                        c.apart(act)
                        act.activation(mg_hi[:, bass.ds(chunk, 1), :].rearrange("p o n -> p (o n)"), X[:, 0, :],
                                       ACT.Copy).then_inc(ah_ready, 1)
                for _ in c.turns(act, 0, 2, PER_TURN["w_out"], "w_out"):
                    for j in range(2):
                        unit_done()
                        group_skipped()
                ffn("ffn2_norm", l, False)
            act.wait_ge(x_ready, c.next("x_ready", DC))
            for i in range(DC):
                square(xT[:, i, :])
            for tc in range(TC):
                act.wait_ge(turned, n_param_tiles + DC + 1 + tc)
                act.activation(out_tok[:, tc, 0:SEQ], B4[:], ACT.Copy)
                act.activation(out_tok[:, tc, SEQ:D], B5[:], ACT.Copy).then_inc(tok_copied, 1)

        @block.vector
        def _(dve):
            c = Tally("vector")

            def settled():
                dve.wait_ge(dve_step, c.now("dve_step"))

            def stepped(ins):
                ins.then_inc(dve_step, c.one("dve_step"))

            def split_lo():
                s = c.split % 2
                c.split += 1
                dve.wait_ge(hi_ready, c.next("hi_ready"))
                dve.tensor_tensor(w_lo[:, s, :], raw[:, s, :], w_hi[:, s, :].bitcast(F32), ALU.subtract).then_inc(lo_ready, 1)

            def piece():
                dve.wait_ge(piece_done, c.next("piece_done"))

            def group():
                p = c.group % 2
                c.group += 1
                return p

            def taken(ins, p):
                ins.then_inc(read_out[p], c.one(f"read_out{p}"))

            def scaled(dst, p, r, n=SEQ, blocks=2):
                taken(dve.tensor_tensor(dst, G[p][:, 0:blocks, 0:n], wide(r[:, 0:n], blocks), ALU.mult), p)

            def begin_sum(signal=None):
                zero = dve.memset(X[:, 1, :], 0.0)
                if signal is None:
                    stepped(zero)
                    settled()
                else:
                    zero.then_inc(signal, c.one("x_ready", DC))

            def add_square(n=SEQ, tile=0):
                dve.wait_ge(sq_ready, c.next("sq_ready"))
                dve.tensor_tensor(X[:, 1, 0:n], X[:, 1, 0:n], X[:, tile, 0:n], ALU.add).then_inc(sq_used, c.one("sq_used"))

            def inverse_rms(dst, d, n=SEQ):
                dve.wait_ge(sum_ready, c.next("sum_ready"))
                tiles = n // P
                dve.tensor_scalar(mean_sq[:, 0:tiles], B7[:, 0:tiles], 1.0 / d, EPS, ALU.mult, ALU.add).then_inc(pow_asked, 1)
                dve.wait_ge(pow_done, c.next("pow_done"))
                for i in range(tiles):
                    last = dve.tensor_scalar(X[:, 1, i * P:(i + 1) * P], ident[:], mean_sq[:, i:i + 1], None, ALU.mult)
                last.then_inc(diag_ready, 1)
                dve.wait_ge(sum_ready, c.next("sum_ready"))
                stepped(dve.tensor_copy(dst[:, 0:n], B7[:, 0:n]))
                settled()

            def lows_of_x(i, gain, l):
                dve.wait_ge(ah_ready, c.next("ah_ready"))
                dve.scalar_tensor_tensor(a_lo[:, i, :], xT[:, i, :], col(gain, l, i), a_hi[:, i, :].bitcast(F32),
                                         ALU.mult, ALU.subtract).then_inc(al_ready, c.one("al_ready"))

            def operand(gain, l, lows=True):
                for i in range(DC if lows else 0):
                    lows_of_x(i, gain, l)
                for i in range(DC):
                    dve.wait_ge(sq_used, c.now("sq_used"))
                    add_square(tile=(0, 2, 3)[i % 3])

            def low_of(dst, full, hi, signal):
                dve.wait_ge(ah_ready, c.next("ah_ready"))
                dve.tensor_tensor(dst, full, hi.bitcast(F32), ALU.subtract).then_inc(sems[signal], 1)

            def group_totals(groups, squares):
                chunks = sum(groups, ())
                dve.wait_ge(sq_ready, c.next("sq_ready", len(chunks)))
                c.apart(dve)
                for group in groups:
                    for i in group[1:]:
                        total = dve.tensor_tensor(squares[group[0]], squares[group[0]], squares[i], ALU.add)
                        if i == chunks[-1]:
                            total.then_inc(totals_ready, 1)
                        else:
                            stepped(total)
                            settled()

            def group_roots(groups, squares):
                dve.wait_ge(sum_ready, c.next("sum_ready"))
                for g, group in enumerate(groups):
                    mean = dve.tensor_scalar(mean_sq[:, g * TC:(g + 1) * TC], B7[:, g * TC:(g + 1) * TC],
                                             1.0 / (P * len(group)), EPS, ALU.mult, ALU.add)
                mean.then_inc(pow_asked, 1)
                dve.wait_ge(pow_done, c.next("pow_done"))
                for g, group in enumerate(groups):
                    for i in range(TC):
                        last = dve.tensor_scalar(squares[group[0]][:, i * P:(i + 1) * P], ident[:],
                                                 mean_sq[:, g * TC + i:g * TC + i + 1], None, ALU.mult)
                    last.then_inc(diag_ready, 1)

            def normalised(src, groups, gains, ring, l):
                chunks = sum(groups, ())

                def low(n):
                    low_of(a_lo[:, chunks[n], :], X[:, ring + n % 2, :], a_hi[:, chunks[n], :], "al_ready")
                    c.one("al_ready")

                n = 0
                for bank, group, gain in zip((B4, B5, B6), groups, gains):
                    dve.wait_ge(sum_ready, c.next("sum_ready"))
                    c.apart(dve)
                    for i in group:
                        if n >= 2:
                            dve.wait_ge(al_ready, c.now("al_ready"))
                        dve.scalar_tensor_tensor(X[:, ring + n % 2, :], src[:, i, :], col(gain[0], l, i - gain[1]), bank[:],
                                                 ALU.mult, ALU.mult).then_inc(src_ready, c.one("src_ready"))
                        if n:
                            low(n - 1)
                        n += 1
                low(n - 1)

            def post_norm(y, gain, l, next_gain=None):
                inverse_rms(rs_b, D)

                for i in range(DC + 1):
                    if i < DC:
                        if i >= 2:
                            dve.wait_ge(x_ready, c.now("x_ready"))
                        stepped(dve.scalar_tensor_tensor(X[:, 2 + i % 2, :], y[:, i, :], col(gain, l, i), rs_b[:],
                                                         ALU.mult, ALU.mult))
                    if i:
                        dve.wait_ge(dve_step, c.now("dve_step") - (i < DC))
                        dve.tensor_tensor(xT[:, i - 1, :], xT[:, i - 1, :], X[:, 2 + (i - 1) % 2, :],
                                          ALU.add).then_inc(x_ready, c.one("x_ready"))
                    if next_gain and i >= 3:
                        lows_of_x(i - 3, next_gain, l)
                if next_gain:
                    lows_of_x(DC - 2, next_gain, l)
                    lows_of_x(DC - 1, next_gain, l)
                dve.wait_ge(x_ready, c.now("x_ready"))

            def ffn(gain, l, post, scale, between=None):
                begin_sum(None if post else x_ready)
                operand(gain, l, lows=not post)
                inverse_rms(rs, D)

                def gate_and_up(i, peeled=False):
                    piece()
                    scaled(X[:, 0:2, :], group(), rs)
                    split_lo()
                    piece()
                    p = group()
                    if not peeled:
                        dve.wait_ge(hl_ready, c.now("hl_ready"))
                    scaled(X[:, 2:4, :], p, rs)
                    dve.wait_ge(silu_ready, c.next("silu_ready"))
                    dve.wait_ge(read_out[p], c.now(f"read_out{p}"))
                    dve.tensor_tensor(X[:, 2:4, :], X[:, 2:4, :], X[:, 0:2, :], ALU.mult).then_inc(h_ready, 1)
                    split_lo()
                    dve.wait_ge(hh_ready, c.next("hh_ready"))
                    dve.tensor_tensor(h_lo[:, bass.ds(i * 2, 2), :], X[:, 2:4, :],
                                      h_hi[:, bass.ds(i * 2, 2), :].bitcast(F32), ALU.subtract).then_inc(hl_ready, c.one("hl_ready"))

                gate_and_up(0, peeled=True)
                for i in c.turns(dve, 1, FF // (2 * P), PER_TURN["ffn_in"], "ffn_in"):
                    gate_and_up(i)
                if between:
                    dve.wait_ge(hl_ready, c.now("hl_ready"))
                    between()
                if post:
                    begin_sum()
                for i in c.turns(dve, 0, 2, PER_TURN["ffn_out"], "ffn_out"):
                    for j in range(2):
                        for _ in range(3):
                            piece()
                            split_lo()
                        p = group()
                        if post:
                            c.one(f"read_out{p}")
                            for _ in range(2):
                                add_square()
                        else:
                            x2 = xT[:, bass.ds(i * 4 + 2 * j, 2), :]
                            taken(dve.scalar_tensor_tensor(x2, G[p][:], scale, x2, ALU.mult, ALU.add), p)
                if post:
                    post_norm(y_ffn, post, l)
                else:
                    for p in range(2):
                        dve.wait_ge(read_out[p], c.now(f"read_out{p}"))

            def attention(steps, l, leave=None):
                n = len(steps)
                for s in range(n + 3):
                    if s < n:
                        st = steps[s]
                        biggest = stats[:, 0, s:s + 1]
                        if s >= 3:
                            dve.wait_ge(t_ready, c.next("t_ready"))
                        dve.wait_ge(s_ready, c.next("s_ready"))
                        c.apart(dve)
                        stepped(dve.tensor_tensor_reduce(prob_tiles[s % 3][:, 0:st["n"]], (B4, B5)[s % 2][:, 0:st["n"]],
                                                         st["mask"], 1.0, -3.0e38, ALU.add, ALU.max, biggest))
                    if 1 <= s <= n:
                        total, inverse = stats[:, 1, s - 1:s], stats[:, 2, s - 1:s]
                        dve.wait_ge(e_ready, c.next("e_ready"))
                        if steps[s - 1]["sink"] is not None:
                            stepped(dve.tensor_tensor(total, total, stats[:, 2, s - 1:s], ALU.add))
                            settled()
                        stepped(dve.reciprocal(inverse, total))
                        settled()
                    if s < n:
                        if s == 0:
                            settled()
                        if st["sink"] is None:
                            negated = dve.tensor_scalar(stats[:, 3, s:s + 1], biggest, -st["scale"], None, ALU.mult)
                        else:
                            negated = dve.tensor_scalar(stats[:, 3, s:s + 1], biggest, -st["scale"],
                                                        minus_sinks[:, bass.ds(l * WINDOW_HEADS + st["sink"], 1)],
                                                        ALU.mult, ALU.min)
                        negated.then_inc(m_ready, 1)
                    if 1 <= s <= n:
                        tile = prob_tiles[(s - 1) % 3][:, 0:steps[s - 1]["n"]]
                        dve.tensor_scalar(tile, tile, inverse, None, ALU.mult).then_inc(p_ready, 1)
                    if s >= 3 and steps[s - 3]["closes"] and leave:
                        leave()
                c.one("t_ready", 3)
                dve.wait_ge(t_ready, c.now("t_ready"))
                dve.wait_ge(p_ready, c.next("p_ready", n))

            def rope_tables(column):
                two_pi = 2 * np.pi
                c1_, rest = 6.28125, two_pi - 6.28125
                c2_ = float(np.round(rest * 2 ** 19) / 2 ** 19)
                c3_ = float(np.round((rest - c2_) * 2 ** 30) / 2 ** 30)
                c4_ = float(rest - c2_ - c3_)
                dve.wait_ge(pos_loaded, c.next("pos_loaded", 16))
                stepped(dve.tensor_copy(X[:, 1, :], X[:, 0, :].bitcast(I32)))
                settled()
                stepped(dve.tensor_scalar(X[:, 1, :], X[:, 1, :], freq[:, column:column + 1], None, ALU.mult))
                settled()
                for quarter in (0.0, 0.25):
                    stepped(dve.tensor_scalar(X[:, 2, :], X[:, 1, :], 1.0 / two_pi, quarter, ALU.mult, ALU.add))
                    settled()
                    stepped(dve.tensor_scalar(X[:, 2, :], X[:, 2, :], 1.5 * 2.0 ** 23, None, ALU.add))
                    settled()
                    stepped(dve.tensor_scalar(X[:, 2, :], X[:, 2, :], -1.5 * 2.0 ** 23, None, ALU.add))
                    settled()
                    src = X[:, 1, :]
                    for part in (c1_, c2_, c3_, c4_):
                        stepped(dve.scalar_tensor_tensor(X[:, 3, :], X[:, 2, :], -part, src, ALU.mult, ALU.add))
                        settled()
                        src = X[:, 3, :]
                    if quarter:
                        stepped(dve.tensor_scalar(X[:, 3, :], X[:, 3, :], float(np.pi / 2), None, ALU.add))
                        settled()
                    dve.tensor_scalar(X[:, 3, :], X[:, 3, :], 3.1415925, -3.1415925, ALU.min, ALU.max).then_inc(angle, c.one("angle"))
                    dve.wait_ge(sin_done, c.next("sin_done"))

            def lru_decay():
                lam_at = columns["lambda"][0]
                lam = params[:, lam_at:lam_at + DEPTH * LC]
                v = [tiny[:, i, :] for i in range(6)]
                stepped(dve.tensor_scalar(v[0], lam, -1.0, None, ALU.mult))
                settled()
                dve.tensor_tensor(v[1], v[0], lam, ALU.min).then_inc(soft_in, c.one("soft_in"))
                dve.wait_ge(soft_exp, c.next("soft_exp"))
                stepped(dve.tensor_scalar(v[3], v[2], 2.0, None, ALU.add))
                settled()
                stepped(dve.reciprocal(v[4], v[3]))
                settled()
                stepped(dve.tensor_tensor(v[2], v[2], v[4], ALU.mult))
                settled()
                stepped(dve.tensor_tensor(v[3], v[2], v[2], ALU.mult))
                settled()
                stepped(dve.tensor_scalar(v[4], v[3], 1.0 / 15, 1.0 / 13, ALU.mult, ALU.add))
                settled()
                for odd in (11, 9, 7, 5, 3, 1):
                    stepped(dve.tensor_tensor(v[4], v[4], v[3], ALU.mult))
                    settled()
                    stepped(dve.tensor_scalar(v[4], v[4], 1.0 / odd, None, ALU.add))
                    settled()
                stepped(dve.tensor_tensor(v[4], v[4], v[2], ALU.mult))
                stepped(dve.tensor_scalar(v[5], v[0], 0.0, None, ALU.max))
                settled()
                stepped(dve.scalar_tensor_tensor(v[3], v[4], 2.0, v[5], ALU.mult, ALU.add))
                settled()
                stepped(dve.tensor_scalar(decay[:, 0, :], v[3], -8.0, None, ALU.mult))
                stepped(dve.tensor_scalar(decay[:, 1, :], v[3], -16.0, None, ALU.mult))
                settled()

            def tables():
                rope_tables(1)
                lru_decay()

            dve.wait_ge(pool_step, 2)
            dve.memset(rows[:], 0.0).then_inc(rows_zeroed, 1)
            dve.memset(ones[:], 1.0).then_inc(sq_used, c.one("sq_used"))
            dve.memset(tiny[:, 0, :], 0.0).then_inc(read_out[0], c.one("read_out0"))
            dve.memset(tiny[:, 4, :], 0.0).then_inc(read_out[1], c.one("read_out1"))
            for s in range(2):
                dve.memset(raw[:, s, :], 0.0).then_inc(lo_ready, 1)
            for i in range(DC):
                dve.wait_ge(turned, i + 1)
                dve.tensor_copy(xT[:, i, :], (B4, B5)[i % 2][:]).then_inc(turn_copied, 1)
            dve.wait_ge(consts_loaded, c.next("consts_loaded", 16 * n_setup_loads))
            stepped(dve.tensor_scalar(minus_sinks[:], sinks[:], -1.0, None, ALU.mult))
            rope_tables(0)
            split_lo()
            split_lo()
            for i in range(DC, DC + n_param_tiles):
                dve.wait_ge(turned, i + 1)
                dve.tensor_copy(params[:, (i - DC) * P:(i - DC + 1) * P], (B4, B5)[i % 2][:, 0:P]).then_inc(turn_copied, 1)
            dve.wait_ge(turn_copied, DC + n_param_tiles)
            dve.memset(tiny[:, 1, :], 0.0).then_inc(x_ready, c.one("x_ready", DC))
            for l in c.layers(dve, PER_LAYER["one"], "one"):
                begin_sum()
                operand("g_pre_mix", l)
                inverse_rms(rs, D)
                piece()
                scaled(zfT[:], group(), rs)
                split_lo()
                begin_sum()
                for i in range(DC):
                    dve.wait_ge(ah_ready, c.next("ah_ready"))
                    dve.scalar_tensor_tensor(m_lo[:, i, :], memT[:, i, :], col("g_mem", l, i), m_hi[:, i, :].bitcast(F32),
                                             ALU.mult, ALU.subtract).then_inc(al_ready, c.one("al_ready"))
                    add_square(MEM)
                for dst, blocks in ((qT[:, 0:2, :], 2), (qT[:, 2:4, :], 2), (zkT[:].unsqueeze(1), 1),
                                    (vT[:].unsqueeze(1), 1), (zmT[:], 2)):
                    piece()
                    scaled(dst, group(), rs, blocks=blocks)
                    split_lo()
                inverse_rms(rs_b, D, MEM)
                for dst in (kmT, vmT):
                    piece()
                    scaled(dst[:], group(), rs_b, n=MEM)
                    split_lo()
                for p in range(2):
                    dve.wait_ge(read_out[p], c.now(f"read_out{p}"))
                for i in range(4):
                    if i:
                        dve.wait_ge(rope_ready, c.now("rope_ready"))
                    dve.wait_ge(rot_ready, c.next("rot_ready"))
                    dve.tensor_tensor(X[:, 2, :], (B4, B5)[i % 2][:], sinT[:], ALU.mult).then_inc(rot_used, c.one("rot_used"))
                    stepped(dve.tensor_tensor(qT[:, i, :], qT[:, i, :], cosT[:], ALU.mult))
                    dve.wait_ge(rot_used, c.now("rot_used"))
                    settled()
                    dve.tensor_tensor(qT[:, i, :], qT[:, i, :], X[:, 2, :], ALU.add).then_inc(rope_ready, c.one("rope_ready"))
                for j in range(2):
                    dve.wait_ge(rope_ready, c.now("rope_ready"))
                    dve.wait_ge(rot_ready, c.next("rot_ready", 2))
                    dve.tensor_tensor(kT[:, j, :], B4[:], cosT[:], ALU.mult).then_inc(rot_used, c.one("rot_used"))
                    dve.tensor_tensor(X[:, 2, :], B5[:], sinT[:], ALU.mult).then_inc(rot_used, c.one("rot_used"))
                    dve.wait_ge(rot_used, c.now("rot_used"))
                    dve.tensor_tensor(kT[:, j, :], kT[:, j, :], X[:, 2, :], ALU.add).then_inc(rope_ready, c.one("rope_ready"))
                attention(window_steps(qT, kT, v_tok), l)
                attention(memory_steps(zmT, kmT, vm_tok), l)
                group_totals(GROUPS, mix_squares)
                group_roots(GROUPS, mix_squares)
                normalised(y_mix, GROUPS, [("g_grp", 0)] * 3, 2, l)
                begin_sum()
                for j in range(4):
                    piece()
                    p = group()
                    c.one(f"read_out{p}")
                    split_lo()
                    for _ in range(2):
                        add_square()
                post_norm(y_mix, "g_post_mix", l, next_gain="g_pre_ffn")
                ffn("g_pre_ffn", l, "g_post_ffn", None)

            for l in c.layers(dve, PER_LAYER["two"], "two"):
                ffn("ffn1_norm", l, None, 0.5, between=tables)
                stepped(dve.memset(glu[:, :, 0:CONV_TAPS - 1], 0.0))
                dve.memset(xpad[:, :, 0:LRU_TAPS - 1], 0.0).then_inc(region_free, 1)
                begin_sum(x_ready)
                operand("mix_norm", l)
                inverse_rms(rs, D)
                settled()

                def conv_taps(first, end):
                    at, per = columns["dw_w"]
                    for n in range(first, end):
                        i, k = n // CONV_TAPS, n % CONV_TAPS
                        w = params[:, bass.ds(l * per + (at + k * LC + i), 1)]
                        src, total = glu[:, i, k:k + SEQ], (conv[:, i, :], X[:, 0, :])[k % 2]
                        if k == 0:
                            stepped(dve.tensor_scalar(total, src, w, col("dw_b", l, i), ALU.mult, ALU.add))
                        elif k == 1:
                            settled()
                            stepped(dve.tensor_scalar(total, src, w, None, ALU.mult))
                        else:
                            dve.wait_ge(dve_step, c.now("dve_step") - 1)
                            stepped(dve.scalar_tensor_tensor(total, src, w, total, ALU.mult, ALU.add))
                        if k == CONV_TAPS - 1:
                            settled()
                            both = dve.tensor_tensor(conv[:, i, :], conv[:, i, :], X[:, 0, :], ALU.add)
                            if i < LC - 1:
                                stepped(both)
                            else:
                                both.then_inc(conv_done, c.one("conv_done"))

                def short_conv(i):
                    at, per = columns["conv4_w"]
                    for k in range(LRU_TAPS):
                        w = params[:, bass.ds(l * per + (at + k * LC + i), 1)]
                        src = xpad[:, i, k:k + SEQ]
                        if k == 0:
                            stepped(dve.tensor_scalar(xa[:, i, :], src, w, col("conv4_b", l, i), ALU.mult, ALU.add))
                        else:
                            settled()
                            tap = dve.scalar_tensor_tensor(xa[:, i, :], src, w, xa[:, i, :], ALU.mult, ALU.add)
                            if k < LRU_TAPS - 1:
                                stepped(tap)
                            else:
                                tap.then_inc(xa_ready, c.one("xa_ready"))

                def lru_root(i):
                    dve.wait_ge(e2_ready, c.next("e2_ready"))
                    stepped(dve.tensor_tensor(xa[:, i, :], sig[:, i, 1, :], xa[:, i, :], ALU.mult))
                    settled()
                    dve.scalar_tensor_tensor(sig[:, i, 1, :], lru_square[i % 2], 1.0, lru_tanh[i % 2],
                                             ALU.add, ALU.mult).then_inc(root_asked, 1)

                def skip_pieces(n):
                    for _ in range(n):
                        piece()
                        c.one(f"read_out{group()}")
                    split_lo()

                taps = 0
                for j in range(LC):
                    piece()
                    scaled(X[:, 2:4, :], group(), rs)
                    split_lo()
                    if j:
                        conv_taps(taps, taps + 11)
                        taps += 11
                    dve.wait_ge(bias_done, c.next("bias_done"))
                    stepped(dve.scalar_tensor_tensor(glu[:, j, CONV_TAPS - 1:], X[:, 2, :], col("b_c", l, j), X[:, 3, :],
                                                     ALU.add, ALU.mult))
                    settled()
                for j in range(4):
                    piece()
                    scaled(X[:, 2:4, :], group(), rs)
                    split_lo()
                    conv_taps(taps, taps + 12)
                    taps += 12
                    dve.wait_ge(bias_done, c.next("bias_done", 2))
                    if j < 2:
                        short_conv(2 * j)
                        short_conv(2 * j + 1)
                for j in range(4):
                    piece()
                    p = group()
                    if j < 2:
                        scaled(X[:, 2:4, :], p, rs)
                    elif j == 2:
                        scaled(X[:, 2:3, :], p, rs, blocks=1)
                    else:
                        taken(dve.tensor_tensor(X[0:QK, 2, :], G[p][0:QK, 0, :], rs[0:QK, :], ALU.mult), p)
                    if j != 2:
                        split_lo()
                    conv_taps(taps, taps + 8)
                    taps += 8
                    dve.wait_ge(bias_done, c.next("bias_done", 2 if j < 2 else 1))
                    if j:
                        lru_root(j - 1)
                group_totals(RANKS, rank_squares)
                conv_taps(taps, LC * CONV_TAPS)
                lru_root(3)
                dve.wait_ge(conv_done, c.now("conv_done"))
                group_roots(RANKS, rank_squares)
                normalised(craw, RANKS, [("q_norm", 0), ("kv_norm", 3)], 1, l)
                dve.wait_ge(mean_ready, c.next("mean_ready"))
                stepped(dve.tensor_scalar(X[:, 3, :], B6[:], 1.0 / LRU, None, ALU.mult))
                settled()
                dve.tensor_tensor(conv[:], conv[:], wide(X[:, 3, :], LC), ALU.subtract).then_inc(centred, c.one("centred"))
                for i in range(LC):
                    dve.wait_ge(root_done, c.next("root_done"))
                    stepped(dve.tensor_tensor(xa[:, i, :], xa[:, i, :], sig[:, i, 1, :], ALU.mult))
                    settled()
                    if i:
                        dve.wait_ge(v_ready, c.now("v_ready"))
                    else:
                        dve.wait_ge(centred, c.now("centred"))
                    stepped(dve.tensor_tensor_scan(X[:, 3, :], sig[:, i, 0, :], xa[:, i, :], 0.0, ALU.mult, ALU.add))
                    settled()
                    dve.tensor_tensor(gelu[:, i, :], gelu[:, i, :], X[:, 3, :], ALU.mult).then_inc(v_ready, c.one("v_ready"))
                group_totals((tuple(range(LC)),), conv_squares)
                dve.wait_ge(v_ready, c.now("v_ready"))
                for i in range(LC):
                    low_of(ya_lo[:, i, :], gelu[:, i, :], ya_hi[:, i, :], "branch_ready")
                skip_pieces(4)
                group_roots((tuple(range(LC)),), conv_squares)
                dve.wait_ge(sum_ready, c.next("sum_ready"))
                c.apart(dve)
                for i in range(LC):
                    dve.tensor_tensor(conv[:, i, :], conv[:, i, :], B4[:], ALU.mult).then_inc(ln_ready, c.one("ln_ready"))
                for i in range(LC):
                    low_of(yc_lo[:, i, :], conv[:, i, :], yc_hi[:, i, :], "branch_ready")
                turn = slice(HEAD, QK)
                dve.wait_ge(rot_ready, c.next("rot_ready"))
                stepped(dve.tensor_tensor(X[turn, 2, :], B5[turn, :], sinT[turn, :], ALU.mult))
                stepped(dve.tensor_tensor(craw[turn, 5, :], craw[turn, 5, :], cosT[turn, :], ALU.mult))
                settled()
                dve.tensor_tensor(craw[turn, 5, :], craw[turn, 5, :], X[turn, 2, :], ALU.add).then_inc(rot_used, c.one("rot_used"))
                dve.wait_ge(rot_used, c.now("rot_used"))
                dve.wait_ge(swap_copied, c.next("swap_copied", MLA_HEADS))
                for h in range(MLA_HEADS):
                    dve.tensor_copy(kv_head[turn, h, :], craw[turn, 5, :]).then_inc(rope_ready, c.one("rope_ready"))
                skip_pieces(2)
                skip_pieces(2)
                for h in range(MLA_HEADS):
                    if h:
                        dve.wait_ge(rope_ready, c.now("rope_ready"))
                    dve.wait_ge(rot_ready, c.next("rot_ready"))
                    dve.tensor_tensor(X[turn, 2, :], (B4, B5)[h % 2][turn, :], sinT[turn, :], ALU.mult).then_inc(rot_used, c.one("rot_used"))
                    stepped(dve.tensor_tensor(q_head[turn, h, :], q_head[turn, h, :], cosT[turn, :], ALU.mult))
                    dve.wait_ge(rot_used, c.now("rot_used"))
                    settled()
                    dve.tensor_tensor(q_head[turn, h, :], q_head[turn, h, :], X[turn, 2, :], ALU.add).then_inc(rope_ready, c.one("rope_ready"))
                dve.wait_ge(rope_ready, c.now("rope_ready"))
                pair = iter(range(LC))

                def leave():
                    i = next(pair)
                    low_of(yb_lo[:, i, :], B7[:], yb_hi[:, i, :], "o_used")
                    for chunk in (2 * i, 2 * i + 1):
                        lows_of_x(chunk, "mix_norm", l)

                attention(mla_steps(q_head, kv_head, v_head), l, leave)
                for i in c.turns(dve, 0, DC // 2, PER_TURN["merge"], "merge"):
                    for j in range(2):
                        chunk = i * 2 + j
                        piece()
                        dve.wait_ge(hl_ready, c.now("hl_ready"))
                        scaled(X[:, 0:2, :], group(), rs)
                        split_lo()
                        piece()
                        p = group()
                        dve.tensor_tensor(X[:, 2, :], G[p][:, 0, :], rs[:], ALU.mult).then_inc(src_ready, c.one("src_ready"))
                        dve.wait_ge(gate_ready, c.next("gate_ready"))
                        taken(dve.tensor_tensor(X[:, 0, :], X[:, 0, :], G[p][:, 1, :], ALU.mult), p)
                        split_lo()
                        piece()
                        q = group()
                        stepped(dve.tensor_tensor(X[:, 1, :], X[:, 1, :], G[q][:, 0, :], ALU.mult))
                        dve.wait_ge(gate_ready, c.next("gate_ready"))
                        taken(dve.scalar_tensor_tensor(X[:, 2, :], G[q][:, 1, :], col("conv_b_out", l, chunk), X[:, 2, :],
                                                       ALU.add, ALU.mult), q)
                        settled()
                        stepped(dve.tensor_tensor(X[:, 0, :], X[:, 0, :], X[:, 1, :], ALU.add))
                        settled()
                        dve.wait_ge(read_out[q], c.now(f"read_out{q}"))
                        dve.tensor_tensor(X[:, 0, :], X[:, 0, :], X[:, 2, :], ALU.add).then_inc(merged_ready, c.one("merged_ready"))
                        split_lo()
                        low_of(mg_lo[:, bass.ds(chunk, 1), :].rearrange("p o n -> p (o n)"), X[:, 0, :],
                               mg_hi[:, bass.ds(chunk, 1), :].rearrange("p o n -> p (o n)"), "hl_ready")
                        c.one("hl_ready")
                for i in c.turns(dve, 0, 2, PER_TURN["w_out"], "w_out"):
                    for j in range(2):
                        piece()
                        p = group()
                        x2 = xT[:, bass.ds(i * 4 + 2 * j, 2), :]
                        taken(dve.tensor_tensor(x2, x2, G[p][:], ALU.add), p)
                        split_lo()
                for p in range(2):
                    dve.wait_ge(read_out[p], c.now(f"read_out{p}"))
                ffn("ffn2_norm", l, None, 0.5)
            begin_sum(x_ready)
            for _ in range(DC):
                add_square()
            inverse_rms(rs, D)
            first = columns["final_norm"][0]
            for i in range(DC):
                last = dve.scalar_tensor_tensor(xT[:, i, :], xT[:, i, :], params[:, first + i:first + i + 1], rs[:],
                                                ALU.mult, ALU.mult)
            last.then_inc(final_ready, 1)

        @block.gpsimd
        def _(pool):
            c = Tally("gpsimd")

            def inverse_roots(n):
                for _ in range(n):
                    pool.wait_ge(pow_asked, c.next("pow_asked"))
                    pool.tensor_tensor(mean_sq[:], mean_sq[:], minus_half[:], ALU.pow).then_inc(pow_done, 1)

            pool.memset(minus_half[:], -0.5).then_inc(pool_step, 1)
            pool.memset(mean_sq[:], 1.0).then_inc(pool_step, 1)
            pool.wait_ge(pool_step, 2)
            pool.wait_ge(x_loaded, 16)
            for l in c.layers(pool, PER_LAYER["one"], "one"):
                pool.wait_ge(x_ready, c.next("x_ready", DC))
                c.apart(pool)
                pool.dma_start(mem_tok[:], t["mem"].rearrange("o (t p) d -> p (o t) d", p=P)).then_inc(mem_loaded, 16)
                inverse_roots(1)
                for name, tile in c1.items():
                    at, n = CONSTS[name]
                    pool.dma_start(tile[:], t["consts"][:, at:at + n]).then_inc(c1_loaded, 16)
                pool.memset(wf[:], 0.0).then_inc(wf_zeroed, 1)
                pool.wait_ge(wf_zeroed, c.next("wf_zeroed"))
                c.apart(pool)
                for half in range(2):
                    pool.dma_start(wf[half * HEAD:(half + 1) * HEAD, :, half * HEAD:(half + 1) * HEAD],
                                   t["w_fourier"][bass.ds(l, 1), half::2].rearrange("o j c e -> c (o j) e")).then_inc(wf_loaded, 16)
                inverse_roots(1)
                pool.wait_ge(piece_done, c.next("piece_done", 6))
                c.apart(pool)
                pool.dma_start(dft[:], t["dft"].rearrange("(t p) i n -> p t i n", p=P)).then_inc(dft_loaded, 16)
                c.one("piece_done", PER_LAYER["one"].get("piece_done", 6) - 6)
                c.one("x_ready", DC)
                inverse_roots(4)
            for l in c.layers(pool, PER_LAYER["two"], "two"):
                inverse_roots(1)
                pool.wait_ge(region_free, c.next("region_free"))
                c.apart(pool)
                pool.memset(gate_w[:], 0.0).then_inc(gate_zeroed, 1)
                pool.wait_ge(gate_zeroed, c.next("gate_zeroed"))
                c.apart(pool)
                for half in range(2):
                    for i in range(2):
                        pool.dma_start(
                            gate_w[half * HEAD:(half + 1) * HEAD, :, i, half * HEAD:(half + 1) * HEAD],
                            t["lru_w_gate_2"][bass.ds(l, 1), half::2, :, i * HEAD:(i + 1) * HEAD].rearrange("o j c e -> c (o j) e"),
                        ).then_inc(gate_loaded, 16)
                inverse_roots(4)
            inverse_roots(1)

    if Tally.wrong:
        raise ValueError(sorted({w[:3] for w in Tally.wrong}))


def row_copies(t, rows, columns):
    whole = {"g_pre_mix": "g_pre_mix", "g_mem": "g_mem", "g_grp": "g_grp", "g_post_mix": "g_post_mix",
             "g_pre_ffn": "g_pre_ffn", "g_post_ffn": "g_post_ffn", "ffn1_norm": "ffn1_norm_2",
             "mix_norm": "mix_norm_2", "conv4_b": "lru_conv_b_2", "lambda": "lru_lambda_2", "q_norm": "q_norm_2",
             "kv_norm": "kv_norm_2", "dw_b": "conv_dw_b_2", "ln_g": "conv_ln_g_2", "ln_b": "conv_ln_b_2",
             "conv_b_out": "conv_b_out_2", "ffn2_norm": "ffn2_norm_2"}
    biases = {"b_a": 0, "b_b": IN_B, "b_c": IN_C, "b_g": IN_G}
    counts = dict(PARAM_ROWS, dw_w=CONV_TAPS * LC)
    out = []
    for name, n in counts.items():
        first, step = columns[name]
        if name != "dw_w":
            dst = rows[first % P:first % P + DEPTH * n, first // P, :]
        if name in whole:
            out.append((dst, t[whole[name]].rearrange("l (c p) -> (l c) p", p=P)))
            continue
        if name == "conv4_w":
            out.append((dst, t["lru_conv_w_2"].rearrange("l k (c p) -> (l k c) p", p=P)))
            continue
        if name == "final_norm":
            out.append((dst, t["final_norm_2"].rearrange("(c p) -> c p", p=P)))
            continue
        for l in range(DEPTH):
            at = first + l * step
            dst = rows[at % P:at % P + n, at // P, :]
            if name in biases:
                src = t["b_in_2"][l, biases[name]:biases[name] + n * P].rearrange("(c p) -> c p", p=P)
            elif name == "b_kpe":
                dst = dst[:, 0:QK]
                src = t["b_in_2"][l:l + 1, IN_C - QK:IN_C]
            elif name in ("b_r", "b_i"):
                half = HEAD * (name == "b_i")
                dst = dst.rearrange("c (t e) -> c t e", t=2)
                src = t["lru_b_gate_2"][l, :, half:half + HEAD].rearrange("(c t) e -> c t e", t=2)
            else:
                assert name == "dw_w"
                src = t["conv_dw_w_2"][l].rearrange("k (c p) -> (k c) p", p=P)
            out.append((dst, src))
    return out


_INS = ["x", "mem", "positions", "w_in", "w_fourier", "w_mem_kv", "w_out", "w_ffn_in", "w_ffn_out", "sink",
        "g_pre_mix", "g_mem", "g_grp", "g_post_mix", "g_pre_ffn", "g_post_ffn",
        "positions_2", "ffn1_norm_2", "ffn1_w1_2", "ffn1_w2_2", "mix_norm_2", "w_in_2", "b_in_2", "lru_conv_w_2",
        "lru_conv_b_2", "lru_w_gate_2", "lru_b_gate_2", "lru_lambda_2", "lru_w_out_2", "q_norm_2", "w_uq_2",
        "kv_norm_2", "w_ukv_2", "mla_w_o_2", "conv_dw_w_2", "conv_dw_b_2", "conv_ln_g_2", "conv_ln_b_2",
        "conv_w_out_2", "conv_b_out_2", "w_out_2", "ffn2_norm_2", "ffn2_w1_2", "ffn2_w2_2", "final_norm_2"]


def kernel(**inputs):
    import concourse.bacc as _bacc
    from concourse.bass_utils import run_bass_kernel_spmd as _run

    nc = _bacc.Bacc("TRN2", target_bir_lowering=False, num_devices=1)
    arrays, t = {}, {}
    for name in _INS:
        arrays[f"in_{name}"] = np.ascontiguousarray(inputs[name])
    arrays["in_consts"] = constants()
    arrays["in_dft"] = sequence_dft()
    for name, a in arrays.items():
        t[name[3:]] = nc.dram_tensor(name, a.shape, mybir.dt.from_np(a.dtype), kind="ExternalInput").ap()
    out = nc.dram_tensor("out_x", (1, SEQ, D), F32, kind="ExternalOutput").ap()
    two_blocks(nc, t, out)
    r = _run(nc, [arrays], core_ids=[0])
    return r.results[0]["out_x"]
```

```python
from contextlib import ExitStack

import numpy as np

import concourse.bass as bass
from concourse import mybir

F32 = mybir.dt.float32
F32R = mybir.dt.float32r
I32 = mybir.dt.int32
ALU = mybir.AluOpType
ACT = mybir.ActivationFunctionType

P = 128
DEPTH = 2
SEQ = 512
D = 1024
DC = D // P
TC = SEQ // P
MEM = 256
FF = 2816
FC = FF // P
HEAD = 64
WINDOW_HEADS = 8
MEM_HEADS = 4
IN_1 = 1280
LRU = 512
LC = LRU // P
Q_RANK = 384
KV_RANK = 256
MLA_HEADS = 8
QK = 96
PE_DIM = 32
CONV_TAPS = 31
LRU_TAPS = 4
IN_B = 1024
IN_C = IN_B + Q_RANK + KV_RANK + PE_DIM
IN_G = IN_C + 1024
D_IN = IN_G + 3 * D
EPS = 1e-6
MASKED = -1e30
UNIT = 16 * P

PARAM_ROWS = [
    ("g_pre_mix", 8), ("g_mem", 8), ("g_grp", 8), ("g_post_mix", 8), ("g_pre_ffn", 8),
    ("g_post_ffn", 8), ("ffn1_norm", 8), ("mix_norm", 8), ("b_a", 8), ("b_b", 5), ("b_kpe", 1),
    ("b_c", 8), ("b_g", 24), ("conv4_w", 16), ("conv4_b", 4), ("b_r", 4), ("b_i", 4),
    ("lambda", 4), ("q_norm", 3), ("kv_norm", 2), ("dw_b", 4), ("ln_g", 4),
    ("ln_b", 4), ("conv_b_out", 8), ("ffn2_norm", 8),
    ("final_norm", DC // DEPTH),
]


def param_columns():
    at, columns = 0, {}
    for name, rows in PARAM_ROWS:
        if at // P != (at + DEPTH * rows - 1) // P:
            at = -(-at // P) * P
        columns[name] = (at, rows)
        at += DEPTH * rows
    at = -(-at // P) * P
    columns["dw_w"] = (at, P)
    return columns, at // P + DEPTH


def rope_frequencies():
    half1 = HEAD // 2
    f1 = np.exp(np.float32(-np.log(10000.0)) * np.arange(half1, dtype=np.float32) * np.float32(2.0 / HEAD))
    f2 = np.float32(10000.0) ** (-np.arange(0, PE_DIM, 2, dtype=np.float32) / np.float32(PE_DIM))
    out = np.zeros((P, 2), np.float32)
    out[:, 0] = np.tile(f1.astype(np.float32), P // half1)
    out[HEAD:HEAD + PE_DIM, 1] = np.tile(f2.astype(np.float32), 2)
    return out


def rotate_half(n, half):
    m = np.zeros((n, n), np.float32)
    for r in range(n):
        base, j = r - r % (2 * half), r % (2 * half)
        if j < half:
            m[base + j + half, r] = -1.0
        else:
            m[base + j - half, r] = 1.0
    return m


CONSTS = {}


def constants():
    parts = []

    def add(name, a):
        wide = np.zeros((P, a.shape[1]), np.float32)
        wide[:a.shape[0]] = a
        CONSTS[name] = (sum(p.shape[1] for p in parts), a.shape[1])
        parts.append(wide)

    i = np.arange(P)
    add("ident", np.eye(P, dtype=np.float32))
    causal = np.where(i[None, :] <= i[:, None], 0.0, MASKED)
    add("causal", np.concatenate([np.zeros((P, 3 * P)), causal], axis=1))
    r96 = np.zeros((P, QK), np.float32)
    r96[HEAD:QK, HEAD:QK] = rotate_half(PE_DIM, PE_DIM // 2)
    add("rot96", r96)
    add("freq", rope_frequencies())
    before = np.where(i[None, :] >= i[:, None], 0.0, MASKED)
    add("window", np.concatenate([before, np.zeros((P, P)), causal], axis=1))
    rot = rotate_half(P, HEAD // 2)
    add("rot_q", rot)
    for j in range(2):
        dup = np.zeros((P, P), np.float32)
        dup[HEAD * j + i % HEAD, i] = 1.0
        add(f"dup{j}", dup)
        add(f"rot_k{j}", dup @ rot)
    n = np.arange(HEAD)
    ang = 2 * np.pi * ((n[:, None] * n[None, :]) % HEAD) / HEAD
    for name, m in (("dft_cos", np.cos(ang) / 8.0), ("dft_sin", -np.sin(ang) / 8.0)):
        add(name, np.kron(np.eye(2), m).astype(np.float32))
    return np.ascontiguousarray(np.concatenate(parts, axis=1).astype(np.float32))


def sequence_dft():
    n = np.arange(SEQ)
    ang = 2 * np.pi * ((n[:, None] * n[None, :]) % SEQ) / SEQ
    return np.ascontiguousarray(
        (np.stack([np.cos(ang), np.sin(ang)], axis=1) / np.sqrt(SEQ)).astype(np.float32))


class Tally:

    wrong = []
    carrier = None

    def __init__(self, eng_name):
        self.eng_name = eng_name
        self.before, self.n = {}, {}
        self.layer = self.turn = None
        self.per_layer, self.per_turn = {}, {}
        self.unit = self.split = self.group = 0

    def apart(self, eng):
        eng.sem_inc(self.carrier, 1)

    def one(self, name, by=1):
        self.n[name] = self.n.get(name, 0) + by
        return by

    def now(self, name):
        value = self.before.get(name, 0) + self.n.get(name, 0)
        if self.layer is not None and self.per_layer.get(name, 0):
            value = self.layer * self.per_layer[name] + value
        if self.turn is not None and self.per_turn.get(name, 0):
            value = self.turn * self.per_turn[name] + value
        return value

    def next(self, name, by=1):
        self.one(name, by)
        return self.now(name)

    def layers(self, eng, per_layer, label):
        self.apart(eng)
        with eng.Fori(0, DEPTH) as layer:
            for name, n in self.n.items():
                self.before[name] = self.before.get(name, 0) + n
            self.layer, self.n, self.per_layer = layer, {}, per_layer
            yield layer
            for name, n in self.n.items():
                if n and n != per_layer.get(name, 0):
                    self.wrong.append((label, name, n, self.eng_name))
            for name, n in per_layer.items():
                self.before[name] = self.before.get(name, 0) + DEPTH * n
            self.layer, self.n = None, {}

    def turns(self, eng, first, end, per_turn, label):
        start = dict(self.n)
        self.apart(eng)
        with eng.Fori(first, end) as turn:
            self.per_turn = per_turn
            self.turn = turn
            for name, n in per_turn.items():
                self.n[name] = self.n.get(name, 0) - first * n
            shifted = dict(self.n)
            yield turn
            for name in set(self.n):
                made = self.n[name] - shifted.get(name, 0)
                if name in per_turn and made == 0:
                    self.n[name] = start.get(name, 0)
                    continue
                if made != per_turn.get(name, 0):
                    self.wrong.append((label, name, made, self.eng_name))
                self.n[name] = start.get(name, 0) + (end - first) * made
            self.turn = None


GROUPS = ((0, 1), (2, 3, 4, 5), (6, 7))
RANKS = ((3, 4), (0, 1, 2))

PER_LAYER = {
    "one": {"ah_ready": 32, "al_ready": 32, "c1_loaded": 128, "dft_loaded": 16, "diag_ready": 8,
        "dve_step": 162, "e_ready": 48, "four_copied": 7, "four_ready": 7, "h_ready": 11, "hh_ready": 11,
        "hi_ready": 46, "hl_ready": 11, "lo_ready": 46, "m_ready": 48, "mem_loaded": 16, "o_ready": 6,
        "o_used": 6, "p_ready": 48, "piece_done": 46, "pow_asked": 6, "pow_done": 6, "pt_ready": 48,
        "raw_loaded0": 736, "raw_loaded1": 736, "read_out0": 19, "read_out1": 19, "rope_ready": 6,
        "rot_ready": 8, "rot_used": 8, "s_ready": 48, "silu_ready": 11, "sq_ready": 48, "sq_used": 40,
        "src_ready": 8, "sum_ready": 14, "swap_copied": 6, "swap_ready": 6, "t_ready": 48,
        "totals_ready": 1, "wf_loaded": 32, "wf_zeroed": 1, "x_ready": 16},
    "two": {"act_step": 4, "ah_ready": 57, "al_ready": 37, "angle": 2, "bias_done": 18, "branch_ready": 8,
        "centred": 1, "conv_done": 1, "diag_ready": 6, "dve_step": 291, "e2_ready": 4, "e_ready": 32,
        "gate_loaded": 64, "gate_ready": 16, "gate_zeroed": 1, "gates_ready": 8, "h_ready": 22,
        "hh_ready": 22, "hi_ready": 110, "hl_ready": 30, "ln_ready": 4, "lo_ready": 110, "m_ready": 32,
        "mean_ready": 1, "merged_ready": 8, "o_ready": 4, "o_used": 4, "p_ready": 32, "piece_done": 116,
        "pos_loaded": 16, "pow_asked": 5, "pow_done": 5, "pt_ready": 32, "raw_loaded0": 1760,
        "raw_loaded1": 1760, "read_out0": 50, "read_out1": 50, "region_free": 1, "root_asked": 4,
        "root_done": 4, "rope_ready": 16, "rot_ready": 9, "rot_used": 9, "s_ready": 32, "sig_ready": 8,
        "silu_ready": 22, "sin_done": 2, "soft_exp": 1, "soft_in": 1, "sq_ready": 33, "sq_used": 24,
        "src_ready": 13, "sum_ready": 11, "swap_copied": 8, "swap_ready": 8, "t_ready": 32,
        "totals_ready": 2, "v_ready": 4, "x_ready": 8, "xa_ready": 4},
}
PER_TURN = {
    "ffn_in": {"h_ready": 1, "hh_ready": 1, "hi_ready": 2, "hl_ready": 1, "lo_ready": 2, "piece_done": 2,
        "raw_loaded0": 32, "raw_loaded1": 32, "read_out0": 1, "read_out1": 1, "silu_ready": 1},
    "ffn_out": {"hi_ready": 6, "lo_ready": 6, "piece_done": 6, "raw_loaded0": 96, "raw_loaded1": 96,
        "read_out0": 1, "read_out1": 1, "sq_ready": 4, "sq_used": 4},
    "w_out": {"hi_ready": 2, "lo_ready": 2, "piece_done": 2, "raw_loaded0": 32, "raw_loaded1": 32,
        "read_out0": 1, "read_out1": 1},
    "merge": {"ah_ready": 2, "dve_step": 4, "gate_ready": 4, "hi_ready": 6, "hl_ready": 2, "lo_ready": 6,
        "merged_ready": 2, "piece_done": 6, "raw_loaded0": 96, "raw_loaded1": 96, "read_out0": 3,
        "read_out1": 3, "src_ready": 2},
}


def two_blocks(nc, t, out):
    columns, n_param_tiles = param_columns()

    base = -(-nc.sbuf_base // 64) * 64
    top = [base]

    def place(name, shape, dt=F32, at=None):
        size = 4 * int(np.prod(shape[1:]))
        offset = top[0] if at is None else at
        if at is None:
            top[0] += -(-size // 32) * 32
        return nc.alloc_sbuf_tensor_at(name, shape, dt, offset=offset)

    KB = 1024
    xT = place("xT", [P, DC, SEQ])
    raw = place("raw", [P, 2, UNIT])
    w_hi = place("w_hi", [P, 2, UNIT], F32R)
    w_lo = place("w_lo", [P, 2, UNIT], F32R)
    ident = place("ident", [P, P])
    ones = place("ones", [P, P])
    rot96 = place("rot96", [P, QK])
    causal = place("causal", [P, SEQ])
    freq = place("freq", [P, 2])
    params = place("params", [P, n_param_tiles * P])
    stats = place("stats", [P, 4, 32])
    sinks = place("sinks", [P, DEPTH * WINDOW_HEADS])
    minus_sinks = place("minus_sinks", [P, DEPTH * WINDOW_HEADS])
    decay = place("decay", [P, 2, DEPTH * LC])
    tiny = place("tiny", [P, 6, DEPTH * LC])
    mean_sq = place("mean_sq", [P, len(GROUPS) * TC])
    minus_half = place("minus_half", [P, len(GROUPS) * TC])
    rs = place("rs", [P, SEQ])
    rs_b = place("rs_b", [P, SEQ])
    cosT = place("cosT", [P, SEQ])
    sinT = place("sinT", [P, SEQ])
    X = place("X", [P, 4, SEQ])
    REGION_A = top[0]
    a_hi = place("a_hi", [P, DC, SEQ], F32R)
    a_lo = place("a_lo", [P, DC, SEQ], F32R)
    y_ffn = place("y_ffn", [P, DC, SEQ], at=REGION_A)
    dft = place("dft", [P, TC, 2, SEQ], at=REGION_A)
    ab = place("ab", [P, TC, SEQ], at=REGION_A + 16 * KB)
    rows = place("rows", [P, n_param_tiles, P], at=REGION_A)
    out_tok = place("out_tok", [P, TC, D], at=REGION_A)
    REGION_B = top[0]
    h_hi = place("h_hi", [P, FC, SEQ], F32R)
    h_lo = place("h_lo", [P, FC, SEQ], F32R)
    x_tok = place("x_tok", [P, TC, D], at=REGION_B)
    b1 = [REGION_B]

    def in_b(name, shape, dt=F32):
        at = b1[0]
        b1[0] += 4 * int(np.prod(shape[1:]))
        assert b1[0] <= top[0]
        return place(name, shape, dt, at=at)

    mem_tok = place("mem_tok", [P, MEM // P, D], at=REGION_B)
    memT = place("memT", [P, DC, MEM], at=REGION_B + 8 * KB)
    y_mix = in_b("y_mix", [P, DC, SEQ])
    zfT = in_b("zfT", [P, 2, SEQ])
    qT = in_b("qT", [P, 4, SEQ])
    zkT = in_b("zkT", [P, SEQ])
    kT = in_b("kT", [P, 2, SEQ])
    vT = in_b("vT", [P, SEQ])
    v_tok = in_b("v_tok", [P, TC, P])
    zmT = in_b("zmT", [P, 2, SEQ])
    kmT = in_b("kmT", [P, 2, MEM])
    vmT = in_b("vmT", [P, 2, MEM])
    vm_tok = in_b("vm_tok", [P, 2, 2 * P])
    wf = in_b("wf", [P, 2, P])
    mf = in_b("mf", [P, 2, 2, P])
    c1 = {name: in_b("c_" + name, [P, CONSTS[name][1]])
          for name in ("window", "rot_q", "dup0", "rot_k0", "dup1", "rot_k1", "dft_cos", "dft_sin")}
    m_hi = in_b("m_hi", [P, DC, MEM], F32R)
    m_lo = in_b("m_lo", [P, DC, MEM], F32R)
    b1[0] = REGION_B
    yc_hi = in_b("yc_hi", [P, LC, SEQ], F32R)
    yc_lo = in_b("yc_lo", [P, LC, SEQ], F32R)
    ya_hi = in_b("ya_hi", [P, LC, SEQ], F32R)
    ya_lo = in_b("ya_lo", [P, LC, SEQ], F32R)
    yb_hi = in_b("yb_hi", [P, LC, SEQ], F32R)
    yb_lo = in_b("yb_lo", [P, LC, SEQ], F32R)
    REGION_T = b1[0]
    gelu = in_b("gelu", [P, LC, SEQ])
    xa = in_b("xa", [P, LC, SEQ])
    sig = in_b("sig", [P, LC, 2, SEQ])
    lru_in = in_b("lru_in", [P, LC, SEQ])
    glu = place("glu", [P, LC, SEQ], at=REGION_B)
    conv = place("conv", [P, LC, SEQ], at=REGION_B + 8 * KB)
    craw_sq = place("craw_sq", [P, 5, SEQ], at=REGION_B + 16 * KB)
    lru_tmp = place("lru_tmp", [P, 3, SEQ], at=REGION_B + 26 * KB)
    craw = place("craw", [P, 6, SEQ], at=REGION_B + 32 * KB)
    gate_w = place("gate_w", [P, LC, 2, P], at=REGION_B + 44 * KB)
    q_head = place("q_head", [P, MLA_HEADS, SEQ], at=REGION_T)
    kv_head = place("kv_head", [P, MLA_HEADS, SEQ], at=REGION_T + 16 * KB)
    v_head = place("v_head", [P, TC, MLA_HEADS * HEAD], at=REGION_T + 32 * KB)
    mg_hi = place("mg_hi", [P, DC, SEQ], F32R, at=REGION_T)
    mg_lo = place("mg_lo", [P, DC, SEQ], F32R, at=REGION_T + 16 * KB)

    def step(q, k, v, n, out, mask, opens, closes, scale, sink=None):
        return dict(q=q, k=k, v=v, n=n, out=out, mask=mask, opens=opens, closes=closes, scale=scale, sink=sink)

    def window_steps(q, k, v):
        steps = []
        for h in range(WINDOW_HEADS):
            half, kv = (h % 2) * HEAD, h // (WINDOW_HEADS // 2)
            for b in range(TC):
                first, end = max(b - 1, 0), min(b + 2, TC)
                steps.append(step(
                    q[half:half + HEAD, h // 2, b * P:(b + 1) * P], k[half:half + HEAD, kv, first * P:end * P],
                    [v[:, j, kv * HEAD:(kv + 1) * HEAD] for j in range(first, end)], (end - first) * P,
                    (half, b * P), c1["window"][:, (first - b + 1) * P:(end - b + 1) * P],
                    h % 2 == 0 and b == 0, h % 2 == 1 and b == TC - 1, HEAD ** -0.5, h))
        return steps

    def memory_steps(q, k, v):
        steps = []
        for h in range(MEM_HEADS):
            half = (h % 2) * HEAD
            for b in range(TC):
                steps.append(step(
                    q[half:half + HEAD, h // 2, b * P:(b + 1) * P], k[half:half + HEAD, h // 2, :],
                    [v[:, j, h * HEAD:(h + 1) * HEAD] for j in range(MEM // P)], MEM,
                    (half, b * P), causal[:, 0:MEM], h % 2 == 0 and b == 0, h % 2 == 1 and b == TC - 1, HEAD ** -0.5))
        return steps

    def mla_steps(q, k, v):
        steps = []
        for h in range(MLA_HEADS):
            for b in range(TC):
                n = (b + 1) * P
                steps.append(step(
                    q[0:QK, h, b * P:n], k[0:QK, h, 0:n], [v[:, j, h * HEAD:(h + 1) * HEAD] for j in range(b + 1)], n,
                    ((h % 2) * HEAD, b * P), causal[:, SEQ - n:SEQ], h % 2 == 0 and b == 0, h % 2 == 1 and b == TC - 1,
                    QK ** -0.5))
        return steps

    stack = ExitStack()
    with stack:
        G = [stack.enter_context(nc.psum_tensor(f"products{i}", [P, 2, SEQ], F32)) for i in range(2)]
        B4, B5, B6, B7 = (stack.enter_context(nc.psum_tensor(f"small{i}", [P, SEQ], F32)) for i in range(4))
        sems = {}

        def sem(name):
            sems[name] = stack.enter_context(nc.semaphore(name))
            return sems[name]

        raw_loaded = [sem("raw_loaded0"), sem("raw_loaded1")]
        hi_ready = sem("hi_ready")
        lo_ready = sem("lo_ready")
        piece_done = sem("piece_done")
        read_out = [sem("read_out0"), sem("read_out1")]
        consts_loaded, x_loaded, rows_zeroed = sem("consts_loaded"), sem("x_loaded"), sem("rows_zeroed")
        rows_loaded, pos_loaded, turned = sem("rows_loaded"), sem("pos_loaded"), sem("turned")
        turn_copied, angle, table = sem("turn_copied"), sem("angle"), sem("table")
        soft_in, soft_exp, setup_done = sem("soft_in"), sem("soft_exp"), sem("setup_done")
        sin_done = sem("sin_done")
        x_ready = sem("x_ready")
        src_ready = sem("src_ready")
        ah_ready, al_ready = sem("ah_ready"), sem("al_ready")
        sq_ready, sq_used = sem("sq_ready"), sem("sq_used")
        totals_ready = sem("totals_ready")
        sum_ready = sem("sum_ready")
        pow_asked, pow_done = sem("pow_asked"), sem("pow_done")
        diag_ready = sem("diag_ready")
        root_asked, root_done = sem("root_asked"), sem("root_done")
        dve_step, act_step, pool_step = sem("dve_step"), sem("act_step"), sem("pool_step")
        silu_ready, h_ready, hh_ready, hl_ready = (sem(n) for n in ("silu_ready", "h_ready", "hh_ready", "hl_ready"))
        y_copied = sem("y_copied")
        mem_loaded, c1_loaded, wf_zeroed, wf_loaded, dft_loaded = (
            sem(n) for n in ("mem_loaded", "c1_loaded", "wf_zeroed", "wf_loaded", "dft_loaded"))
        rot_ready, rot_used, rope_ready = sem("rot_ready"), sem("rot_used"), sem("rope_ready")
        swap_ready, swap_copied = sem("swap_ready"), sem("swap_copied")
        four_ready, four_copied = sem("four_ready"), sem("four_copied")
        s_ready, m_ready, e_ready, p_ready = (sem(n) for n in ("s_ready", "m_ready", "e_ready", "p_ready"))
        t_ready, pt_ready, o_ready, o_used = (sem(n) for n in ("t_ready", "pt_ready", "o_ready", "o_used"))
        gate_zeroed, gate_loaded = sem("gate_zeroed"), sem("gate_loaded")
        branch_ready = sem("branch_ready")
        bias_done, xa_ready = sem("bias_done"), sem("xa_ready")
        gates_ready, sig_ready, e2_ready, v_ready = (sem(n) for n in ("gates_ready", "sig_ready", "e2_ready", "v_ready"))
        conv_done, mean_ready, centred, ln_ready = (sem(n) for n in ("conv_done", "mean_ready", "centred", "ln_ready"))
        gate_ready, merged_ready = sem("gate_ready"), sem("merged_ready")
        final_ready, tok_copied, stored = sem("final_ready"), sem("tok_copied"), sem("stored")

        Tally.carrier = sem("wait_carrier")
        row_loads = row_copies(t, rows, columns)
        n_setup_loads = 5

        block = stack.enter_context(nc.Block())

        def col(name, l, c, last=P):
            first, step = columns[name]
            return params[0:last, bass.ds(l * step + (first + c), 1)]

        prob_tiles = [X[:, i, :] for i in range(3)]
        turned_tiles = [X[:, 3, :], rs_b]
        turn_banks = [B6[:], G[1][:, 1, :]]

        mix_squares = [qT[:, i, :] for i in range(4)] + [tile[:, i, :] for tile in (zmT, kT) for i in range(2)]
        conv_squares = [glu[:, i, :] for i in range(LC)]
        lru_tanh, lru_square = (lru_tmp[:, 0, :], lru_tmp[:, 1, :]), (lru_tmp[:, 2, :], rs_b[:])
        rank_squares = [craw_sq[:, i, :] for i in range(5)]

        def wide(ap, n):
            return ap.unsqueeze(1).broadcast_to([ap.shape[0], n, ap.shape[-1]])

        @block.sync
        def _(sp):
            c = Tally("sync")
            sp.dma_start(x_tok[:], t["x"].rearrange("o (t p) d -> p (o t) d", p=P)).then_inc(x_loaded, 16)
            sp.wait_ge(rows_zeroed, 1)
            for dst, src in row_loads[1::2]:
                sp.dma_start(dst, src).then_inc(rows_loaded, 16)

            def unit(*parts):
                s = c.unit % 2
                c.unit += 1
                assert len(parts) == 2
                sp.wait_ge(lo_ready, c.next("lo_ready"))
                c.apart(sp)
                for w, l, row, nk, first, n, at in parts:
                    sp.dma_start(
                        raw[:, s, at:at + nk * n].rearrange("p (k n) -> p k n", n=n),
                        t[w][bass.ds(l, 1), row:row + nk * P, bass.ds(first, n)].rearrange("o (k p) n -> p (o k) n", p=P),
                    ).then_inc(raw_loaded[s], 16)

            def tall(w, l, first, n=2 * P, row=0, nk=DC):
                half = nk // 2
                unit((w, l, row, half, first, n, 0), (w, l, row + half * P, nk - half, first, n, half * n))

            def ffn(w1, w2, l, label):
                tall(w1, l, 0)
                tall(w1, l, FF)
                for i in c.turns(sp, 1, FF // (2 * P), PER_TURN["ffn_in"], "ffn_in"):
                    tall(w1, l, i * (2 * P))
                    tall(w1, l, i * (2 * P) + FF)
                for i in c.turns(sp, 0, 2, PER_TURN["ffn_out"], "ffn_out"):
                    for j in range(2):
                        for row, nk in ((0, 8), (8, 8), (16, 6)):
                            tall(w2, l, i * (4 * P) + 2 * P * j, row=row * P, nk=nk)

            for l in c.layers(sp, PER_LAYER["one"], "one"):
                tall("w_in", l, 0)
                tall("w_in", l, 2 * P)
                tall("w_in", l, 4 * P)
                tall("w_in", l, 6 * P, P)
                tall("w_in", l, 7 * P, P)
                tall("w_in", l, 8 * P)
                for j in range(2):
                    tall("w_mem_kv", l, 2 * P * j)
                for i in c.turns(sp, 0, 2, PER_TURN["w_out"], "w_out"):
                    for j in range(2):
                        tall("w_out", l, i * (4 * P) + 2 * P * j)
                ffn("w_ffn_in", "w_ffn_out", l, "one")
            for l in c.layers(sp, PER_LAYER["two"], "two"):
                ffn("ffn1_w1_2", "ffn1_w2_2", l, "two")
                for j in range(LC):
                    unit(("w_in_2", l, 0, DC, IN_C + P * j, P, 0), ("w_in_2", l, 0, DC, IN_C + LRU + P * j, P, UNIT // 2))
                for j in range(4):
                    tall("w_in_2", l, 2 * P * j)
                tall("w_in_2", l, IN_B)
                tall("w_in_2", l, IN_B + 2 * P)
                tall("w_in_2", l, IN_B + 4 * P, n=P + PE_DIM)
                unit(("w_ukv_2", l, 0, 1, 0, 2 * LRU, 0), ("w_ukv_2", l, P, 1, 0, 2 * LRU, 2 * LRU))
                for j in range(2):
                    unit(("w_uq_2", l, 0, 2, 4 * QK * j, 4 * QK, 0), ("w_uq_2", l, 2 * P, 1, 4 * QK * j, 4 * QK, 8 * QK))
                for i in c.turns(sp, 0, DC // 2, PER_TURN["merge"], "merge"):
                    for j in range(2):
                        at = i * (2 * P) + P * j
                        unit(("w_in_2", l, 0, DC, at + IN_G, P, 0), ("w_in_2", l, 0, DC, at + (IN_G + D), P, UNIT // 2))
                        unit(("w_in_2", l, 0, DC, at + (IN_G + 2 * D), P, 0), ("lru_w_out_2", l, 0, LC, at, P, UNIT // 2))
                        unit(("mla_w_o_2", l, 0, LC, at, P, 0), ("conv_w_out_2", l, 0, LC, at, P, LC * P))
                for i in c.turns(sp, 0, 2, PER_TURN["w_out"], "w_out"):
                    for j in range(2):
                        tall("w_out_2", l, i * (4 * P) + 2 * P * j)
                ffn("ffn2_w1_2", "ffn2_w2_2", l, "two")
            for s in range(2):
                sp.wait_ge(lo_ready, c.next("lo_ready"))
                sp.sem_inc(raw_loaded[s], 32)
            for half in range(2):
                sp.wait_ge(tok_copied, (half + 1) * DC // 2)
                channels = slice(half * SEQ, (half + 1) * SEQ)
                sp.dma_start(out[0].rearrange("(t p) d -> p t d", p=P)[:, :, channels],
                             out_tok[:, :, channels]).then_inc(stored, 16)
            sp.wait_ge(stored, 2 * 16)

        @block.tensor
        def _(pe):
            c = Tally("tensor")
            c.n["lo_ready"] = 2
            c.n["sq_used"] = 1

            def take_unit():
                pe.wait_ge(lo_ready, c.next("lo_ready"))
                c.unit += 1

            def piece(blocks, first=True, last=True, n=SEQ, fresh=None, between=None, signals=True):
                s = (c.unit - 1) % 2
                pair = c.group % 2
                if first:
                    pe.wait_ge(read_out[pair], c.next(f"read_out{pair}"))
                for b, (m, terms) in enumerate(blocks):
                    if b == 1 and between:
                        between()
                    for k, (at, hi, lo) in enumerate(terms):
                        if fresh and b == 0:
                            pe.wait_ge(sems[fresh], c.next(fresh))
                        for q, (w, x) in enumerate(((w_hi, hi), (w_hi, lo), (w_lo, hi))):
                            mm = pe.matmul(G[pair][0:m, b, 0:n], w[:, s, at:at + m], x,
                                           start=first and k == 0 and q == 0,
                                           stop=last and k == len(terms) - 1 and q == 2)
                if signals:
                    mm.then_inc(piece_done, 1)
                if last:
                    c.group += 1

            def tall(nk, width, hi, lo, k0=0, blocks=2, **how):
                piece([(P, [(k * width + b * P, hi[:, k0 + k, :], lo[:, k0 + k, :]) for k in range(nk)])
                       for b in range(blocks)], **how)

            def full(fresh=None, blocks=2, hi=a_hi, lo=a_lo, n=SEQ, between=None):
                take_unit()
                tall(DC, blocks * P, hi, lo, blocks=blocks, fresh=fresh, n=n, between=between)

            def sum_channels(n=SEQ):
                pe.wait_ge(sq_used, c.now("sq_used"))
                for i in range(n // P):
                    mm = pe.matmul(B7[:, i:i + 1], X[:, 1, i * P:(i + 1) * P], ones[:, 0:1], start=True, stop=True)
                mm.then_inc(sum_ready, 1)

            def sum_groups(totals, columns=B7[:]):
                pe.wait_ge(totals_ready, c.next("totals_ready"))
                for g, total in enumerate(totals):
                    for i in range(TC):
                        at = g * TC + i
                        mm = pe.matmul(columns[:, at:at + 1], total[:, i * P:(i + 1) * P], ones[:, 0:1], start=True, stop=True)
                mm.then_inc(sum_ready, 1)

            def spread_groups(totals, banks):
                for bank, total in zip(banks, totals):
                    pe.wait_ge(diag_ready, c.next("diag_ready"))
                    pe.matmul(bank, ones[:], total, start=True, stop=True).then_inc(sum_ready, 1)

            def spread(n=SEQ):
                pe.wait_ge(diag_ready, c.next("diag_ready"))
                pe.matmul(B7[:, 0:n], ones[:], X[:, 1, 0:n], start=True, stop=True).then_inc(sum_ready, 1)

            def ffn(post_norm, squares=True):
                full(fresh="al_ready")
                c.one("sq_used", DC if squares else 0)
                sum_channels()
                full(between=spread)
                for _ in c.turns(pe, 1, FF // (2 * P), PER_TURN["ffn_in"], "ffn_in"):
                    full()
                    full()
                pe.wait_ge(hl_ready, c.next("hl_ready", FF // (2 * P) - 1))
                c.one("hl_ready")
                for _ in c.turns(pe, 0, 2, PER_TURN["ffn_out"], "ffn_out"):
                    for j in range(2):
                        for k0, nk in ((0, 8), (8, 8), (16, 6)):
                            take_unit()
                            if k0 == 16:
                                pe.wait_ge(hl_ready, c.now("hl_ready"))
                            tall(nk, 2 * P, h_hi, h_lo, k0=k0, first=k0 == 0, last=k0 == 16)
                if post_norm:
                    c.one("sq_used", DC)
                    sum_channels()
                    spread()

            def attention(steps, between=None):
                n = len(steps)
                for s in range(n + 3):
                    if s < n:
                        st = steps[s]
                        if s >= 2:
                            pe.wait_ge(m_ready, c.next("m_ready"))
                        pe.matmul((B4, B5)[s % 2][:, 0:st["n"]], st["q"], st["k"], start=True, stop=True).then_inc(s_ready, 1)
                    if 2 <= s < n + 2:
                        st, tile = steps[s - 2], prob_tiles[(s - 2) % 3]
                        pe.wait_ge(p_ready, c.next("p_ready"))
                        for j in range(st["n"] // P):
                            mm = pe.transpose(turn_banks[s % 2][:, j * P:(j + 1) * P], tile[:, j * P:(j + 1) * P], ident[:])
                        mm.then_inc(t_ready, 1)
                    if s >= 3:
                        st, tile = steps[s - 3], turned_tiles[(s - 3) % 2]
                        pe.wait_ge(pt_ready, c.next("pt_ready"))
                        if st["opens"] and s > 3:
                            pe.wait_ge(o_used, c.next("o_used"))
                        vs = st["v"]
                        r0, c0 = st["out"]
                        for j, v in enumerate(vs):
                            mm = pe.matmul(B7[r0:r0 + HEAD, c0:c0 + P], v, tile[:, j * P:(j + 1) * P],
                                           start=j == 0, stop=j == len(vs) - 1)
                        if st["closes"]:
                            mm.then_inc(o_ready, 1)
                    if between:
                        between(s)
                c.one("m_ready", 2)
                c.one("o_used")

            def all_read_out():
                for p in range(2):
                    pe.wait_ge(read_out[p], c.now(f"read_out{p}") + 1)

            pe.wait_ge(consts_loaded, c.next("consts_loaded", 16 * n_setup_loads))
            pe.wait_ge(x_loaded, 16)
            for i in range(DC):
                if i >= 2:
                    pe.wait_ge(turn_copied, i - 1)
                for tc in range(TC):
                    mm = pe.transpose((B4, B5)[i % 2][:, tc * P:(tc + 1) * P], x_tok[:, tc, i * P:(i + 1) * P], ident[:])
                mm.then_inc(turned, 1)
            pe.wait_ge(rows_loaded, c.next("rows_loaded", 16 * len(row_loads)))
            for i in range(DC, DC + n_param_tiles):
                pe.wait_ge(turn_copied, i - 1)
                pe.transpose((B4, B5)[i % 2][:, 0:P], rows[:, i - DC, :], ident[:]).then_inc(turned, 1)

            for l in c.layers(pe, PER_LAYER["one"], "one"):
                full(fresh="al_ready")
                c.one("sq_used", DC)
                sum_channels()
                pe.wait_ge(mem_loaded, c.next("mem_loaded", 16))
                for i in range(DC // 2):
                    if i:
                        pe.wait_ge(swap_copied, c.next("swap_copied"))
                    for j in range(4):
                        mm = pe.transpose(B6[:, j * P:(j + 1) * P],
                                          mem_tok[:, j % 2, (2 * i + j // 2) * P:(2 * i + j // 2 + 1) * P], ident[:])
                    mm.then_inc(swap_ready, 1)
                c.one("swap_copied")
                full(between=spread)
                full()
                full(blocks=1)
                full(blocks=1)
                full()
                take_unit()
                tall(DC, 2 * P, m_hi, m_lo, fresh="al_ready", n=MEM)
                c.one("sq_used", DC)
                sum_channels(MEM)
                spread(MEM)
                full(hi=m_hi, lo=m_lo, n=MEM)
                pe.wait_ge(c1_loaded, c.next("c1_loaded", 16 * len(c1)))
                all_read_out()
                for i in range(4):
                    if i >= 2:
                        pe.wait_ge(rot_used, c.next("rot_used"))
                    pe.matmul((B4, B5)[i % 2][:], c1["rot_q"][:], qT[:, i, :], start=True, stop=True).then_inc(rot_ready, 1)
                for j in range(2):
                    for bank, name in ((B4, f"dup{j}"), (B5, f"rot_k{j}")):
                        pe.wait_ge(rot_used, c.next("rot_used"))
                        pe.matmul(bank[:], c1[name][:], zkT[:], start=True, stop=True).then_inc(rot_ready, 1)
                c.one("rot_used", 2)
                pe.wait_ge(swap_copied, c.now("swap_copied"))
                for j in range(TC):
                    mm = pe.transpose(B6[:, j * P:(j + 1) * P], vT[:, j * P:(j + 1) * P], ident[:])
                mm.then_inc(swap_ready, 1)
                for j in range(4):
                    mm = pe.transpose(B7[:, j * P:(j + 1) * P], vmT[:, j % 2, (j // 2) * P:(j // 2 + 1) * P], ident[:])
                mm.then_inc(swap_ready, 1)
                pe.wait_ge(wf_loaded, c.next("wf_loaded", 32))
                pe.wait_ge(rot_used, c.now("rot_used"))
                for j in range(2):
                    for i, name in enumerate(("dft_cos", "dft_sin")):
                        at = (2 * j + i) * P
                        mm = pe.matmul(B4[:, at:at + P], c1[name][:], wf[:, j, :], start=True, stop=True)
                mm.then_inc(four_ready, 1)
                for tc in range(TC):
                    pe.wait_ge(four_copied, c.next("four_copied"))
                    for j in range(2):
                        mm = pe.matmul((B5, B4)[tc % 2][:, j * 2 * P:(j + 1) * 2 * P], zfT[:, j, tc * P:(tc + 1) * P],
                                       mf[:, j, :, :], start=True, stop=True)
                    mm.then_inc(four_ready, 1)
                pe.wait_ge(four_copied, c.next("four_copied"))
                pe.wait_ge(dft_loaded, c.next("dft_loaded", 16))
                for j in range(2):
                    for tc in range(TC):
                        for i in range(2):
                            mm = pe.matmul((B4, B5)[j][:], ab[:, tc, (2 * j + i) * P:(2 * j + i + 1) * P], dft[:, tc, i, :],
                                           start=tc == 0 and i == 0, stop=tc == TC - 1 and i == 1)
                    mm.then_inc(four_ready, 1)
                c.one("four_copied", 2)
                pe.wait_ge(four_copied, c.now("four_copied"))
                c.one("swap_copied", 2)
                pe.wait_ge(swap_copied, c.now("swap_copied"))
                pe.wait_ge(rope_ready, c.next("rope_ready", 6))
                attention(window_steps(qT, kT, v_tok))
                attention(memory_steps(zmT, kmT, vm_tok))
                totals = [mix_squares[chunks[0]] for chunks in GROUPS]
                sum_groups(totals)
                spread_groups(totals, (B4[:], B5[:], B6[:]))
                take_unit()
                tall(DC, 2 * P, a_hi, a_lo, fresh="al_ready")
                full()
                full()
                full()
                c.one("sq_used", DC)
                sum_channels()
                spread()
                ffn(True)
            c.one("sq_used", DC)
            for l in c.layers(pe, PER_LAYER["two"], "two"):
                ffn(False, squares=False)
                full_two_parts = [(P, [(b * UNIT // 2 + k * P, a_hi[:, k, :], a_lo[:, k, :]) for k in range(DC)]) for b in range(2)]
                take_unit()
                piece(full_two_parts, fresh="al_ready")
                c.one("sq_used", DC)
                sum_channels()
                take_unit()
                piece(full_two_parts, between=spread)
                for _ in range(LC - 2):
                    take_unit()
                    piece(full_two_parts)
                for _ in range(4):
                    full()
                pe.wait_ge(gate_loaded, c.next("gate_loaded", 64))
                for i in range(LC):
                    pe.wait_ge(xa_ready, c.next("xa_ready"))
                    if i >= 2:
                        pe.wait_ge(sig_ready, c.next("sig_ready", 2))
                    for j in range(2):
                        pe.matmul((B4, B5, B6, B7)[i % 2 * 2 + j][:], gate_w[:, i, j, :], xa[:, i, :],
                                  start=True, stop=True).then_inc(gates_ready, 1)
                c.one("sig_ready", 4)
                full()
                full()
                take_unit()
                wide_n = P + PE_DIM
                piece([(P, [(k * wide_n, a_hi[:, k, :], a_lo[:, k, :]) for k in range(DC)])])
                piece([(QK, [(k * wide_n + HEAD, a_hi[:, k, :], a_lo[:, k, :]) for k in range(DC)])])

                pe.wait_ge(sig_ready, c.now("sig_ready"))
                totals = [rank_squares[chunks[0]] for chunks in RANKS]
                sum_groups(totals)
                spread_groups(totals, (B4[:], B5[:]))
                pe.wait_ge(al_ready, c.next("al_ready", 2))
                take_unit()
                for g in range(4):
                    piece([(P, [(k * 2 * LRU + (2 * g + b) * P, a_hi[:, 3 + k, :], a_lo[:, 3 + k, :]) for k in range(2)])
                           for b in range(2)])
                pe.matmul(B5[0:QK, :], rot96[0:QK, :], craw[0:QK, 5, :], start=True, stop=True).then_inc(rot_ready, 1)
                all_read_out()
                for h in range(MLA_HEADS):
                    if h >= 2:
                        pe.wait_ge(swap_copied, c.next("swap_copied"))
                    for j in range(TC):
                        mm = pe.transpose((B6, B7)[h % 2][:, j * P:(j + 1) * P], kv_head[:, h, j * P:(j + 1) * P], ident[:])
                    mm.then_inc(swap_ready, 1)
                c.one("swap_copied", 2)
                pe.wait_ge(al_ready, c.next("al_ready", 3))

                def rotated(heads):
                    for h in heads:
                        if h >= 1:
                            pe.wait_ge(rot_used, c.next("rot_used"))
                        pe.matmul((B4, B5)[h % 2][0:QK, :], rot96[0:QK, :], q_head[0:QK, h, :], start=True, stop=True).then_inc(rot_ready, 1)

                for u in range(2):
                    take_unit()
                    for g in range(2):
                        piece([(QK, [(k * 4 * QK + (2 * g + b) * QK, a_hi[:, k, :], a_lo[:, k, :]) for k in range(3)])
                               for b in range(2)])
                        if u:
                            rotated((2 * g, 2 * g + 1))
                all_read_out()
                rotated(range(4, MLA_HEADS))
                c.one("rot_used", 2)
                pe.wait_ge(swap_copied, c.now("swap_copied"))
                pe.wait_ge(rope_ready, c.next("rope_ready", 2 * MLA_HEADS))
                pe.wait_ge(rot_used, c.now("rot_used"))

                def layer_norm(s):
                    if s == 22:
                        pe.wait_ge(conv_done, c.next("conv_done"))
                        for i in range(LC):
                            mm = pe.matmul(G[0][:, 0, :], ones[:], conv[:, i, :], start=i == 0, stop=i == LC - 1)
                        mm.then_inc(mean_ready, 1)
                    if s == 27:
                        sum_groups([conv_squares[0]], columns=G[0][:, 1, :])
                    if s == 30:
                        spread_groups([conv_squares[0]], (G[1][:, 0, :],))

                attention(mla_steps(q_head, kv_head, v_head), layer_norm)
                pe.wait_ge(o_used, c.now("o_used"))
                c.one("branch_ready", 2 * LC)
                pe.wait_ge(al_ready, c.next("al_ready", DC))

                def eight(at):
                    return (P, [(at + k * P, a_hi[:, k, :], a_lo[:, k, :]) for k in range(DC)])

                def four(at, hi, lo):
                    return (P, [(at + k * P, hi[:, k, :], lo[:, k, :]) for k in range(LC)])

                for _ in c.turns(pe, 0, DC // 2, PER_TURN["merge"], "merge"):
                    for j in range(2):
                        take_unit()
                        piece([eight(0), eight(UNIT // 2)])
                        take_unit()
                        piece([eight(0), four(UNIT // 2, ya_hi, ya_lo)])
                        take_unit()
                        pe.wait_ge(branch_ready, c.now("branch_ready"))
                        piece([four(0, yb_hi, yb_lo), four(LC * P, yc_hi, yc_lo)])
                pe.wait_ge(hl_ready, c.next("hl_ready", DC - 1))
                c.one("hl_ready")
                last = DC - 1
                for _ in c.turns(pe, 0, 2, PER_TURN["w_out"], "w_out"):
                    for j in range(2):
                        take_unit()
                        piece([(P, [(k * 2 * P + b * P, mg_hi[:, k, :], mg_lo[:, k, :]) for k in range(last)])
                               for b in range(2)], last=False, signals=False)
                        pe.wait_ge(hl_ready, c.now("hl_ready"))
                        piece([(P, [(last * 2 * P + b * P, mg_hi[:, last, :], mg_lo[:, last, :])]) for b in range(2)],
                              first=False)
                ffn(False)
                c.one("sq_used", DC)
            sum_channels()
            spread()
            for i in range(DC):
                pe.wait_ge(final_ready, i + 1)
                if i >= 2:
                    pe.wait_ge(tok_copied, i - 1)
                for tc in range(TC):
                    mm = pe.transpose((B4, B5)[i % 2][:, tc * P:(tc + 1) * P], xT[:, i, tc * P:(tc + 1) * P], ident[:])
                mm.then_inc(turned, 1)


        @block.scalar
        def _(act):
            c = Tally("scalar")
            c.n.update(read_out0=1, read_out1=1, sq_used=1)

            def split_hi():
                s = c.split % 2
                c.split += 1
                act.wait_ge(raw_loaded[s], c.next(f"raw_loaded{s}", 32))
                act.activation(w_hi[:, s, :], raw[:, s, :], ACT.Copy).then_inc(hi_ready, 1)

            def unit_done(pieces=1):
                act.wait_ge(piece_done, c.next("piece_done", pieces))
                split_hi()

            def out_name():
                name = c.group % 2
                c.group += 1
                return name

            def group_read():
                p = out_name()
                act.wait_ge(read_out[p], c.next(f"read_out{p}"))

            def group_skipped():
                c.one(f"read_out{out_name()}")

            def square(src, n=SEQ, at_register=False):
                act.wait_ge(sq_used, c.now("sq_used"))
                if at_register:
                    c.apart(act)
                act.activation(X[:, 0, 0:n], src, ACT.Square).then_inc(sq_ready, 1)
                c.one("sq_used")

            def operand(gain, l, squares=True):
                for i in range(DC):
                    if squares:
                        act.wait_ge(x_ready, c.next("x_ready"))
                    c.apart(act)
                    act.activation(a_hi[:, i, :], xT[:, i, :], ACT.Copy, scale=col(gain, l, i)).then_inc(ah_ready, 1)
                if squares:
                    squares_of_x()

            def squares_of_x():
                for i in range(DC):
                    if i >= 3:
                        act.wait_ge(sq_used, c.now("sq_used") - 2)
                    act.activation(X[:, (0, 2, 3)[i % 3], :], xT[:, i, :], ACT.Square).then_inc(sq_ready, 1)
                    c.one("sq_used")

            def high_and_square(chunks, gain, l):
                group_read()
                c.apart(act)
                for i in chunks if gain else ():
                    c.apart(act)
                    act.activation(a_hi[:, i, :], xT[:, i, :], ACT.Copy, scale=col(gain, l, i)).then_inc(ah_ready, 1)
                for i in chunks:
                    if i >= 3:
                        act.wait_ge(sq_used, c.now("sq_used") - 2)
                    act.activation(X[:, (0, 2, 3)[i % 3], :], xT[:, i, :], ACT.Square).then_inc(sq_ready, 1)
                    c.one("sq_used")

            def ffn(gain, l, post_norm, between=None, early=False, next_gain=None, squares=True, last=False):
                if not early:
                    operand(gain, l, squares)

                def gate_and_up(i):
                    unit_done()
                    group_read()
                    act.activation(X[:, 0:2, :], X[:, 0:2, :], ACT.Silu).then_inc(silu_ready, 1)
                    unit_done()
                    group_skipped()
                    act.wait_ge(h_ready, c.next("h_ready"))
                    c.apart(act)
                    act.activation(h_hi[:, bass.ds(i * 2, 2), :], X[:, 2:4, :], ACT.Copy).then_inc(hh_ready, 1)

                gate_and_up(0)
                for i in c.turns(act, 1, FF // (2 * P), PER_TURN["ffn_in"], "ffn_in"):
                    gate_and_up(i)
                if between:
                    between()
                for i in range(2) if next_gain or last else c.turns(act, 0, 2, PER_TURN["ffn_out"], "ffn_out"):
                    for j in range(2):
                        for _ in range(3):
                            unit_done()
                        if post_norm:
                            copy_and_square(y_ffn, i * 4 + 2 * j)
                        elif next_gain or last:
                            high_and_square((4 * i + 2 * j, 4 * i + 2 * j + 1), next_gain, l)
                        else:
                            group_skipped()

            def copy_and_square(y, chunk):
                p = out_name()
                c.apart(act)
                act.activation(y[:, bass.ds(chunk, 2), :], G[p][:], ACT.Copy).then_inc(read_out[p], c.one(f"read_out{p}"))
                act.wait_ge(read_out[p], c.now(f"read_out{p}"))
                for b in range(2):
                    square(y[:, bass.ds(chunk + b, 1), :].rearrange("p o n -> p (o n)"), at_register=True)

            def attention(steps, l, leave, between=None):
                n = len(steps)
                for s in range(n + 3):
                    if s >= 3:
                        st = steps[s - 3]
                        act.wait_ge(t_ready, c.next("t_ready"))
                        act.activation(turned_tiles[(s - 3) % 2][:, 0:st["n"]], turn_banks[(s - 1) % 2][:, 0:st["n"]], ACT.Copy).then_inc(pt_ready, 1)
                    if s < n:
                        st = steps[s]
                        tile = prob_tiles[s % 3][:, 0:st["n"]]
                        act.wait_ge(m_ready, c.next("m_ready"))
                        e = act.activation(tile, tile, ACT.Exp, bias=stats[:, 3, s:s + 1], scale=st["scale"],
                                           accum_out=stats[:, 1, s:s + 1])
                        if st["sink"] is not None:
                            e = act.activation(stats[:, 2, s:s + 1], sinks[:, bass.ds(l * WINDOW_HEADS + st["sink"], 1)],
                                               ACT.Exp, bias=stats[:, 3, s:s + 1])
                        e.then_inc(e_ready, 1)
                    if s >= 3 and steps[s - 3]["closes"]:
                        act.wait_ge(o_ready, c.next("o_ready"))
                        leave()
                    if between:
                        between(s)

            act.dma_start(ident[:], t["consts"][:, CONSTS["ident"][0]:CONSTS["ident"][0] + P]).then_inc(consts_loaded, 16)
            for name, tile in (("rot96", rot96), ("causal", causal), ("freq", freq)):
                at, n = CONSTS[name]
                act.dma_start(tile[:], t["consts"][:, at:at + n]).then_inc(consts_loaded, 16)
            act.dma_start(sinks[:], t["sink"].rearrange("l h -> (l h)").partition_broadcast(P)).then_inc(consts_loaded, 16)
            act.dma_start(X[:, 0, :].bitcast(I32), t["positions"][0].partition_broadcast(P)).then_inc(pos_loaded, c.one("pos_loaded", 16))
            act.wait_ge(rows_zeroed, 1)
            for dst, src in row_loads[0::2]:
                act.dma_start(dst, src).then_inc(rows_loaded, 16)

            def sines():
                act.wait_ge(angle, c.next("angle"))
                act.activation(sinT[:], X[:, 3, :], ACT.Sin).then_inc(sin_done, c.one("sin_done"))
                act.wait_ge(angle, c.next("angle"))
                act.activation(cosT[:], X[:, 3, :], ACT.Sin).then_inc(sin_done, c.one("sin_done"))

            sines()
            split_hi()
            split_hi()

            for l in c.layers(act, PER_LAYER["one"], "one"):
                operand("g_pre_mix", l)
                unit_done()
                group_skipped()
                for i in range(DC // 2):
                    act.wait_ge(swap_ready, c.next("swap_ready"))
                    act.activation(memT[:, 2 * i:2 * i + 2, :], B6[:], ACT.Copy).then_inc(swap_copied, 1)
                act.wait_ge(swap_copied, c.next("swap_copied", DC // 2))
                c.apart(act)
                for i in range(DC):
                    act.activation(m_hi[:, i, :], memT[:, i, :], ACT.Copy, scale=col("g_mem", l, i)).then_inc(ah_ready, 1)
                    square(memT[:, i, :], MEM)
                for _ in range(7):
                    unit_done()
                    group_skipped()
                act.wait_ge(swap_ready, c.next("swap_ready"))
                act.activation(v_tok[:], B6[:], ACT.Copy).then_inc(swap_copied, 1)
                act.wait_ge(swap_ready, c.next("swap_ready"))
                act.activation(vm_tok[:], B7[:], ACT.Copy).then_inc(swap_copied, 1)
                c.one("swap_copied", 2)
                act.wait_ge(four_ready, c.next("four_ready"))
                act.activation(mf[:], B4[:], ACT.Copy).then_inc(four_copied, 1)
                for tc in range(TC):
                    act.wait_ge(four_ready, c.next("four_ready"))
                    act.activation(ab[:, tc, :], (B5, B4)[tc % 2][:], ACT.Copy).then_inc(four_copied, 1)
                for j in range(2):
                    act.wait_ge(four_ready, c.next("four_ready"))
                    act.activation(y_mix[:, j, :], (B4, B5)[j][:], ACT.Copy).then_inc(four_copied, 1)
                c.one("four_copied", 3 + TC)
                chunk = iter(range(2, DC))

                def leave():
                    act.activation(y_mix[:, next(chunk), :], B7[:], ACT.Copy).then_inc(o_used, c.one("o_used"))

                attention(window_steps(qT, kT, v_tok), l, leave)
                attention(memory_steps(zmT, kmT, vm_tok), l, leave)
                act.wait_ge(o_used, c.now("o_used"))
                act.wait_ge(four_copied, c.now("four_copied"))
                for i in range(DC):
                    act.activation(mix_squares[i], y_mix[:, i, :], ACT.Square).then_inc(sq_ready, 1)
                for i in range(DC):
                    act.wait_ge(src_ready, c.next("src_ready"))
                    act.activation(a_hi[:, i, :], X[:, 2 + i % 2, :], ACT.Copy).then_inc(ah_ready, 1)
                for j in range(4):
                    unit_done()
                    copy_and_square(y_mix, 2 * j)
                ffn("g_pre_ffn", l, True)

            act.wait_ge(x_ready, c.next("x_ready", DC))
            c.apart(act)
            squares_of_x()

            def tables():
                act.wait_ge(hl_ready, c.next("hl_ready", FF // (2 * P)))
                c.apart(act)
                act.dma_start(X[:, 0, :].bitcast(I32), t["positions_2"][0].partition_broadcast(P)).then_inc(
                    pos_loaded, c.one("pos_loaded", 16))
                sines()
                act.wait_ge(soft_in, c.next("soft_in"))
                act.activation(tiny[:, 2, :], tiny[:, 1, :], ACT.Exp).then_inc(soft_exp, c.one("soft_exp"))
                c.one("hl_ready", DC + FF // (2 * P))

            for l in c.layers(act, PER_LAYER["two"], "two"):
                ffn("ffn1_norm", l, False, between=tables, next_gain="mix_norm", squares=False)
                for j in range(LC):
                    unit_done()
                    group_read()
                    c.apart(act)
                    act.activation(X[:, 3, :], X[:, 3, :], ACT.Sigmoid, bias=col("b_c", l, LC + j)).then_inc(bias_done, 1)
                for j in range(4):
                    unit_done()
                    group_read()
                    c.apart(act)
                    for b in range(2):
                        i = 2 * j + b
                        dst = lru_in[:, i, :] if j < 2 else gelu[:, i - LC, :]
                        act.activation(dst, X[:, 2 + b, :], ACT.Identity if j < 2 else ACT.Gelu_apprx_tanh,
                                       bias=col("b_a", l, i)).then_inc(bias_done, 1)
                for i in range(LC):
                    for j, name in enumerate(("b_r", "b_i")):
                        act.wait_ge(gates_ready, c.next("gates_ready"))
                        c.apart(act)
                        act.activation(sig[:, i, j, :], (B4, B5, B6, B7)[i % 2 * 2 + j][:], ACT.Sigmoid,
                                       bias=col(name, l, i)).then_inc(sig_ready, 1)
                c.one("sig_ready", 2 * LC)

                def lru_powers(i):
                    if i >= 2:
                        act.wait_ge(root_asked, c.next("root_asked"))
                    c.apart(act)
                    once, twice = (decay[:, j, bass.ds(l * LC + i, 1)] for j in range(2))
                    act.activation(lru_tanh[i % 2], sig[:, i, 0, :], ACT.Tanh, scale=once)
                    act.activation(lru_square[i % 2], sig[:, i, 0, :], ACT.Exp, scale=twice)
                    act.activation(sig[:, i, 0, :], sig[:, i, 0, :], ACT.Exp, scale=once).then_inc(e2_ready, 1)

                act.wait_ge(sig_ready, c.now("sig_ready"))
                for j in range(4):
                    if j != 2:
                        unit_done()
                    else:
                        act.wait_ge(piece_done, c.next("piece_done"))
                    group_read()
                    c.apart(act)
                    if j < 2:
                        for b in range(2):
                            act.activation(craw[:, 2 * j + b, :], X[:, 2 + b, :], ACT.Identity,
                                           bias=col("b_b", l, 2 * j + b)).then_inc(bias_done, 1)
                    elif j == 2:
                        act.activation(craw[:, 4, :], X[:, 2, :], ACT.Identity, bias=col("b_b", l, 4)).then_inc(bias_done, 1)
                    else:
                        act.activation(craw[0:QK, 5, :], X[0:QK, 2, :], ACT.Identity,
                                       bias=col("b_kpe", l, 0, QK)).then_inc(bias_done, 1)
                    if j == 0:
                        c.one("bias_done", LC + 8)
                    c.one("bias_done", 2 if j < 2 else 1)
                    if j < 3:
                        lru_powers(j)
                    if j in (1, 2):
                        act.wait_ge(bias_done, c.now("bias_done"))
                        c.apart(act)
                        for i in (0, 1, 2, 3) if j == 1 else (4,):
                            act.activation(rank_squares[i], craw[:, i, :], ACT.Square).then_inc(sq_ready, 1)
                act.wait_ge(bias_done, c.now("bias_done"))
                lru_powers(3)
                for n, i in enumerate(sum(RANKS, ())):
                    act.wait_ge(src_ready, c.next("src_ready"))
                    act.activation(a_hi[:, i, :], X[:, 1 + n % 2, :], ACT.Copy).then_inc(ah_ready, 1)
                act.wait_ge(root_asked, c.next("root_asked", 2))
                c.apart(act)
                for i in range(LC):
                    act.activation(sig[:, i, 1, :], sig[:, i, 1, :], ACT.Sqrt, scale=-1.0).then_inc(root_done, 1)

                def take_heads(m, tile, first, end, before=None):
                    for h in range(first, end, 2):
                        if before:
                            before(h // 2)
                        act.wait_ge(piece_done, c.next("piece_done"))
                        p = out_name()
                        act.activation(tile[0:m, h:h + 2, :], G[p][0:m], ACT.Copy).then_inc(read_out[p], c.one(f"read_out{p}"))
                    split_hi()

                def high_of_lru(i):
                    act.wait_ge(v_ready, c.next("v_ready"))
                    act.activation(ya_hi[:, i, :], gelu[:, i, :], ACT.Copy).then_inc(ah_ready, 1)

                take_heads(P, kv_head, 0, MLA_HEADS, high_of_lru)
                for h in range(MLA_HEADS):
                    act.wait_ge(swap_ready, c.next("swap_ready"))
                    act.activation(v_head[:, :, h * HEAD:(h + 1) * HEAD],
                                   (B6, B7)[h % 2][:].rearrange("p (t e) -> p t e", t=TC)[:, :, HEAD:P], ACT.Copy).then_inc(swap_copied, 1)
                act.wait_ge(branch_ready, c.next("branch_ready", LC))
                take_heads(QK, q_head, 0, MLA_HEADS // 2)
                take_heads(QK, q_head, MLA_HEADS // 2, MLA_HEADS)
                pair = iter(range(LC))

                def leave():
                    i = next(pair)
                    act.activation(yb_hi[:, i, :], B7[:], ACT.Copy).then_inc(ah_ready, 1)
                    for chunk in (2 * i, 2 * i + 1):
                        act.activation(a_hi[:, chunk, :], xT[:, chunk, :], ACT.Copy,
                                       scale=col("mix_norm", l, chunk)).then_inc(ah_ready, 1)

                def layer_norm(s):
                    if s == 24:
                        act.wait_ge(centred, c.next("centred"))
                        for i in range(LC):
                            act.activation(conv_squares[i], conv[:, i, :], ACT.Square).then_inc(sq_ready, 1)

                attention(mla_steps(q_head, kv_head, v_head), l, leave, layer_norm)
                for i in range(LC):
                    act.wait_ge(ln_ready, c.next("ln_ready"))
                    c.apart(act)
                    act.activation(conv[:, i, :], conv[:, i, :], ACT.Silu, bias=col("ln_b", l, i),
                                   scale=col("ln_g", l, i)).then_inc(act_step, c.one("act_step"))
                    act.wait_ge(act_step, c.now("act_step"))
                    act.activation(yc_hi[:, i, :], conv[:, i, :], ACT.Copy).then_inc(ah_ready, 1)
                c.one("branch_ready", LC)
                for i in c.turns(act, 0, DC // 2, PER_TURN["merge"], "merge"):
                    for j in range(2):
                        chunk = i * 2 + j
                        unit_done()
                        group_read()
                        c.apart(act)
                        for b in range(2):
                            g = act.activation(X[:, b, :], X[:, b, :], ACT.Sigmoid, bias=col("b_g", l, chunk + DC * b))
                        g.then_inc(gate_ready, c.one("gate_ready"))
                        unit_done()
                        group_skipped()
                        act.wait_ge(src_ready, c.next("src_ready"))
                        c.apart(act)
                        act.activation(X[:, 2, :], X[:, 2, :], ACT.Sigmoid,
                                       bias=col("b_g", l, chunk + DC * 2)).then_inc(gate_ready, c.one("gate_ready"))
                        unit_done()
                        group_skipped()
                        act.wait_ge(merged_ready, c.next("merged_ready"))
                        c.apart(act)
                        act.activation(mg_hi[:, bass.ds(chunk, 1), :].rearrange("p o n -> p (o n)"), X[:, 0, :],
                                       ACT.Copy).then_inc(ah_ready, 1)
                for j in range(4):
                    unit_done()
                    high_and_square((2 * j, 2 * j + 1), "ffn2_norm", l)
                ffn("ffn2_norm", l, False, early=True, last=True)
            for i in range(DC):
                act.wait_ge(turned, n_param_tiles + DC + 1 + i)
                act.activation(out_tok[:, :, i * P:(i + 1) * P], (B4, B5)[i % 2][:].rearrange("p (t e) -> p t e", t=TC),
                               ACT.Copy).then_inc(tok_copied, 1)

        @block.vector
        def _(dve):
            c = Tally("vector")

            def settled():
                dve.wait_ge(dve_step, c.now("dve_step"))

            def stepped(ins):
                ins.then_inc(dve_step, c.one("dve_step"))

            def split_lo():
                s = c.split % 2
                c.split += 1
                dve.wait_ge(hi_ready, c.next("hi_ready"))
                dve.tensor_tensor(w_lo[:, s, :], raw[:, s, :], w_hi[:, s, :].bitcast(F32), ALU.subtract).then_inc(lo_ready, 1)

            def piece():
                dve.wait_ge(piece_done, c.next("piece_done"))

            def group():
                p = c.group % 2
                c.group += 1
                return p

            def taken(ins, p):
                ins.then_inc(read_out[p], c.one(f"read_out{p}"))

            def scaled(dst, p, r, n=SEQ, blocks=2):
                taken(dve.tensor_tensor(dst, G[p][:, 0:blocks, 0:n], wide(r[:, 0:n], blocks), ALU.mult), p)

            def begin_sum():
                stepped(dve.memset(X[:, 1, :], 0.0))
                settled()

            def add_square(n=SEQ, tile=0):
                dve.wait_ge(sq_ready, c.next("sq_ready"))
                dve.tensor_tensor(X[:, 1, 0:n], X[:, 1, 0:n], X[:, tile, 0:n], ALU.add).then_inc(sq_used, c.one("sq_used"))

            def low_and_square(chunks, gain, l):
                for i in chunks if gain else ():
                    lows_of_x(i, gain, l)
                for i in chunks:
                    dve.wait_ge(sq_used, c.now("sq_used"))
                    add_square(tile=(0, 2, 3)[i % 3])

            def inverse_rms(dst, d, n=SEQ):
                dve.wait_ge(sum_ready, c.next("sum_ready"))
                tiles = n // P
                dve.tensor_scalar(mean_sq[:, 0:tiles], B7[:, 0:tiles], 1.0 / d, EPS, ALU.mult, ALU.add).then_inc(pow_asked, 1)
                dve.wait_ge(pow_done, c.next("pow_done"))
                for i in range(tiles):
                    last = dve.tensor_scalar(X[:, 1, i * P:(i + 1) * P], ident[:], mean_sq[:, i:i + 1], None, ALU.mult)
                last.then_inc(diag_ready, 1)
                dve.wait_ge(sum_ready, c.next("sum_ready"))
                stepped(dve.tensor_copy(dst[:, 0:n], B7[:, 0:n]))
                settled()

            def lows_of_x(i, gain, l):
                dve.wait_ge(ah_ready, c.next("ah_ready"))
                dve.scalar_tensor_tensor(a_lo[:, i, :], xT[:, i, :], col(gain, l, i), a_hi[:, i, :].bitcast(F32),
                                         ALU.mult, ALU.subtract).then_inc(al_ready, c.one("al_ready"))

            def operand(gain, l, lows=True, squares=True):
                for i in range(DC if lows else 0):
                    lows_of_x(i, gain, l)
                for i in range(DC if squares else 0):
                    dve.wait_ge(sq_used, c.now("sq_used"))
                    add_square(tile=(0, 2, 3)[i % 3])

            def low_of(dst, full, hi, signal):
                dve.wait_ge(ah_ready, c.next("ah_ready"))
                dve.tensor_tensor(dst, full, hi.bitcast(F32), ALU.subtract).then_inc(sems[signal], 1)

            def group_totals(groups, squares):
                chunks = sum(groups, ())
                dve.wait_ge(sq_ready, c.next("sq_ready", len(chunks)))
                c.apart(dve)
                for group in groups:
                    for i in group[1:]:
                        total = dve.tensor_tensor(squares[group[0]], squares[group[0]], squares[i], ALU.add)
                        if i == chunks[-1]:
                            total.then_inc(totals_ready, 1)
                        else:
                            stepped(total)
                            settled()

            def group_roots(groups, squares, columns=B7[:], meanwhile=None):
                dve.wait_ge(sum_ready, c.next("sum_ready"))
                for g, group in enumerate(groups):
                    mean = dve.tensor_scalar(mean_sq[:, g * TC:(g + 1) * TC], columns[:, g * TC:(g + 1) * TC],
                                             1.0 / (P * len(group)), EPS, ALU.mult, ALU.add)
                mean.then_inc(pow_asked, 1)
                if meanwhile:
                    meanwhile()
                dve.wait_ge(pow_done, c.next("pow_done"))
                for g, group in enumerate(groups):
                    for i in range(TC):
                        last = dve.tensor_scalar(squares[group[0]][:, i * P:(i + 1) * P], ident[:],
                                                 mean_sq[:, g * TC + i:g * TC + i + 1], None, ALU.mult)
                    last.then_inc(diag_ready, 1)

            def normalised(src, groups, gains, ring, l):
                chunks = sum(groups, ())

                def low(n):
                    low_of(a_lo[:, chunks[n], :], X[:, ring + n % 2, :], a_hi[:, chunks[n], :], "al_ready")
                    c.one("al_ready")

                n = 0
                for bank, group, gain in zip((B4, B5, B6), groups, gains):
                    dve.wait_ge(sum_ready, c.next("sum_ready"))
                    c.apart(dve)
                    for i in group:
                        if n >= 2:
                            dve.wait_ge(al_ready, c.now("al_ready"))
                        dve.scalar_tensor_tensor(X[:, ring + n % 2, :], src[:, i, :], col(gain[0], l, i - gain[1]), bank[:],
                                                 ALU.mult, ALU.mult).then_inc(src_ready, c.one("src_ready"))
                        if n:
                            low(n - 1)
                        n += 1
                low(n - 1)

            def post_norm(y, gain, l, next_gain=None):
                inverse_rms(rs_b, D)

                for i in range(DC + 1):
                    if i < DC:
                        if i >= 2:
                            dve.wait_ge(x_ready, c.now("x_ready"))
                        stepped(dve.scalar_tensor_tensor(X[:, 2 + i % 2, :], y[:, i, :], col(gain, l, i), rs_b[:],
                                                         ALU.mult, ALU.mult))
                    if i:
                        dve.wait_ge(dve_step, c.now("dve_step") - (i < DC))
                        dve.tensor_tensor(xT[:, i - 1, :], xT[:, i - 1, :], X[:, 2 + (i - 1) % 2, :],
                                          ALU.add).then_inc(x_ready, c.one("x_ready"))
                    if next_gain and i >= 3:
                        lows_of_x(i - 3, next_gain, l)
                if next_gain:
                    lows_of_x(DC - 2, next_gain, l)
                    lows_of_x(DC - 1, next_gain, l)
                dve.wait_ge(x_ready, c.now("x_ready"))

            def ffn(gain, l, post, scale, between=None, early=False, next_gain=None, squares=True, last=False):
                if squares and not early:
                    begin_sum()
                if not early:
                    operand(gain, l, lows=not post, squares=squares)
                inverse_rms(rs, D)

                def gate_and_up(i, peeled=False):
                    piece()
                    scaled(X[:, 0:2, :], group(), rs)
                    split_lo()
                    piece()
                    p = group()
                    if not peeled:
                        dve.wait_ge(hl_ready, c.now("hl_ready"))
                    scaled(X[:, 2:4, :], p, rs)
                    dve.wait_ge(silu_ready, c.next("silu_ready"))
                    dve.wait_ge(read_out[p], c.now(f"read_out{p}"))
                    dve.tensor_tensor(X[:, 2:4, :], X[:, 2:4, :], X[:, 0:2, :], ALU.mult).then_inc(h_ready, 1)
                    split_lo()
                    dve.wait_ge(hh_ready, c.next("hh_ready"))
                    dve.tensor_tensor(h_lo[:, bass.ds(i * 2, 2), :], X[:, 2:4, :],
                                      h_hi[:, bass.ds(i * 2, 2), :].bitcast(F32), ALU.subtract).then_inc(hl_ready, c.one("hl_ready"))

                gate_and_up(0, peeled=True)
                for i in c.turns(dve, 1, FF // (2 * P), PER_TURN["ffn_in"], "ffn_in"):
                    gate_and_up(i)
                if between:
                    dve.wait_ge(hl_ready, c.now("hl_ready"))
                    between()
                if post or next_gain or last:
                    begin_sum()
                for i in range(2) if next_gain or last else c.turns(dve, 0, 2, PER_TURN["ffn_out"], "ffn_out"):
                    for j in range(2):
                        for u in range(3):
                            piece()
                            split_lo()
                            if (next_gain or last) and u == 0 and i + j:
                                low_and_square((4 * i + 2 * j - 2, 4 * i + 2 * j - 1), next_gain, l)
                        p = group()
                        if post:
                            c.one(f"read_out{p}")
                            for _ in range(2):
                                add_square()
                        else:
                            x2 = xT[:, bass.ds(i * 4 + 2 * j, 2), :]
                            taken(dve.scalar_tensor_tensor(x2, G[p][:], scale, x2, ALU.mult, ALU.add), p)
                if post:
                    post_norm(y_ffn, post, l)
                else:
                    for p in range(2):
                        dve.wait_ge(read_out[p], c.now(f"read_out{p}"))
                    if next_gain or last:
                        low_and_square((DC - 2, DC - 1), next_gain, l)

            def attention(steps, l, leave=None, between=None):
                n = len(steps)
                for s in range(n + 3):
                    if s < n:
                        st = steps[s]
                        biggest = stats[:, 0, s:s + 1]
                        if s >= 3:
                            dve.wait_ge(t_ready, c.next("t_ready"))
                        dve.wait_ge(s_ready, c.next("s_ready"))
                        c.apart(dve)
                        stepped(dve.tensor_tensor_reduce(prob_tiles[s % 3][:, 0:st["n"]], (B4, B5)[s % 2][:, 0:st["n"]],
                                                         st["mask"], 1.0, -3.0e38, ALU.add, ALU.max, biggest))
                    if 1 <= s <= n:
                        total, inverse = stats[:, 1, s - 1:s], stats[:, 2, s - 1:s]
                        dve.wait_ge(e_ready, c.next("e_ready"))
                        if steps[s - 1]["sink"] is not None:
                            stepped(dve.tensor_tensor(total, total, stats[:, 2, s - 1:s], ALU.add))
                            settled()
                        stepped(dve.reciprocal(inverse, total))
                        settled()
                    if s < n:
                        if s == 0:
                            settled()
                        if st["sink"] is None:
                            negated = dve.tensor_scalar(stats[:, 3, s:s + 1], biggest, -st["scale"], None, ALU.mult)
                        else:
                            negated = dve.tensor_scalar(stats[:, 3, s:s + 1], biggest, -st["scale"],
                                                        minus_sinks[:, bass.ds(l * WINDOW_HEADS + st["sink"], 1)],
                                                        ALU.mult, ALU.min)
                        negated.then_inc(m_ready, 1)
                    if 1 <= s <= n:
                        tile = prob_tiles[(s - 1) % 3][:, 0:steps[s - 1]["n"]]
                        dve.tensor_scalar(tile, tile, inverse, None, ALU.mult).then_inc(p_ready, 1)
                    if s >= 3 and steps[s - 3]["closes"] and leave:
                        leave()
                    if between:
                        between(s)
                c.one("t_ready", 3)
                dve.wait_ge(t_ready, c.now("t_ready"))
                dve.wait_ge(p_ready, c.next("p_ready", n))

            def rope_tables(column):
                two_pi = 2 * np.pi
                c1_, rest = 6.28125, two_pi - 6.28125
                c2_ = float(np.round(rest * 2 ** 19) / 2 ** 19)
                c3_ = float(np.round((rest - c2_) * 2 ** 30) / 2 ** 30)
                c4_ = float(rest - c2_ - c3_)
                dve.wait_ge(pos_loaded, c.next("pos_loaded", 16))
                stepped(dve.tensor_copy(X[:, 1, :], X[:, 0, :].bitcast(I32)))
                settled()
                stepped(dve.tensor_scalar(X[:, 1, :], X[:, 1, :], freq[:, column:column + 1], None, ALU.mult))
                settled()
                for quarter in (0.0, 0.25):
                    stepped(dve.tensor_scalar(X[:, 2, :], X[:, 1, :], 1.0 / two_pi, quarter, ALU.mult, ALU.add))
                    settled()
                    stepped(dve.tensor_scalar(X[:, 2, :], X[:, 2, :], 1.5 * 2.0 ** 23, None, ALU.add))
                    settled()
                    stepped(dve.tensor_scalar(X[:, 2, :], X[:, 2, :], -1.5 * 2.0 ** 23, None, ALU.add))
                    settled()
                    src = X[:, 1, :]
                    for part in (c1_, c2_, c3_, c4_):
                        stepped(dve.scalar_tensor_tensor(X[:, 3, :], X[:, 2, :], -part, src, ALU.mult, ALU.add))
                        settled()
                        src = X[:, 3, :]
                    if quarter:
                        stepped(dve.tensor_scalar(X[:, 3, :], X[:, 3, :], float(np.pi / 2), None, ALU.add))
                        settled()
                    dve.tensor_scalar(X[:, 3, :], X[:, 3, :], 3.1415925, -3.1415925, ALU.min, ALU.max).then_inc(angle, c.one("angle"))
                    dve.wait_ge(sin_done, c.next("sin_done"))

            def lru_decay():
                lam_at = columns["lambda"][0]
                lam = params[:, lam_at:lam_at + DEPTH * LC]
                v = [tiny[:, i, :] for i in range(6)]
                stepped(dve.tensor_scalar(v[0], lam, -1.0, None, ALU.mult))
                settled()
                dve.tensor_tensor(v[1], v[0], lam, ALU.min).then_inc(soft_in, c.one("soft_in"))
                dve.wait_ge(soft_exp, c.next("soft_exp"))
                stepped(dve.tensor_scalar(v[3], v[2], 2.0, None, ALU.add))
                settled()
                stepped(dve.reciprocal(v[4], v[3]))
                settled()
                stepped(dve.tensor_tensor(v[2], v[2], v[4], ALU.mult))
                settled()
                stepped(dve.tensor_tensor(v[3], v[2], v[2], ALU.mult))
                settled()
                stepped(dve.tensor_scalar(v[4], v[3], 1.0 / 15, 1.0 / 13, ALU.mult, ALU.add))
                settled()
                for odd in (11, 9, 7, 5, 3, 1):
                    stepped(dve.tensor_tensor(v[4], v[4], v[3], ALU.mult))
                    settled()
                    stepped(dve.tensor_scalar(v[4], v[4], 1.0 / odd, None, ALU.add))
                    settled()
                stepped(dve.tensor_tensor(v[4], v[4], v[2], ALU.mult))
                stepped(dve.tensor_scalar(v[5], v[0], 0.0, None, ALU.max))
                settled()
                stepped(dve.scalar_tensor_tensor(v[3], v[4], 2.0, v[5], ALU.mult, ALU.add))
                settled()
                stepped(dve.tensor_scalar(decay[:, 0, :], v[3], -8.0, None, ALU.mult))
                stepped(dve.tensor_scalar(decay[:, 1, :], v[3], -16.0, None, ALU.mult))
                settled()

            def tables():
                rope_tables(1)
                lru_decay()

            dve.wait_ge(pool_step, 2)
            dve.memset(rows[:], 0.0).then_inc(rows_zeroed, 1)
            dve.memset(ones[:], 1.0).then_inc(sq_used, c.one("sq_used"))
            dve.memset(tiny[:, 0, :], 0.0).then_inc(read_out[0], c.one("read_out0"))
            dve.memset(tiny[:, 4, :], 0.0).then_inc(read_out[1], c.one("read_out1"))
            for s in range(2):
                dve.memset(raw[:, s, :], 0.0).then_inc(lo_ready, 1)
            for i in range(DC):
                dve.wait_ge(turned, i + 1)
                dve.tensor_copy(xT[:, i, :], (B4, B5)[i % 2][:]).then_inc(turn_copied, 1)
            dve.wait_ge(consts_loaded, c.next("consts_loaded", 16 * n_setup_loads))
            stepped(dve.tensor_scalar(minus_sinks[:], sinks[:], -1.0, None, ALU.mult))
            rope_tables(0)
            for i in range(DC, DC + n_param_tiles):
                dve.wait_ge(turned, i + 1)
                dve.tensor_copy(params[:, (i - DC) * P:(i - DC + 1) * P], (B4, B5)[i % 2][:, 0:P]).then_inc(turn_copied, 1)
            dve.wait_ge(turn_copied, DC + n_param_tiles)
            dve.memset(tiny[:, 1, :], 0.0).then_inc(x_ready, c.one("x_ready", DC))
            split_lo()
            split_lo()
            for l in c.layers(dve, PER_LAYER["one"], "one"):
                begin_sum()
                operand("g_pre_mix", l)
                inverse_rms(rs, D)
                piece()
                scaled(zfT[:], group(), rs)
                split_lo()
                begin_sum()
                for i in range(DC):
                    dve.wait_ge(ah_ready, c.next("ah_ready"))
                    dve.scalar_tensor_tensor(m_lo[:, i, :], memT[:, i, :], col("g_mem", l, i), m_hi[:, i, :].bitcast(F32),
                                             ALU.mult, ALU.subtract).then_inc(al_ready, c.one("al_ready"))
                    add_square(MEM)
                for dst, blocks in ((qT[:, 0:2, :], 2), (qT[:, 2:4, :], 2), (zkT[:].unsqueeze(1), 1),
                                    (vT[:].unsqueeze(1), 1), (zmT[:], 2)):
                    piece()
                    scaled(dst, group(), rs, blocks=blocks)
                    split_lo()
                inverse_rms(rs_b, D, MEM)
                for dst in (kmT, vmT):
                    piece()
                    scaled(dst[:], group(), rs_b, n=MEM)
                    split_lo()
                for p in range(2):
                    dve.wait_ge(read_out[p], c.now(f"read_out{p}"))
                for i in range(4):
                    if i:
                        dve.wait_ge(rope_ready, c.now("rope_ready"))
                    dve.wait_ge(rot_ready, c.next("rot_ready"))
                    dve.tensor_tensor(X[:, 2, :], (B4, B5)[i % 2][:], sinT[:], ALU.mult).then_inc(rot_used, c.one("rot_used"))
                    stepped(dve.tensor_tensor(qT[:, i, :], qT[:, i, :], cosT[:], ALU.mult))
                    dve.wait_ge(rot_used, c.now("rot_used"))
                    settled()
                    dve.tensor_tensor(qT[:, i, :], qT[:, i, :], X[:, 2, :], ALU.add).then_inc(rope_ready, c.one("rope_ready"))
                for j in range(2):
                    dve.wait_ge(rope_ready, c.now("rope_ready"))
                    dve.wait_ge(rot_ready, c.next("rot_ready", 2))
                    dve.tensor_tensor(kT[:, j, :], B4[:], cosT[:], ALU.mult).then_inc(rot_used, c.one("rot_used"))
                    dve.tensor_tensor(X[:, 2, :], B5[:], sinT[:], ALU.mult).then_inc(rot_used, c.one("rot_used"))
                    dve.wait_ge(rot_used, c.now("rot_used"))
                    dve.tensor_tensor(kT[:, j, :], kT[:, j, :], X[:, 2, :], ALU.add).then_inc(rope_ready, c.one("rope_ready"))
                attention(window_steps(qT, kT, v_tok), l)
                attention(memory_steps(zmT, kmT, vm_tok), l)
                group_totals(GROUPS, mix_squares)
                group_roots(GROUPS, mix_squares)
                normalised(y_mix, GROUPS, [("g_grp", 0)] * 3, 2, l)
                begin_sum()
                for j in range(4):
                    piece()
                    p = group()
                    c.one(f"read_out{p}")
                    split_lo()
                    for _ in range(2):
                        add_square()
                post_norm(y_mix, "g_post_mix", l, next_gain="g_pre_ffn")
                ffn("g_pre_ffn", l, "g_post_ffn", None)

            begin_sum()
            for i in range(DC):
                dve.wait_ge(sq_used, c.now("sq_used"))
                add_square(tile=(0, 2, 3)[i % 3])
            for l in c.layers(dve, PER_LAYER["two"], "two"):
                ffn("ffn1_norm", l, None, 0.5, between=tables, next_gain="mix_norm", squares=False)
                inverse_rms(rs, D)
                settled()

                at31, per31 = columns["dw_w"]
                todo = [(i, k) for pair in ((0, 1), (2, 3)) for k in reversed(range(CONV_TAPS)) for i in pair]
                written = {}

                def conv_taps(count):
                    for _ in range(min(count, len(todo))):
                        i, k = todo.pop(0)
                        w = params[:, bass.ds(l * per31 + (at31 + k * LC + i), 1)]
                        late = CONV_TAPS - 1 - k
                        if late == 0:
                            tap = dve.tensor_scalar(conv[:, i, :], glu[:, i, :], w, col("dw_b", l, i), ALU.mult, ALU.add)
                        else:
                            dve.wait_ge(dve_step, c.now("dve_step") - (c.n["dve_step"] - written[i]))
                            tap = dve.scalar_tensor_tensor(conv[:, i, late:], glu[:, i, 0:SEQ - late], w,
                                                           conv[:, i, late:], ALU.mult, ALU.add)
                        if todo:
                            stepped(tap)
                            written[i] = c.n["dve_step"]
                        else:
                            tap.then_inc(conv_done, c.one("conv_done"))

                def short_conv(i):
                    at, per = columns["conv4_w"]
                    for k in reversed(range(LRU_TAPS)):
                        w = params[:, bass.ds(l * per + (at + k * LC + i), 1)]
                        late = LRU_TAPS - 1 - k
                        if late == 0:
                            stepped(dve.tensor_scalar(xa[:, i, :], lru_in[:, i, :], w, col("conv4_b", l, i), ALU.mult, ALU.add))
                        else:
                            settled()
                            tap = dve.scalar_tensor_tensor(xa[:, i, late:], lru_in[:, i, 0:SEQ - late], w, xa[:, i, late:],
                                                           ALU.mult, ALU.add)
                            if k:
                                stepped(tap)
                            else:
                                tap.then_inc(xa_ready, c.one("xa_ready"))

                def lru_root(i):
                    dve.wait_ge(e2_ready, c.next("e2_ready"))
                    stepped(dve.tensor_tensor(xa[:, i, :], sig[:, i, 1, :], xa[:, i, :], ALU.mult))
                    settled()
                    dve.scalar_tensor_tensor(sig[:, i, 1, :], lru_square[i % 2], 1.0, lru_tanh[i % 2],
                                             ALU.add, ALU.mult).then_inc(root_asked, 1)

                def skip_pieces(n):
                    for _ in range(n):
                        piece()
                        c.one(f"read_out{group()}")
                    split_lo()

                for j in range(LC):
                    piece()
                    scaled(X[:, 2:4, :], group(), rs)
                    split_lo()
                    if j >= 2:
                        conv_taps(7)
                    dve.wait_ge(bias_done, c.next("bias_done"))
                    stepped(dve.scalar_tensor_tensor(glu[:, j, :], X[:, 2, :], col("b_c", l, j), X[:, 3, :],
                                                     ALU.add, ALU.mult))
                    settled()
                for j in range(4):
                    piece()
                    scaled(X[:, 2:4, :], group(), rs)
                    split_lo()
                    if j >= 2:
                        conv_taps(9)
                    dve.wait_ge(bias_done, c.next("bias_done", 2))
                    if j < 2:
                        short_conv(2 * j)
                        short_conv(2 * j + 1)
                conv_taps(12)
                for j in range(4):
                    piece()
                    p = group()
                    if j < 2:
                        scaled(X[:, 2:4, :], p, rs)
                    elif j == 2:
                        scaled(X[:, 2:3, :], p, rs, blocks=1)
                    else:
                        taken(dve.tensor_tensor(X[0:QK, 2, :], G[p][0:QK, 0, :], rs[0:QK, :], ALU.mult), p)
                    if j == 3:
                        group_totals(RANKS, rank_squares)
                    if j != 2:
                        split_lo()
                    if j < 2:
                        conv_taps(7)
                    dve.wait_ge(bias_done, c.next("bias_done", 2 if j < 2 else 1))
                    if j:
                        lru_root(j - 1)
                group_roots(RANKS, rank_squares, meanwhile=lambda: conv_taps(2))
                lru_root(3)
                normalised(craw, RANKS, [("kv_norm", 3), ("q_norm", 0)], 1, l)
                for i in range(LC):
                    dve.wait_ge(root_done, c.next("root_done"))
                    stepped(dve.tensor_tensor(xa[:, i, :], xa[:, i, :], sig[:, i, 1, :], ALU.mult))
                    settled()
                    if i:
                        dve.wait_ge(v_ready, c.now("v_ready"))
                    stepped(dve.tensor_tensor_scan(X[:, 3, :], sig[:, i, 0, :], xa[:, i, :], 0.0, ALU.mult, ALU.add))
                    settled()
                    dve.tensor_tensor(gelu[:, i, :], gelu[:, i, :], X[:, 3, :], ALU.mult).then_inc(v_ready, c.one("v_ready"))
                conv_taps(6)
                dve.wait_ge(v_ready, c.now("v_ready"))
                for i in range(LC):
                    low_of(ya_lo[:, i, :], gelu[:, i, :], ya_hi[:, i, :], "branch_ready")
                skip_pieces(4)
                conv_taps(12)
                turn = slice(HEAD, QK)
                dve.wait_ge(rot_ready, c.next("rot_ready"))
                stepped(dve.tensor_tensor(X[turn, 2, :], B5[turn, :], sinT[turn, :], ALU.mult))
                stepped(dve.tensor_tensor(craw[turn, 5, :], craw[turn, 5, :], cosT[turn, :], ALU.mult))
                settled()
                dve.tensor_tensor(craw[turn, 5, :], craw[turn, 5, :], X[turn, 2, :], ALU.add).then_inc(rot_used, c.one("rot_used"))
                dve.wait_ge(rot_used, c.now("rot_used"))
                dve.wait_ge(swap_copied, c.next("swap_copied", MLA_HEADS))
                for h in range(MLA_HEADS):
                    dve.tensor_copy(kv_head[turn, h, :], craw[turn, 5, :]).then_inc(rope_ready, c.one("rope_ready"))
                conv_taps(4)
                skip_pieces(2)
                for first in range(0, MLA_HEADS, 2):
                    dve.wait_ge(rope_ready, c.now("rope_ready"))
                    for h in (first, first + 1):
                        dve.wait_ge(rot_ready, c.next("rot_ready"))
                        dve.tensor_tensor(X[turn, 2 + h % 2, :], (B4, B5)[h % 2][turn, :], sinT[turn, :],
                                          ALU.mult).then_inc(rot_used, c.one("rot_used"))
                        stepped(dve.tensor_tensor(q_head[turn, h, :], q_head[turn, h, :], cosT[turn, :], ALU.mult))
                    dve.wait_ge(rot_used, c.now("rot_used"))
                    settled()
                    for h in (first, first + 1):
                        dve.tensor_tensor(q_head[turn, h, :], q_head[turn, h, :], X[turn, 2 + h % 2, :],
                                          ALU.add).then_inc(rope_ready, c.one("rope_ready"))
                skip_pieces(2)
                dve.wait_ge(rope_ready, c.now("rope_ready"))
                pair = iter(range(LC))

                def leave():
                    i = next(pair)
                    low_of(yb_lo[:, i, :], B7[:], yb_hi[:, i, :], "o_used")
                    for chunk in (2 * i, 2 * i + 1):
                        lows_of_x(chunk, "mix_norm", l)

                every = ((tuple(range(LC)),), conv_squares)

                def layer_norm(s):
                    if s < 21:
                        conv_taps(2)
                    if s == 21:
                        conv_taps(len(todo))
                    if s == 23:
                        dve.wait_ge(mean_ready, c.next("mean_ready"))
                        dve.wait_ge(conv_done, c.now("conv_done"))
                        c.apart(dve)
                        for i in range(LC):
                            less = dve.scalar_tensor_tensor(conv[:, i, :], G[0][:, 0, :], -1.0 / LRU, conv[:, i, :],
                                                            ALU.mult, ALU.add)
                        less.then_inc(centred, c.one("centred"))
                    if s == 26:
                        group_totals(*every)
                    if s == 28:
                        group_roots(*every, columns=G[0][:, 1, :])
                    if s == 32:
                        dve.wait_ge(sum_ready, c.next("sum_ready"))
                        dve.wait_ge(centred, c.now("centred"))
                        c.apart(dve)
                        for i in range(LC):
                            dve.tensor_tensor(conv[:, i, :], conv[:, i, :], G[1][:, 0, :], ALU.mult).then_inc(ln_ready, c.one("ln_ready"))

                attention(mla_steps(q_head, kv_head, v_head), l, leave, layer_norm)
                for i in range(LC):
                    low_of(yc_lo[:, i, :], conv[:, i, :], yc_hi[:, i, :], "branch_ready")
                for i in c.turns(dve, 0, DC // 2, PER_TURN["merge"], "merge"):
                    for j in range(2):
                        chunk = i * 2 + j
                        piece()
                        dve.wait_ge(hl_ready, c.now("hl_ready"))
                        scaled(X[:, 0:2, :], group(), rs)
                        split_lo()
                        piece()
                        p = group()
                        dve.tensor_tensor(X[:, 2, :], G[p][:, 0, :], rs[:], ALU.mult).then_inc(src_ready, c.one("src_ready"))
                        dve.wait_ge(gate_ready, c.next("gate_ready"))
                        taken(dve.tensor_tensor(X[:, 0, :], X[:, 0, :], G[p][:, 1, :], ALU.mult), p)
                        split_lo()
                        piece()
                        q = group()
                        stepped(dve.tensor_tensor(X[:, 1, :], X[:, 1, :], G[q][:, 0, :], ALU.mult))
                        dve.wait_ge(gate_ready, c.next("gate_ready"))
                        taken(dve.scalar_tensor_tensor(X[:, 2, :], G[q][:, 1, :], col("conv_b_out", l, chunk), X[:, 2, :],
                                                       ALU.add, ALU.mult), q)
                        settled()
                        stepped(dve.tensor_tensor(X[:, 0, :], X[:, 0, :], X[:, 1, :], ALU.add))
                        settled()
                        dve.wait_ge(read_out[q], c.now(f"read_out{q}"))
                        dve.tensor_tensor(X[:, 0, :], X[:, 0, :], X[:, 2, :], ALU.add).then_inc(merged_ready, c.one("merged_ready"))
                        split_lo()
                        low_of(mg_lo[:, bass.ds(chunk, 1), :].rearrange("p o n -> p (o n)"), X[:, 0, :],
                               mg_hi[:, bass.ds(chunk, 1), :].rearrange("p o n -> p (o n)"), "hl_ready")
                        c.one("hl_ready")
                dve.wait_ge(hl_ready, c.now("hl_ready"))
                begin_sum()
                for j in range(4):
                    piece()
                    p = group()
                    x2 = xT[:, 2 * j:2 * j + 2, :]
                    taken(dve.tensor_tensor(x2, x2, G[p][:], ALU.add), p)
                    split_lo()
                    dve.wait_ge(read_out[p], c.now(f"read_out{p}"))
                    low_and_square((2 * j, 2 * j + 1), "ffn2_norm", l)
                ffn("ffn2_norm", l, None, 0.5, early=True, last=True)
            inverse_rms(rs, D)
            first = columns["final_norm"][0]
            for i in range(DC):
                dve.scalar_tensor_tensor(xT[:, i, :], xT[:, i, :], params[:, first + i:first + i + 1], rs[:],
                                         ALU.mult, ALU.mult).then_inc(final_ready, 1)

        @block.gpsimd
        def _(pool):
            c = Tally("gpsimd")

            def inverse_roots(n):
                for _ in range(n):
                    pool.wait_ge(pow_asked, c.next("pow_asked"))
                    pool.tensor_tensor(mean_sq[:], mean_sq[:], minus_half[:], ALU.pow).then_inc(pow_done, 1)

            pool.memset(minus_half[:], -0.5).then_inc(pool_step, 1)
            pool.memset(mean_sq[:], 1.0).then_inc(pool_step, 1)
            pool.wait_ge(pool_step, 2)
            pool.wait_ge(x_loaded, 16)
            for l in c.layers(pool, PER_LAYER["one"], "one"):
                pool.wait_ge(x_ready, c.next("x_ready", DC))
                c.apart(pool)
                pool.dma_start(mem_tok[:], t["mem"].rearrange("o (t p) d -> p (o t) d", p=P)).then_inc(mem_loaded, 16)
                inverse_roots(1)
                for name, tile in c1.items():
                    at, n = CONSTS[name]
                    pool.dma_start(tile[:], t["consts"][:, at:at + n]).then_inc(c1_loaded, 16)
                pool.memset(wf[:], 0.0).then_inc(wf_zeroed, 1)
                pool.wait_ge(wf_zeroed, c.next("wf_zeroed"))
                c.apart(pool)
                for half in range(2):
                    pool.dma_start(wf[half * HEAD:(half + 1) * HEAD, :, half * HEAD:(half + 1) * HEAD],
                                   t["w_fourier"][bass.ds(l, 1), half::2].rearrange("o j c e -> c (o j) e")).then_inc(wf_loaded, 16)
                inverse_roots(1)
                pool.wait_ge(piece_done, c.next("piece_done", 6))
                c.apart(pool)
                pool.dma_start(dft[:], t["dft"].rearrange("(t p) i n -> p t i n", p=P)).then_inc(dft_loaded, 16)
                c.one("piece_done", PER_LAYER["one"].get("piece_done", 6) - 6)
                c.one("x_ready", DC)
                inverse_roots(4)
            for l in c.layers(pool, PER_LAYER["two"], "two"):
                inverse_roots(1)
                pool.wait_ge(piece_done, c.next("piece_done", 34))
                c.apart(pool)
                pool.memset(gate_w[:], 0.0).then_inc(gate_zeroed, 1)
                pool.wait_ge(gate_zeroed, c.next("gate_zeroed"))
                c.apart(pool)
                for half in range(2):
                    for i in range(2):
                        pool.dma_start(
                            gate_w[half * HEAD:(half + 1) * HEAD, :, i, half * HEAD:(half + 1) * HEAD],
                            t["lru_w_gate_2"][bass.ds(l, 1), half::2, :, i * HEAD:(i + 1) * HEAD].rearrange("o j c e -> c (o j) e"),
                        ).then_inc(gate_loaded, 16)
                c.one("piece_done", PER_LAYER["two"]["piece_done"] - 34)
                inverse_roots(4)
            inverse_roots(1)

    if Tally.wrong:
        raise ValueError(sorted({w[:3] for w in Tally.wrong}))


def row_copies(t, rows, columns):
    whole = {"g_pre_mix": "g_pre_mix", "g_mem": "g_mem", "g_grp": "g_grp", "g_post_mix": "g_post_mix",
             "g_pre_ffn": "g_pre_ffn", "g_post_ffn": "g_post_ffn", "ffn1_norm": "ffn1_norm_2",
             "mix_norm": "mix_norm_2", "conv4_b": "lru_conv_b_2", "lambda": "lru_lambda_2", "q_norm": "q_norm_2",
             "kv_norm": "kv_norm_2", "dw_b": "conv_dw_b_2", "ln_g": "conv_ln_g_2", "ln_b": "conv_ln_b_2",
             "conv_b_out": "conv_b_out_2", "ffn2_norm": "ffn2_norm_2"}
    biases = {"b_a": 0, "b_b": IN_B, "b_c": IN_C, "b_g": IN_G}
    counts = dict(PARAM_ROWS, dw_w=CONV_TAPS * LC)
    out = []
    for name, n in counts.items():
        first, step = columns[name]
        if name != "dw_w":
            dst = rows[first % P:first % P + DEPTH * n, first // P, :]
        if name in whole:
            out.append((dst, t[whole[name]].rearrange("l (c p) -> (l c) p", p=P)))
            continue
        if name == "conv4_w":
            out.append((dst, t["lru_conv_w_2"].rearrange("l k (c p) -> (l k c) p", p=P)))
            continue
        if name == "final_norm":
            out.append((dst, t["final_norm_2"].rearrange("(c p) -> c p", p=P)))
            continue
        for l in range(DEPTH):
            at = first + l * step
            dst = rows[at % P:at % P + n, at // P, :]
            if name in biases:
                src = t["b_in_2"][l, biases[name]:biases[name] + n * P].rearrange("(c p) -> c p", p=P)
            elif name == "b_kpe":
                dst = dst[:, 0:QK]
                src = t["b_in_2"][l:l + 1, IN_C - QK:IN_C]
            elif name in ("b_r", "b_i"):
                half = HEAD * (name == "b_i")
                dst = dst.rearrange("c (t e) -> c t e", t=2)
                src = t["lru_b_gate_2"][l, :, half:half + HEAD].rearrange("(c t) e -> c t e", t=2)
            else:
                assert name == "dw_w"
                src = t["conv_dw_w_2"][l].rearrange("k (c p) -> (k c) p", p=P)
            out.append((dst, src))
    return out


_INS = ["x", "mem", "positions", "w_in", "w_fourier", "w_mem_kv", "w_out", "w_ffn_in", "w_ffn_out", "sink",
        "g_pre_mix", "g_mem", "g_grp", "g_post_mix", "g_pre_ffn", "g_post_ffn",
        "positions_2", "ffn1_norm_2", "ffn1_w1_2", "ffn1_w2_2", "mix_norm_2", "w_in_2", "b_in_2", "lru_conv_w_2",
        "lru_conv_b_2", "lru_w_gate_2", "lru_b_gate_2", "lru_lambda_2", "lru_w_out_2", "q_norm_2", "w_uq_2",
        "kv_norm_2", "w_ukv_2", "mla_w_o_2", "conv_dw_w_2", "conv_dw_b_2", "conv_ln_g_2", "conv_ln_b_2",
        "conv_w_out_2", "conv_b_out_2", "w_out_2", "ffn2_norm_2", "ffn2_w1_2", "ffn2_w2_2", "final_norm_2"]


def kernel(**inputs):
    import concourse.bacc as _bacc
    from concourse.bass_utils import run_bass_kernel_spmd as _run

    nc = _bacc.Bacc("TRN2", target_bir_lowering=False, num_devices=1)
    arrays, t = {}, {}
    for name in _INS:
        arrays[f"in_{name}"] = np.ascontiguousarray(inputs[name])
    arrays["in_consts"] = constants()
    arrays["in_dft"] = sequence_dft()
    for name, a in arrays.items():
        t[name[3:]] = nc.dram_tensor(name, a.shape, mybir.dt.from_np(a.dtype), kind="ExternalInput").ap()
    out = nc.dram_tensor("out_x", (1, SEQ, D), F32, kind="ExternalOutput").ap()
    two_blocks(nc, t, out)
    r = _run(nc, [arrays], core_ids=[0])
    return r.results[0]["out_x"]
```
